# Optimizing a Trainium2 kernel written in Bass

```python
import jax, jax.numpy as jnp
from jax import lax
import numpy as np

D_MODEL = 1024
BATCH = 1
SEQ = 2048
DEPTH = 2
DEC_BATCH = 8
DEC_SEQ = 1
PAST_LEN = 8192
PAGE_SIZE = 128

MIX_WIDTH = D_MODEL
A_HEADS = 8
A_HEAD_DIM = MIX_WIDTH // 2 // A_HEADS
A_WIDTH = A_HEADS * A_HEAD_DIM
Q_BLOCK = 128
B_GROUPS = 8
B_WIDTH = MIX_WIDTH - A_WIDTH
B_GROUP_DIM = B_WIDTH // B_GROUPS
B_CHUNK = 128
C_HEADS = 4
C_WIDTH = MIX_WIDTH
C_HEAD_DIM = C_WIDTH // C_HEADS
C_CHUNK = 128
CONV_W = 4
N_ATTN_LAYERS = (DEPTH + 1) // 2
N_MLSTM_LAYERS = DEPTH // 2
EVEN_COLS = 4 * A_WIDTH + A_HEADS + 3 * B_WIDTH
ODD_COLS = 3 * C_WIDTH + 2 * C_HEADS
EPS = 1e-6

kernel_name = "fox_gmlp_mlstm_hybrid_step"

F32 = jnp.float32

def _split(x, sizes):
    out, o = [], 0
    for s in sizes:
        out.append(x[..., o:o + s])
        o += s
    return out

def rmsnorm(x, g):
    xf = x.astype(F32)
    return (xf * lax.rsqrt(jnp.mean(xf * xf, -1, keepdims=True) + EPS) * g).astype(x.dtype)

def fox_block(q, k, v, cq, ck, qpos, kpos):
    s = jnp.einsum('bqhd,bkhd->bhqk', q, k).astype(F32) * (q.shape[-1] ** -0.5)
    s = s + cq.swapaxes(1, 2)[:, :, :, None] - ck.swapaxes(1, 2)[:, :, None, :]
    s = jnp.where(kpos[None, :] <= qpos[:, None], s, -jnp.inf)
    p = jax.nn.softmax(s, axis=-1)
    return jnp.einsum('bhqk,bkhd->bqhd', p.astype(v.dtype), v)

def fox_prompt(q, k, v, logf):
    B, S, H, Dh = q.shape
    c = jnp.cumsum(logf, axis=1)
    nb = S // Q_BLOCK
    kpos = jnp.arange(S)
    qb = q.reshape(B, nb, Q_BLOCK, H, Dh).swapaxes(0, 1)
    cb = c.reshape(B, nb, Q_BLOCK, H).swapaxes(0, 1)

    def one_block(args):
        i, qi, ci = args
        return fox_block(qi, k, v, ci, c, i * Q_BLOCK + jnp.arange(Q_BLOCK), kpos)

    out = lax.map(one_block, (jnp.arange(nb), qb, cb))
    return out.swapaxes(0, 1).reshape(B, S, H, Dh)

def fox_sample(q, k, v, logf, kc, vc, lfc, page_table):
    DB, T, H, Dh = q.shape
    past = page_table.shape[1] * kc.shape[1]
    k_all = jnp.concatenate([kc[page_table].reshape(DB, past, H, Dh).astype(k.dtype), k], 1)
    v_all = jnp.concatenate([vc[page_table].reshape(DB, past, H, Dh).astype(v.dtype), v], 1)
    lf_all = jnp.concatenate([lfc[page_table].reshape(DB, past, H).astype(F32), logf], 1)
    c = jnp.cumsum(lf_all, axis=1)
    return fox_block(q, k_all, v_all, c[:, past:], c, past + jnp.arange(T), jnp.arange(past + T))

def gmlp_mix(v, w_s, b_s):
    B, L, _ = v.shape
    n = -(-L // B_CHUNK)
    vp = jnp.pad(v, ((0, 0), (0, n * B_CHUNK - L), (0, 0)))
    vc = vp.reshape(B, n, B_CHUNK, B_GROUPS, B_GROUP_DIM)
    w = jnp.tril(w_s)
    y = jnp.einsum('gts,bnsgc->bntgc', w, vc) + b_s.T[None, None, :, :, None]
    return y.reshape(B, n * B_CHUNK, B_WIDTH)[:, :L]

def even_mixer(h, g, w_in, b_f, ln_g, ln_b, w_s, b_s, w_out, past):
    B, L, _ = h.shape
    xn = rmsnorm(h, g)
    q, k, v, fg, za, u, vb, zb = _split(xn @ w_in, (A_WIDTH, A_WIDTH, A_WIDTH, A_HEADS, A_WIDTH, B_WIDTH, B_WIDTH, B_WIDTH))
    q = q.reshape(B, L, A_HEADS, A_HEAD_DIM)
    k = k.reshape(B, L, A_HEADS, A_HEAD_DIM)
    v = v.reshape(B, L, A_HEADS, A_HEAD_DIM)
    logf = jax.nn.log_sigmoid(fg.astype(F32) + b_f)
    if past is None:
        att = fox_prompt(q, k, v, logf)
    else:
        att = fox_sample(q, k, v, logf, *past)
    ya = att.reshape(B, L, A_WIDTH) * jax.nn.silu(za)
    u = jax.nn.gelu(u, approximate=False)
    vf = jax.nn.gelu(vb, approximate=False).astype(F32)
    mu = jnp.mean(vf, -1, keepdims=True)
    var = jnp.mean((vf - mu) ** 2, -1, keepdims=True)
    vn = ((vf - mu) * lax.rsqrt(var + EPS) * ln_g + ln_b).astype(h.dtype)
    yb = u * gmlp_mix(vn, w_s, b_s) * jax.nn.silu(zb)
    y = jnp.concatenate([ya, yb], -1) @ w_out
    return (h + y).astype(h.dtype), (k, v, logf, vn)

def causal_conv(x, buf, w, b):
    L = x.shape[1]
    xp = jnp.concatenate([buf.astype(x.dtype), x], 1)
    y = b + sum(xp[:, j:j + L] * w[j] for j in range(CONV_W))
    return y, xp[:, xp.shape[1] - (CONV_W - 1):]

def mlstm_chunkwise(q, k, v, log_i, log_f, C0, n0, m0):
    B, L, H, D = q.shape
    Lc = C_CHUNK if L % C_CHUNK == 0 else L
    nc = L // Lc

    def to_chunks(a):
        return a.reshape(B, nc, Lc, *a.shape[2:]).swapaxes(0, 1)

    xs = tuple(map(to_chunks, (q.astype(F32) * (D ** -0.5), k.astype(F32), v.astype(F32), log_i, log_f)))
    causal = jnp.tril(jnp.ones((Lc, Lc), bool))

    def step(carry, inp):
        C, n, m = carry
        qc, kc, vc, ic, fc = inp
        bT = jnp.cumsum(fc, axis=1).swapaxes(1, 2)
        iT = ic.swapaxes(1, 2)
        Dm = jnp.where(causal, bT[:, :, :, None] - bT[:, :, None, :] + iT[:, :, None, :], -jnp.inf)
        prior = bT + m[:, :, None]
        mt = jnp.maximum(prior, jnp.max(Dm, -1))
        W = jnp.exp(Dm - mt[..., None])
        a = jnp.exp(prior - mt)
        Sm = W * jnp.einsum('bthd,bshd->bhts', qc, kc)
        num = jnp.einsum('bhts,bshd->bthd', Sm, vc) + a.swapaxes(1, 2)[..., None] * jnp.einsum('bthk,bhkv->bthv', qc, C)
        den = jnp.sum(Sm, -1) + a * jnp.einsum('bthk,bhk->bht', qc, n)
        den = jnp.maximum(jnp.abs(den), jnp.exp(-mt))
        hc = num / den.swapaxes(1, 2)[..., None]
        m_new = mt[:, :, -1]
        wl = jnp.exp(bT[:, :, -1:] - bT + iT - m_new[..., None])
        a_l = jnp.exp(prior[:, :, -1] - m_new)
        C_new = a_l[..., None, None] * C + jnp.einsum('bhs,bshk,bshv->bhkv', wl, kc, vc)
        n_new = a_l[..., None] * n + jnp.einsum('bhs,bshk->bhk', wl, kc)
        return (C_new, n_new, m_new), hc

    (C, n, m), hs = lax.scan(step, (C0.astype(F32), n0.astype(F32), m0.astype(F32)), xs)
    return hs.swapaxes(0, 1).reshape(B, L, H, D), C, n, m

def mlstm_mixer(h, g, w_in, b_i, b_f, cw, cb, wq, wk, wv, ng, skip, w_out, C0, n0, m0, buf):
    B, L, _ = h.shape
    xn = rmsnorm(h, g)
    xc, z, o, ig, fg = _split(xn @ w_in, (C_WIDTH, C_WIDTH, C_WIDTH, C_HEADS, C_HEADS))
    xconv, new_buf = causal_conv(xc, buf, cw, cb)
    xconv = jax.nn.silu(xconv)
    xh = xconv.reshape(B, L, C_HEADS, C_HEAD_DIM)
    q = jnp.einsum('blhd,hde->blhe', xh, wq)
    k = jnp.einsum('blhd,hde->blhe', xh, wk)
    v = jnp.einsum('blhd,hde->blhe', xc.reshape(B, L, C_HEADS, C_HEAD_DIM), wv)
    log_i = ig.astype(F32) + b_i
    log_f = jax.nn.log_sigmoid(fg.astype(F32) + b_f)
    hc, C, n, m = mlstm_chunkwise(q, k, v, log_i, log_f, C0, n0, m0)
    mu = jnp.mean(hc, -1, keepdims=True)
    var = jnp.mean((hc - mu) ** 2, -1, keepdims=True)
    hn = ((hc - mu) * lax.rsqrt(var + EPS)).reshape(B, L, C_WIDTH) * ng
    y = (jax.nn.sigmoid(o) * hn + skip * xconv) * jax.nn.silu(z)
    return (h + y @ w_out).astype(h.dtype), (C, n, m, new_buf)

def setup_inputs(seed: int = 0) -> dict:
    key = jax.random.key(seed)
    keys = iter(jax.random.split(key, 48))

    def rnd(shape, scale=1.0, shift=0.0):
        return jax.random.normal(next(keys), shape, F32) * scale + shift

    n_pages = PAST_LEN // PAGE_SIZE
    n_used = DEC_BATCH * n_pages
    n_phys = n_used + max(1, n_used // 4)
    perm = jax.random.permutation(next(keys), n_phys)
    page_table = perm[:n_used].reshape(DEC_BATCH, n_pages).astype(jnp.int32)
    LA, LC = N_ATTN_LAYERS, N_MLSTM_LAYERS
    return {
        "x_prompt": rnd((BATCH, SEQ, D_MODEL)),
        "x_sample": rnd((DEC_BATCH, DEC_SEQ, D_MODEL)),
        "cache_k": rnd((LA, n_phys, PAGE_SIZE, A_HEADS, A_HEAD_DIM)),
        "cache_v": rnd((LA, n_phys, PAGE_SIZE, A_HEADS, A_HEAD_DIM)),
        "cache_logf": jax.nn.log_sigmoid(rnd((LA, n_phys, PAGE_SIZE, A_HEADS), 1.0, 3.0)),
        "state_c": rnd((LC, DEC_BATCH, C_HEADS, C_HEAD_DIM, C_HEAD_DIM), 0.1),
        "state_n": rnd((LC, DEC_BATCH, C_HEADS, C_HEAD_DIM), 0.1),
        "state_m": rnd((LC, DEC_BATCH, C_HEADS), 0.5),
        "state_conv": rnd((LC, DEC_BATCH, CONV_W - 1, C_WIDTH)),
        "page_table": page_table,
        "norm_g": rnd((DEPTH, D_MODEL), 0.02, 1.0),
        "final_g": rnd((D_MODEL,), 0.02, 1.0),
        "even_w_in": rnd((LA, D_MODEL, EVEN_COLS), D_MODEL ** -0.5),
        "even_b_f": rnd((LA, A_HEADS), 0.5, 3.0),
        "gmlp_ln_g": rnd((LA, B_WIDTH), 0.02, 1.0),
        "gmlp_ln_b": rnd((LA, B_WIDTH), 0.02),
        "gmlp_w_s": rnd((LA, B_GROUPS, B_CHUNK, B_CHUNK), B_CHUNK ** -0.5),
        "gmlp_b_s": rnd((LA, B_GROUPS, B_CHUNK), 0.02, 1.0),
        "even_w_out": rnd((LA, MIX_WIDTH, D_MODEL), MIX_WIDTH ** -0.5),
        "odd_w_in": rnd((LC, D_MODEL, ODD_COLS), D_MODEL ** -0.5),
        "odd_b_i": rnd((LC, C_HEADS), 0.1),
        "odd_b_f": jnp.linspace(3.0, 6.0, C_HEADS, dtype=F32)[None, :] + rnd((LC, C_HEADS), 0.1),
        "conv_w": rnd((LC, CONV_W, C_WIDTH), CONV_W ** -0.5),
        "conv_b": rnd((LC, C_WIDTH), 0.02),
        "mlstm_w_q": rnd((LC, C_HEADS, C_HEAD_DIM, C_HEAD_DIM), C_HEAD_DIM ** -0.5),
        "mlstm_w_k": rnd((LC, C_HEADS, C_HEAD_DIM, C_HEAD_DIM), C_HEAD_DIM ** -0.5),
        "mlstm_w_v": rnd((LC, C_HEADS, C_HEAD_DIM, C_HEAD_DIM), C_HEAD_DIM ** -0.5),
        "mlstm_norm_g": rnd((LC, C_WIDTH), 0.02, 1.0),
        "mlstm_skip": rnd((LC, C_WIDTH), 0.02, 1.0),
        "odd_w_out": rnd((LC, C_WIDTH, D_MODEL), C_WIDTH ** -0.5),
    }

def reference(x_prompt, x_sample, cache_k, cache_v, cache_logf, state_c, state_n, state_m, state_conv, page_table,
              norm_g, final_g, even_w_in, even_b_f, gmlp_ln_g, gmlp_ln_b, gmlp_w_s, gmlp_b_s, even_w_out,
              odd_w_in, odd_b_i, odd_b_f, conv_w, conv_b, mlstm_w_q, mlstm_w_k, mlstm_w_v, mlstm_norm_g,
              mlstm_skip, odd_w_out):
    hp, hs = x_prompt, x_sample
    kp, vp, lp, ks, vs, ls, chv = [], [], [], [], [], [], []
    cp, np_, mp, bp, cs, ns, ms, bs = [], [], [], [], [], [], [], []
    for l in range(DEPTH):
        j = l // 2
        if l % 2 == 0:
            ew = (norm_g[l], even_w_in[j], even_b_f[j], gmlp_ln_g[j], gmlp_ln_b[j], gmlp_w_s[j], gmlp_b_s[j], even_w_out[j])
            hp, (k1, v1, lf1, _) = even_mixer(hp, *ew, past=None)
            hs, (k2, v2, lf2, vb2) = even_mixer(hs, *ew, past=(cache_k[j], cache_v[j], cache_logf[j], page_table))
            kp.append(k1); vp.append(v1); lp.append(lf1)
            ks.append(k2); vs.append(v2); ls.append(lf2); chv.append(vb2)
        else:
            ow = (norm_g[l], odd_w_in[j], odd_b_i[j], odd_b_f[j], conv_w[j], conv_b[j], mlstm_w_q[j], mlstm_w_k[j],
                  mlstm_w_v[j], mlstm_norm_g[j], mlstm_skip[j], odd_w_out[j])
            B = hp.shape[0]
            C0 = jnp.zeros((B, C_HEADS, C_HEAD_DIM, C_HEAD_DIM), F32)
            n0 = jnp.zeros((B, C_HEADS, C_HEAD_DIM), F32)
            m0 = jnp.zeros((B, C_HEADS), F32)
            buf0 = jnp.zeros((B, CONV_W - 1, C_WIDTH), hp.dtype)
            hp, (c1, n1, m1, b1) = mlstm_mixer(hp, *ow, C0, n0, m0, buf0)
            hs, (c2, n2, m2, b2) = mlstm_mixer(hs, *ow, state_c[j], state_n[j], state_m[j], state_conv[j])
            cp.append(c1); np_.append(n1); mp.append(m1); bp.append(b1)
            cs.append(c2); ns.append(n2); ms.append(m2); bs.append(b2)
    y_prompt = rmsnorm(hp, final_g)
    y_sample = rmsnorm(hs, final_g)
    return (y_prompt, y_sample,
            jnp.stack(kp), jnp.stack(vp), jnp.stack(lp),
            jnp.stack(ks), jnp.stack(vs), jnp.stack(ls), jnp.stack(chv),
            jnp.stack(cp), jnp.stack(np_), jnp.stack(mp), jnp.stack(bp),
            jnp.stack(cs), jnp.stack(ns), jnp.stack(ms), jnp.stack(bs))


_drawn_inputs = setup_inputs


def setup_inputs(seed=0):
    import zlib

    import numpy as np

    out = dict(_drawn_inputs(seed))
    spreads = {}
    factors = {'cache_logf': 3.339,
     'final_g': 7.994,
     'gmlp_ln_g': 10.692,
     'gmlp_ln_b': 9.316,
     'gmlp_b_s': 7.104,
     'mlstm_norm_g': 42.682,
     'mlstm_skip': 35.59}
    for name, (base, spread) in spreads.items():
        noise = np.random.default_rng([zlib.crc32(name.encode()), seed]).standard_normal(out[name].shape)
        drawn = base * np.exp(spread * noise) if base else spread * noise
        out[name] = __import__('jax').numpy.asarray(drawn.astype(out[name].dtype))
    for name, factor in factors.items():
        out[name] = (out[name] * factor).astype(out[name].dtype)
    return out
```

```python
import concourse.bass as bass
from concourse import mybir
from contextlib import ExitStack

F32 = mybir.dt.float32
BF16 = mybir.dt.bfloat16
I32 = mybir.dt.int32
ALU = mybir.AluOpType
ACT = mybir.ActivationFunctionType
AX = mybir.AxisListType

P = 128
D = 1024
KC = D // P
SEQ = 2048
NT = SEQ // P
NB = 8
PAGES = 64
N_PHYS = 640
AH, AD = 8, 64
AW = AH * AD
BW = 512
BG = 8
CH, CD = 4, 256
CW = CH * CD
EVEN_COLS = 4 * AW + AH + 3 * BW
ODD_COLS = 3 * CW + 2 * CH
EPS = 1e-6
NEG = -1e30

COL = {"q": 0, "k": AW, "v": 2 * AW, "fg": 3 * AW, "za": 3 * AW + AH, "u": 4 * AW + AH,
       "vb": 4 * AW + AH + BW, "zb": 4 * AW + AH + 2 * BW}

LEAD = 2


def wait_stage(eng, stage, tile, back=0, per_tile=1, nth=None):
    nth = per_tile if nth is None else nth
    eng.wait_ge(stage, (tile + (LEAD - back)) * per_tile + nth)


def wait_dma(eng, stage, tile, back=0, dmas=1):
    eng.wait_ge(stage, (tile + (LEAD + 1 - back)) * (16 * dmas))


class Chain:

    def __init__(self, sem, names):
        self.sem, self.names = sem, names

    def wait(self, eng, name):
        n = self.names.index(name)
        if n:
            eng.wait_ge(self.sem, n)


class Scope:

    def __init__(self, nc, stack, tag):
        self.nc, self.stack, self.tag, self.taken = nc, stack, tag, []
        stack.callback(self.close)

    def close(self):
        if self.taken:
            self.nc.all_engine_barrier()
            self.nc.clear_and_free_semaphores(self.taken)
            self.nc.all_engine_barrier()

    def sb(self, name, shape, dt=F32):
        return self.stack.enter_context(self.nc.sbuf_tensor(f"{self.tag}_{name}", shape, dt))

    def ps(self, name, shape=(P, 512), dt=F32):
        return self.stack.enter_context(self.nc.psum_tensor(f"{self.tag}_{name}", list(shape), dt))

    def sem(self, name):
        self.taken.append(self.nc.alloc_semaphore(name=f"{self.tag}_{name}"))
        return self.taken[-1]

    def sems(self, names):
        return {n: self.sem(n) for n in names.split()}


def even_project(nc, io, keep):
    with ExitStack() as stack:
        s = Scope(nc, stack, "ep")
        w = s.sb("w", [P, KC, EVEN_COLS])
        x_in = [s.sb(f"x{i}", [P, D]) for i in range(2)]
        xT = [s.sb(f"xT{i}", [P, KC, P]) for i in range(2)]
        g_row = s.sb("g_row", [P, D])
        ln_g = s.sb("ln_g", [P, BW])
        ln_b = s.sb("ln_b", [P, BW])
        b_sT = s.sb("b_sT", [P, BG])
        mixT = s.sb("mixT", [P, BG, P])
        q_sb, k_sb, v_sb = (s.sb(n, [P, AW]) for n in ("q", "k", "v"))
        vg, ug, thb, tha = (s.sb(n, [P, BW]) for n in ("vg", "ug", "thb", "tha"))
        mixed = s.sb("mixed", [P, D])
        kpage = [s.sb(f"kpage{i}", [P, 2, AW]) for i in range(4)]
        q_bc = [s.sb(f"q_bc{i}", [P, AW]) for i in range(2)]
        b_f = s.sb("b_f", [P, AH])
        ssq = s.sb("ssq", [P, 1])
        msq = s.sb("msq", [P, 1])
        rstd = s.sb("rstd", [P, 1])
        stats = s.sb("stats", [P, 6])
        muvar = s.sb("muvar", [P, 2])
        lnr = s.sb("lnr", [P, 1])
        lnv = s.sb("lnv", [P, 1])
        w00 = s.sb("w00", [NB, BG])
        b0 = s.sb("b0", [NB, BG])
        pages = s.sb("pages", [1, NB * PAGES], I32)
        TR = [s.ps(f"TR{i}") for i in range(2)]
        PJ = [s.ps(f"PJ{i}") for i in range(4)]
        MX = s.ps("MX")
        SM = s.ps("SM")
        BANK = {"vb": PJ[0], "u": PJ[1], "zb": PJ[2], "za": PJ[3], "q": PJ[0], "k": PJ[1], "v": PJ[2]}
        SBANK = {"vb": PJ[0], "u": PJ[1], "zb": PJ[2], "za": PJ[3], "q": TR[0], "k": TR[1], "v": MX}
        w_s_in = xT[1]

        with ExitStack() as st2:
            s2 = Scope(nc, st2, "ep0")
            loads = s2.sems("x w vec ws pages")
            const = s2.sem("const")
            step = Chain(s2.sem("step"), "mask_ws turn_ws mixT square meansq rstd xn turn xT project gates "
                         "stats muvar lnvar lnrstd vn1 vn2 vn3 gza gzb mix1 mix2 mix3 mix4 fg self1 self2".split())
            stored = s2.sem("stored")
            block = st2.enter_context(nc.Block())
            xs = x_in[0][0:NB, :]

            @block.sync
            def _(sp):
                sp.dma_start(xs, io["x_sample"]).then_inc(loads["x"], 16)
                sp.dma_start(w_s_in[:], io["gmlp_w_s"].rearrange("g t s -> t g s")).then_inc(loads["ws"], 16)
                for k in range(KC):
                    sp.dma_start(w[:, k, :], io["even_w_in"][k * P:(k + 1) * P, :]).then_inc(loads["w"], 16)
                sp.dma_start(pages[:], io["page_table"].rearrange("(o b) p -> o (b p)", o=1)).then_inc(loads["pages"], 16)
                sp.wait_ge(loads["pages"], 16)
                sp.wait_ge(step.sem, step.names.index("gates") + 1)
                sp.dma_start(io["q_sample"], q_sb[0:NB, :]).then_inc(stored, 16)
                sp.dma_start(io["k_sample"], k_sb[0:NB, :]).then_inc(stored, 16)
                sp.dma_start(io["v_sample"], v_sb[0:NB, :]).then_inc(stored, 16)
                sp.wait_ge(step.sem, step.names.index("vn3") + 1)
                sp.dma_start(io["chunk_v"], vg[0:NB, :]).then_inc(stored, 16)
                sp.wait_ge(step.sem, step.names.index("mix4") + 1)
                sp.dma_start(io["s_mixed"], mixed[0:NB, :]).then_inc(stored, 16)
                sp.wait_ge(stored, 80)

            @block.gpsimd
            def _(pool):
                nc.gpsimd.memset(keep["ident"][:], 0.0).then_inc(const, 1)
                nc.gpsimd.memset(keep["ones"][:], 1.0).then_inc(const, 1)
                nc.gpsimd.memset(keep["minus_half"][:], -0.5).then_inc(const, 1)
                nc.gpsimd.memset(keep["half"][:], 0.5).then_inc(const, 1)
                nc.gpsimd.memset(keep["scores"][:, :, :, PAGES:PAGES + 1], NEG).then_inc(const, 1)
                nc.gpsimd.memset(keep["mask_bf"][:], 0.0).then_inc(const, 1)
                nc.gpsimd.memset(keep["maskT_bf"][:], 0.0).then_inc(const, 1)
                nc.gpsimd.memset(keep["ident_bf"][:], 0.0).then_inc(const, 1)
                pool.wait_ge(const, 8)
                nc.gpsimd.affine_select(out=keep["ident"][:], in_=keep["ident"][:], compare_op=ALU.not_equal,
                                        fill=1.0, base=0, pattern=[[-1, P]], channel_multiplier=1).then_inc(const, 1)
                nc.gpsimd.affine_select(out=keep["ident_bf"][:], in_=keep["ident_bf"][:], compare_op=ALU.not_equal,
                                        fill=1.0, base=0, pattern=[[-1, P]], channel_multiplier=1).then_inc(const, 1)
                nc.gpsimd.affine_select(out=keep["upto"][:], in_=keep["ones"][:], compare_op=ALU.is_ge,
                                        fill=0.0, base=0, pattern=[[1, P]], channel_multiplier=-1).then_inc(const, 1)
                nc.gpsimd.affine_select(out=keep["after"][:], in_=keep["ones"][:], compare_op=ALU.is_gt,
                                        fill=0.0, base=0, pattern=[[-1, P]], channel_multiplier=1).then_inc(const, 1)
                nc.gpsimd.affine_select(out=keep["mask_bf"][:], in_=keep["mask_bf"][:], compare_op=ALU.is_ge,
                                        fill=NEG, base=0, pattern=[[-1, P]], channel_multiplier=1).then_inc(const, 1)
                nc.gpsimd.affine_select(out=keep["maskT_bf"][:], in_=keep["maskT_bf"][:], compare_op=ALU.is_ge,
                                        fill=-NEG, base=0, pattern=[[1, P]], channel_multiplier=-1).then_inc(const, 1)
                pool.wait_ge(loads["ws"], 16)
                nc.gpsimd.affine_select(out=w_s_in[:], in_=w_s_in[:], compare_op=ALU.is_ge, fill=0.0, base=0,
                                        pattern=[[0, BG], [-1, P]], channel_multiplier=1).then_inc(step.sem, 1)
                step.wait(pool, "meansq")
                nc.gpsimd.tensor_scalar(msq[0:NB, :], ssq[0:NB, :], 1.0 / D, EPS, ALU.mult, ALU.add).then_inc(step.sem, 1)
                step.wait(pool, "rstd")
                nc.gpsimd.tensor_tensor(rstd[0:NB, :], msq[0:NB, :], keep["minus_half"][0:NB, :], ALU.pow).then_inc(step.sem, 1)
                step.wait(pool, "lnvar")
                nc.gpsimd.tensor_scalar(msq[0:NB, :], muvar[0:NB, 1:2], 1.0, EPS, ALU.mult, ALU.add).then_inc(step.sem, 1)
                step.wait(pool, "lnrstd")
                nc.gpsimd.tensor_tensor(lnr[0:NB, :], msq[0:NB, :], keep["minus_half"][0:NB, :], ALU.pow).then_inc(step.sem, 1)

            @block.scalar
            def _(act):
                act.dma_start(g_row[:], io["norm_g"][0, :].partition_broadcast(P)).then_inc(loads["vec"], 16)
                act.dma_start(ln_g[:], io["gmlp_ln_g"].partition_broadcast(P)).then_inc(loads["vec"], 16)
                act.dma_start(ln_b[:], io["gmlp_ln_b"].partition_broadcast(P)).then_inc(loads["vec"], 16)
                act.dma_start(b_f[:], io["even_b_f"].partition_broadcast(P)).then_inc(loads["vec"], 16)
                with nc.allow_non_contiguous_dma(reason="small vectors"):
                    act.dma_start(b_sT[:], io["gmlp_b_s"].rearrange("g t -> t g")).then_inc(loads["vec"], 16)
                    act.dma_start(w00[:], io["gmlp_w_s"][:, 0, 0].partition_broadcast(NB)).then_inc(loads["vec"], 16)
                    act.dma_start(b0[:], io["gmlp_b_s"][:, 0].partition_broadcast(NB)).then_inc(loads["vec"], 16)
                step.wait(act, "mixT")
                for h in range(2):
                    op = nc.scalar.activation(mixT[:, 4 * h:4 * h + 4, :], TR[h][:].rearrange("p (g t) -> p g t", g=4), ACT.Copy)
                op.then_inc(step.sem, 1)
                act.wait_ge(loads["x"], 16)
                step.wait(act, "square")
                nc.scalar.activation(xT[0][0:NB, :, :].rearrange("p a b -> p (a b)"), xs, ACT.Square, accum_out=ssq[0:NB, :]).then_inc(step.sem, 1)
                step.wait(act, "xT")
                nc.scalar.activation(xT[0][:, :, 0:NB], TR[0][:, 0:KC * NB].rearrange("p (k b) -> p k b", b=NB), ACT.Copy).then_inc(step.sem, 1)
                step.wait(act, "gates")
                nc.scalar.activation(vg[0:NB, :], SBANK["vb"][0:NB, :], ACT.Gelu)
                nc.scalar.activation(ug[0:NB, :], SBANK["u"][0:NB, :], ACT.Gelu)
                nc.scalar.activation(thb[0:NB, :], SBANK["zb"][0:NB, :], ACT.Tanh, scale=0.5)
                nc.scalar.activation(tha[0:NB, :], SBANK["za"][0:NB, :], ACT.Tanh, scale=0.5)
                nc.scalar.activation(q_sb[0:NB, :], SBANK["q"][0:NB, :], ACT.Copy, scale=AD ** -0.5)
                nc.scalar.activation(k_sb[0:NB, :], SBANK["k"][0:NB, :], ACT.Copy)
                nc.scalar.activation(v_sb[0:NB, :], SBANK["v"][0:NB, :], ACT.Copy).then_inc(step.sem, 1)

            @block.vector
            def _(dve):
                dve.wait_ge(loads["vec"], 7 * 16)
                step.wait(dve, "xn")
                nc.vector.scalar_tensor_tensor(xs, xs, rstd[0:NB, :], g_row[0:NB, :], ALU.mult, ALU.mult).then_inc(step.sem, 1)
                step.wait(dve, "stats")
                nc.vector.bn_stats(stats[0:NB, :], vg[0:NB, :]).then_inc(step.sem, 1)
                step.wait(dve, "muvar")
                nc.vector.bn_aggr(muvar[0:NB, :], stats[0:NB, :]).then_inc(step.sem, 1)
                step.wait(dve, "vn1")
                nc.vector.tensor_scalar(vg[0:NB, :], vg[0:NB, :], muvar[0:NB, 0:1], lnr[0:NB, :], ALU.subtract, ALU.mult).then_inc(step.sem, 1)
                step.wait(dve, "vn2")
                nc.vector.tensor_tensor(vg[0:NB, :], vg[0:NB, :], ln_g[0:NB, :], ALU.mult).then_inc(step.sem, 1)
                step.wait(dve, "vn3")
                nc.vector.tensor_tensor(vg[0:NB, :], vg[0:NB, :], ln_b[0:NB, :], ALU.add).then_inc(step.sem, 1)
                step.wait(dve, "gza")
                nc.vector.scalar_tensor_tensor(mixed[0:NB, 0:AW], tha[0:NB, :], 1.0, SBANK["za"][0:NB, :], ALU.add, ALU.mult).then_inc(step.sem, 1)
                step.wait(dve, "gzb")
                nc.vector.scalar_tensor_tensor(thb[0:NB, :], thb[0:NB, :], 1.0, SBANK["zb"][0:NB, :], ALU.add, ALU.mult).then_inc(step.sem, 1)
                step.wait(dve, "mix1")
                v3 = lambda ap: ap.rearrange("p (g c) -> p g c", g=BG)
                wide = lambda ap: ap[:].unsqueeze(2).to_broadcast([NB, BG, 64])
                nc.vector.tensor_tensor(v3(tha[0:NB, :]), v3(vg[0:NB, :]), wide(w00), ALU.mult).then_inc(step.sem, 1)
                step.wait(dve, "mix2")
                nc.vector.tensor_tensor(v3(tha[0:NB, :]), v3(tha[0:NB, :]), wide(b0), ALU.add).then_inc(step.sem, 1)
                step.wait(dve, "mix3")
                nc.vector.scalar_tensor_tensor(ug[0:NB, :], ug[0:NB, :], 0.5, thb[0:NB, :], ALU.mult, ALU.mult).then_inc(step.sem, 1)
                step.wait(dve, "mix4")
                nc.vector.tensor_tensor(mixed[0:NB, AW:D], ug[0:NB, :], tha[0:NB, :], ALU.mult).then_inc(step.sem, 1)
                step.wait(dve, "fg")
                nc.vector.tensor_tensor(keep["s_fg"][:], SM[0:NB, 0:AH], b_f[0:NB, :], ALU.add).then_inc(step.sem, 1)
                step.wait(dve, "self1")
                nc.vector.tensor_tensor(thb[0:NB, :], q_sb[0:NB, :], k_sb[0:NB, :], ALU.mult).then_inc(step.sem, 1)
                step.wait(dve, "self2")
                nc.vector.tensor_reduce(keep["s_self"][:], v3(thb[0:NB, :]), AX.X, ALU.add).then_inc(step.sem, 1)

            @block.tensor
            def _(pe):
                pe.wait_ge(const, 14)
                step.wait(pe, "turn_ws")
                for g in range(BG):
                    op = nc.tensor.transpose(TR[g // 4][:, (g % 4) * P:(g % 4 + 1) * P], w_s_in[:, g, :], keep["ident"][:])
                op.then_inc(step.sem, 1)
                step.wait(pe, "turn")
                for k in range(KC):
                    op = nc.tensor.transpose(TR[0][:, k * NB:(k + 1) * NB], xs[:, k * P:(k + 1) * P], keep["ident"][0:NB, 0:NB])
                op.then_inc(step.sem, 1)
                pe.wait_ge(loads["w"], 16 * KC)
                step.wait(pe, "project")
                for k in range(KC):
                    nc.tensor.matmul(SM[0:NB, 0:AH], xT[0][:, k, 0:NB], w[:, k, COL["fg"]:COL["fg"] + AH], start=k == 0, stop=k == KC - 1)
                for name in ("vb", "u", "zb", "za", "q", "k", "v"):
                    for k in range(KC):
                        op = nc.tensor.matmul(SBANK[name][0:NB, :], xT[0][:, k, 0:NB], w[:, k, COL[name]:COL[name] + 512],
                                              start=k == 0, stop=k == KC - 1)
                op.then_inc(step.sem, 1)

        with ExitStack() as st2:
            s2 = Scope(nc, st2, "ep1")
            ld = s2.sems("x0 x1 qb0 qb1 kp0 kp1 kp2 kp3")
            out = {n: s2.sem(f"{n}_stored") for n in ("q", "k", "v", "mixed")}
            st = s2.sems("ssq msq rstd xn turned xT "
                         "p_vb p_u p_zb p_za p_q p_k p_v p_fg p_mix "
                         "a_vb a_u a_zb a_za a_q a_k a_v "
                         "stats muvar lnvar lnr vn1 vn vn2 gza gzb half_y bias_y mixed fg_out scored")
            pr = [s2.sem(f"prod{i}") for i in range(4)]
            fr = [s2.sem(f"free{i}") for i in range(4)]
            block = st2.enter_context(nc.Block())
            GROUPS = 16
            USES = GROUPS // 4

            def tiles(eng, body):
                with eng.Fori(0, NT // 2 - 1) as i:
                    body(i * 2, i, 0, False)
                    body(i * 2 + 1, i, 1, False)
                body(NT - 2, NT // 2 - 1, 0, False)
                body(NT - 1, NT // 2 - 1, 1, True)

            @block.sync
            def _(sp):
                for n in ("x0", "x1", "qb0", "qb1"):
                    sp.sem_inc(ld[n], 16 * LEAD)
                for n in ("kp0", "kp1", "kp2", "kp3"):
                    sp.sem_inc(ld[n], 32 * LEAD * USES)
                sp.sem_inc(out["mixed"], 16 * LEAD)
                sp.dma_start(x_in[0][:], io["x_prompt"][0:P, :]).then_inc(ld["x0"], 16)
                sp.dma_start(q_bc[0][:], io["q_sample"][0, :].partition_broadcast(P)).then_inc(ld["qb0"], 16)

                def body(t, pair, r, last):
                    n = 1 - r
                    if not last:
                        wait_stage(sp, st["turned"], t, back=1)
                        nxt = pair + r
                        sp.dma_start(x_in[n][:], io["x_prompt"][bass.ds((t + 1) * P, P), :]).then_inc(ld[f"x{n}"], 16)
                        wait_stage(sp, st["scored"], t, back=1)
                        sp.dma_start(q_bc[n][:], io["q_sample_flat"][bass.ds(nxt * AW, AW)].partition_broadcast(P)).then_inc(ld[f"qb{n}"], 16)
                    for g in range(GROUPS):
                        wait_stage(sp, fr[g % 4], t, per_tile=USES, nth=g // 4)
                        for j in range(2):
                            page = sp.value_load(pages[0:1, bass.ds(t * 32 + (2 * g + j), 1)], min_val=0, max_val=N_PHYS - 1)
                            sp.dma_start(kpage[g % 4][:, j, :], io["cache_k"][bass.ds(page * P, P), :]).then_inc(ld[f"kp{g % 4}"], 16)
                    wait_stage(sp, st["mixed"], t)
                    sp.dma_start(io["mix_scratch"][bass.ds(t * P, P), :], mixed[:]).then_inc(out["mixed"], 16)
                tiles(sp, body)
                wait_dma(sp, out["mixed"], NT - 1)

            @block.gpsimd
            def _(pool):
                for n in ("rstd", "lnr"):
                    pool.sem_inc(st[n], LEAD)

                def norm(t):
                    wait_stage(pool, st["xn"], t, back=1)
                    wait_stage(pool, st["msq"], t)
                    nc.gpsimd.tensor_tensor(rstd[:], msq[:], keep["minus_half"][:], ALU.pow).then_inc(st["rstd"], 1)
                norm(0)

                def body(t, pair, r, last):
                    if not last:
                        norm(t + 1)
                    wait_stage(pool, st["lnvar"], t)
                    wait_stage(pool, st["vn1"], t, back=1)
                    nc.gpsimd.tensor_tensor(lnr[:], lnv[:], keep["minus_half"][:], ALU.pow).then_inc(st["lnr"], 1)
                tiles(pool, body)

            @block.scalar
            def _(act):
                for n in ("ssq", "xT", "a_vb", "a_u", "a_zb", "a_za", "a_q", "a_k", "a_v"):
                    act.sem_inc(st[n], LEAD)
                for n in ("q", "k", "v"):
                    act.sem_inc(out[n], 16 * LEAD)

                def square(t, slot, nth):
                    act.wait_ge(ld[f"x{slot}"], nth)
                    nc.scalar.activation(xT[slot][:].rearrange("p k n -> p (k n)"), x_in[slot][:],
                                         ACT.Square, accum_out=ssq[:]).then_inc(st["ssq"], 1)

                def turn_out(t, slot):
                    wait_stage(act, st["turned"], t)
                    wait_stage(act, st["p_v"], t, back=2)
                    for h in range(2):
                        op = nc.scalar.activation(xT[slot][:, 4 * h:4 * h + 4, :], TR[h][:].rearrange("p (g t) -> p g t", g=4), ACT.Copy)
                    op.then_inc(st["xT"], 1)
                square(0, 0, 16 * (LEAD + 1))
                turn_out(0, 0)

                def body(t, pair, r, last):
                    wait_stage(act, st["p_vb"], t)
                    wait_stage(act, st["p_mix"], t, back=1)
                    nc.scalar.activation(vg[:], BANK["vb"][:], ACT.Gelu).then_inc(st["a_vb"], 1)
                    wait_stage(act, st["p_u"], t)
                    wait_stage(act, st["mixed"], t, back=1)
                    nc.scalar.activation(ug[:], BANK["u"][:], ACT.Gelu).then_inc(st["a_u"], 1)
                    wait_stage(act, st["p_zb"], t)
                    nc.scalar.activation(thb[:], BANK["zb"][:], ACT.Tanh, scale=0.5).then_inc(st["a_zb"], 1)
                    if not last:
                        wait_stage(act, st["p_v"], t, back=1)
                        wait_stage(act, st["msq"], t)
                        square(t + 1, 1 - r, (pair + (r + LEAD + 1)) * 16)
                    wait_stage(act, st["p_za"], t)
                    wait_stage(act, st["gza"], t, back=1)
                    nc.scalar.activation(tha[:], BANK["za"][:], ACT.Tanh, scale=0.5).then_inc(st["a_za"], 1)
                    for n, buf, scale in (("q", q_sb, AD ** -0.5), ("k", k_sb, 1.0), ("v", v_sb, 1.0)):
                        wait_stage(act, st[f"p_{n}"], t)
                        wait_dma(act, out[n], t, back=1)
                        nc.scalar.activation(buf[:], BANK[n][:], ACT.Copy, scale=scale).then_inc(st[f"a_{n}"], 1)
                        wait_stage(act, st[f"a_{n}"], t)
                        act.dma_start(io[f"{n}_prompt"][bass.ds(t * P, P), :], buf[:]).then_inc(out[n], 16)
                    if not last:
                        turn_out(t + 1, 1 - r)
                tiles(act, body)
                for n in ("q", "k", "v"):
                    wait_dma(act, out[n], NT - 1)

            @block.vector
            def _(dve):
                for n in ("msq", "lnvar", "xn", "stats", "muvar", "vn1", "vn", "vn2", "gza", "gzb", "half_y", "bias_y", "mixed", "fg_out", "scored"):
                    dve.sem_inc(st[n], LEAD)
                for i in range(4):
                    dve.sem_inc(pr[i], LEAD * USES)
                    dve.sem_inc(fr[i], LEAD * USES)

                def mean_square(t):
                    wait_stage(dve, st["ssq"], t)
                    wait_stage(dve, st["rstd"], t, back=1)
                    return nc.vector.tensor_scalar(msq[:], ssq[:], 1.0 / D, EPS, ALU.mult, ALU.add).then_inc(st["msq"], 1)

                def normed(t, slot):
                    wait_stage(dve, st["rstd"], t)
                    nc.vector.scalar_tensor_tensor(x_in[slot][:], x_in[slot][:], rstd[:], g_row[:], ALU.mult, ALU.mult).then_inc(st["xn"], 1)
                mean_square(0)
                normed(0, 0)

                def body(t, pair, r, last):
                    v3 = lambda ap: ap.rearrange("p (g c) -> p g c", g=BG)

                    def score(g):
                        i = g % 4
                        if g == 0:
                            dve.wait_ge(ld[f"qb{r}"], (pair + (LEAD + 1)) * 16)
                        dve.wait_ge(ld[f"kp{i}"], (t + LEAD) * (32 * USES) + 32 * (g // 4 + 1))
                        nc.vector.tensor_tensor(kpage[i][:], kpage[i][:], q_bc[r][:].unsqueeze(1).to_broadcast([P, 2, AW]), ALU.mult).then_inc(pr[i], 1)

                    def total(g):
                        i = g % 4
                        wait_stage(dve, pr[i], t, per_tile=USES, nth=g // 4 + 1)
                        flat = keep["scores"][:].rearrange("p b h g -> p (b h g)")
                        first = r * 32 + 2 * g
                        dst = keep["scores"][:, bass.ds(pair, 1), :, first:first + 2].rearrange("p a h g -> p (a g) h")
                        op = nc.vector.tensor_reduce(dst, kpage[i][:].rearrange("p j (h d) -> p j h d", h=AH), AX.X, ALU.add)
                        op.then_inc(fr[i], 1)

                    def tile_ops():
                        wait_stage(dve, st["p_fg"], t)
                        yield nc.vector.tensor_tensor(keep["fg"][:, bass.ds(t, 1), :].rearrange("p a h -> p (a h)"), SM[:, 0:AH], b_f[:], ALU.add).then_inc(st["fg_out"], 1)
                        wait_stage(dve, st["a_vb"], t)
                        wait_stage(dve, st["lnr"], t, back=1)
                        yield nc.vector.bn_stats(stats[:], vg[:]).then_inc(st["stats"], 1)
                        wait_stage(dve, st["stats"], t)
                        wait_stage(dve, st["lnr"], t, back=1)
                        yield
                        yield nc.vector.bn_aggr(muvar[:], stats[:]).then_inc(st["muvar"], 1)
                        wait_stage(dve, st["muvar"], t)
                        yield nc.vector.tensor_scalar(lnv[:], muvar[:, 1:2], 1.0, EPS, ALU.mult, ALU.add).then_inc(st["lnvar"], 1)
                        if not last:
                            yield mean_square(t + 1)
                        wait_stage(dve, st["a_zb"], t)
                        yield nc.vector.scalar_tensor_tensor(thb[:], thb[:], 1.0, BANK["zb"][:], ALU.add, ALU.mult).then_inc(st["gzb"], 1)
                        wait_stage(dve, st["lnr"], t)
                        yield nc.vector.tensor_scalar(vg[:], vg[:], muvar[:, 0:1], lnr[:], ALU.subtract, ALU.mult).then_inc(st["vn1"], 1)
                        wait_stage(dve, st["vn1"], t)
                        yield nc.vector.tensor_tensor(vg[:], vg[:], ln_g[:], ALU.mult).then_inc(st["vn"], 1)
                        wait_stage(dve, st["vn"], t)
                        yield nc.vector.tensor_tensor(vg[:], vg[:], ln_b[:], ALU.add).then_inc(st["vn2"], 1)
                        if not last:
                            yield normed(t + 1, 1 - r)
                        wait_stage(dve, st["a_za"], t)
                        wait_dma(dve, out["mixed"], t, back=1)
                        yield nc.vector.scalar_tensor_tensor(mixed[:, 0:AW], tha[:], 1.0, BANK["za"][:], ALU.add, ALU.mult).then_inc(st["gza"], 1)
                        wait_stage(dve, st["a_u"], t)
                        wait_stage(dve, st["gzb"], t)
                        yield nc.vector.scalar_tensor_tensor(ug[:], ug[:], 0.5, thb[:], ALU.mult, ALU.mult).then_inc(st["half_y"], 1)
                        wait_stage(dve, st["p_mix"], t)
                        wait_stage(dve, st["half_y"], t)
                        yield nc.vector.tensor_tensor(v3(thb[:]), v3(MX[:]), b_sT[:].unsqueeze(2).to_broadcast([P, BG, 64]), ALU.add).then_inc(st["bias_y"], 1)
                        wait_stage(dve, st["bias_y"], t)
                        yield nc.vector.tensor_tensor(mixed[:, AW:D], ug[:], thb[:], ALU.mult).then_inc(st["mixed"], 1)

                    ops = tile_ops()
                    for g in range(GROUPS):
                        score(g)
                        next(ops, None)
                        total(g)
                    for _ in ops:
                        pass
                    dve.wait_ge(fr[3], (t + (LEAD + 1)) * USES)
                    dve.sem_inc(st["scored"], 1)
                tiles(dve, body)

            @block.tensor
            def _(pe):
                for n in ("turned", "p_vb", "p_u", "p_zb", "p_za", "p_q", "p_k", "p_v", "p_fg", "p_mix"):
                    pe.sem_inc(st[n], LEAD)

                def turn(t, slot):
                    wait_stage(pe, st["xn"], t)
                    wait_stage(pe, st["xT"], t, back=1)
                    for k in range(KC):
                        op = nc.tensor.transpose(TR[k // 4][:, (k % 4) * P:(k % 4 + 1) * P], x_in[slot][:, k * P:(k + 1) * P], keep["ident"][:])
                    op.then_inc(st["turned"], 1)
                turn(0, 0)

                def body(t, pair, r, last):
                    def project(name, bank_users):
                        for stage, back in bank_users:
                            wait_stage(pe, st[stage], t, back=back)
                        for k in range(KC):
                            op = nc.tensor.matmul(BANK[name][:], xT[r][:, k, :], w[:, k, COL[name]:COL[name] + 512], start=k == 0, stop=k == KC - 1)
                        op.then_inc(st[f"p_{name}"], 1)
                    wait_stage(pe, st["xT"], t)
                    project("vb", [("a_q", 1)])
                    project("u", [("a_k", 1)])
                    project("zb", [("a_v", 1)])
                    wait_stage(pe, st["fg_out"], t, back=1)
                    for k in range(KC):
                        op = nc.tensor.matmul(SM[:, 0:AH], xT[r][:, k, :], w[:, k, COL["fg"]:COL["fg"] + AH], start=k == 0, stop=k == KC - 1)
                    op.then_inc(st["p_fg"], 1)
                    project("za", [("gza", 1)])
                    project("q", [("a_vb", 0)])
                    project("k", [("a_u", 0)])
                    if not last:
                        turn(t + 1, 1 - r)
                    project("v", [("gzb", 0)])
                    wait_stage(pe, st["vn2"], t)
                    wait_stage(pe, st["bias_y"], t, back=1)
                    for g in range(BG):
                        op = nc.tensor.matmul(MX[:, g * 64:(g + 1) * 64], mixT[:, g, :], vg[:, g * 64:(g + 1) * 64], start=True, stop=True)
                    op.then_inc(st["p_mix"], 1)
                tiles(pe, body)


def decode_softmax(nc, io, keep):
    HG = AH * PAGES
    with ExitStack() as st:
        s = Scope(nc, st, "dm")
        rows = s.sb("rows", [P, 4, D])
        lf = s.sb("lf", [P, NB, HG])
        later = s.sb("later", [P, NB, HG])
        run = s.sb("run", [P, NB * HG])
        run_t = s.sb("run_t", [P, AH * NT])
        idx = s.sb("idx", [P, 4], I32)
        pz, sz = s.sb("pz", [P, NT * AH]), s.sb("sz", [NB, AH])
        plf, slf = s.sb("plf", [P, NT, AH]), s.sb("slf", [NB, AH])
        plf_h = s.sb("plf_h", [P, AH, NT])
        pincl = s.sb("pincl", [P, AH * NT])
        mx = s.sb("mx", [P, NB * AH])
        mx1 = s.sb("mx1", [NB * AH, 1])
        diag = s.sb("diag", [NB * AH, NB * AH])
        total = s.sb("total", [P, NB * AH])
        B = [s.ps(f"B{i}") for i in range(8)]
        loads = s.sems("idx rows")
        stored = s.sem("self_out")
        back = s.sem("self_in")
        outs = s.sem("outs")
        run_ready = s.sem("run_ready")
        step = Chain(s.sem("step"), "abs exp ln logf self turn lf "
                     "scan later prompt_h prompt_scan prompt_excl suffix bias cum negc max turn_max max1 diag spread "
                     "minus exps sums spread_sums inverse norm".split())
        scores = keep["scores"]
        flat = scores[:].rearrange("p b h g -> p (b h) g")
        block = st.enter_context(nc.Block())

        @block.sync
        def _(sp):
            with nc.allow_non_contiguous_dma(reason="512 page numbers"):
                sp.dma_start(idx[:], io["page_table"].rearrange("b g -> (b g)").rearrange("(i p) -> p i", p=P)).then_inc(loads["idx"], 16)
            sp.wait_ge(step.sem, step.names.index("logf") + 1)
            with nc.allow_non_contiguous_dma(reason="gates are eight wide"):
                sp.dma_start(io["logf_prompt"].rearrange("(t p) h -> p t h", p=P), plf[:]).then_inc(outs, 16)
                sp.dma_start(io["logf_sample"], slf[:]).then_inc(outs, 16)
            sp.wait_ge(step.sem, step.names.index("self") + 1)
            sp.dma_start(io["self_row"], keep["s_self"][:]).then_inc(stored, 16)
            sp.wait_ge(stored, 16)
            with nc.allow_non_contiguous_dma(reason="64 scores"):
                sp.dma_start(scores[0:1, :, :, PAGES], io["self_row"].rearrange("(o b) h -> o b h", o=1)).then_inc(back, 16)
            sp.wait_ge(step.sem, len(step.names))
            with nc.allow_non_contiguous_dma(reason="64 weights"):
                sp.dma_start(io["self_row"].rearrange("(o b) h -> o b h", o=1), scores[0:1, :, :, PAGES]).then_inc(stored, 16)
            sp.wait_ge(stored, 32)
            sp.dma_start(keep["s_self"][:], io["self_row"]).then_inc(back, 16)
            sp.wait_ge(back, 32)
            sp.wait_ge(outs, 32)

        @block.gpsimd
        def _(pool):
            pool.wait_ge(loads["idx"], 16)
            for i in range(4):
                pool.indirect_dma_start(out=rows[:, i, :], out_offset=None, in_=io["cache_logf"],
                                        in_offset=bass.IndirectOffsetOnAxis(ap=idx[:, i:i + 1], axis=0)).then_inc(loads["rows"], 16)
            nc.gpsimd.memset(run[:], 1.0).then_inc(run_ready, 1)
            pool.wait_ge(run_ready, 1)
            nc.gpsimd.memset(run[:].rearrange("p (n g) -> p n g", g=PAGES)[:, :, 0:1], 0.0).then_inc(run_ready, 1)
            nc.gpsimd.memset(run_t[:], 1.0).then_inc(run_ready, 1)
            pool.wait_ge(run_ready, 3)
            nc.gpsimd.memset(run_t[:].rearrange("p (h t) -> p h t", t=NT)[:, :, 0:1], 0.0).then_inc(run_ready, 1)

        @block.scalar
        def _(act):
            nc.scalar.activation(pz[:], keep["fg"][:].rearrange("p t h -> p (t h)"), ACT.Abs)
            nc.scalar.activation(sz[:], keep["s_fg"][:], ACT.Abs).then_inc(step.sem, 1)
            step.wait(act, "exp")
            nc.scalar.activation(pz[:], pz[:], ACT.Exp, scale=-1.0)
            nc.scalar.activation(sz[:], sz[:], ACT.Exp, scale=-1.0).then_inc(step.sem, 1)
            step.wait(act, "ln")
            nc.scalar.activation(pz[:], pz[:], ACT.Ln, bias=1.0)
            nc.scalar.activation(sz[:], sz[:], ACT.Ln, bias=1.0).then_inc(step.sem, 1)
            step.wait(act, "lf")
            for i in range(4):
                for h in range(2):
                    dst = lf[:, 2 * i:2 * i + 2, 256 * h:256 * h + 256].rearrange("p b (h g) -> p h b g", h=4)
                    op = nc.scalar.activation(dst, B[2 * i + h][:].rearrange("p (h b g) -> p h b g", h=4, b=2), ACT.Copy)
            op.then_inc(step.sem, 1)
            step.wait(act, "negc")
            nc.scalar.activation(keep["negc"][:].rearrange("p t h -> p h t"), B[0][:, 0:P].rearrange("p (h t) -> p h t", t=NT), ACT.Copy, scale=-1.0).then_inc(step.sem, 1)
            step.wait(act, "exps")
            nc.scalar.activation(flat, flat, ACT.Exp).then_inc(step.sem, 1)

        @block.vector
        def _(dve):
            step.wait(dve, "logf")
            nc.vector.scalar_tensor_tensor(plf[:].rearrange("p t h -> p (t h)"), keep["fg"][:].rearrange("p t h -> p (t h)"), 0.0, pz[:], ALU.min, ALU.subtract)
            nc.vector.scalar_tensor_tensor(slf[:], keep["s_fg"][:], 0.0, sz[:], ALU.min, ALU.subtract).then_inc(step.sem, 1)
            step.wait(dve, "self")
            nc.vector.tensor_tensor(keep["s_self"][:], keep["s_self"][:], slf[:], ALU.subtract).then_inc(step.sem, 1)
            step.wait(dve, "scan")
            dve.wait_ge(run_ready, 4)
            nc.vector.tensor_tensor_scan(later[:].rearrange("p b n -> p (b n)"), run[:], lf[:].rearrange("p b n -> p (b n)"), 0.0, ALU.mult, ALU.add).then_inc(step.sem, 1)
            step.wait(dve, "later")
            l4 = later[:].rearrange("p b (h g) -> p (b h) g", g=PAGES)
            nc.vector.tensor_copy(total[:], l4[:, :, PAGES - 1:PAGES].rearrange("p n g -> p (n g)")).then_inc(step.sem, 1)
            step.wait(dve, "prompt_h")
            nc.vector.tensor_tensor(l4, total[:].unsqueeze(2).to_broadcast([P, NB * AH, PAGES]), l4, ALU.subtract)
            nc.vector.tensor_copy(plf_h[:], plf[:].rearrange("p t h -> p h t")).then_inc(step.sem, 1)
            step.wait(dve, "prompt_scan")
            nc.vector.tensor_tensor_scan(pincl[:], run_t[:], plf_h[:].rearrange("p h t -> p (h t)"), 0.0, ALU.mult, ALU.add).then_inc(step.sem, 1)
            step.wait(dve, "prompt_excl")
            nc.vector.tensor_tensor(pincl[:], pincl[:], plf_h[:].rearrange("p h t -> p (h t)"), ALU.subtract).then_inc(step.sem, 1)
            step.wait(dve, "bias")
            for b in range(NB):
                op = nc.vector.tensor_tensor(scores[:, b, :, 0:PAGES], scores[:, b, :, 0:PAGES], B[b][:].rearrange("p (h g) -> p h g", h=AH), ALU.add)
            op.then_inc(step.sem, 1)
            dve.wait_ge(back, 16)
            step.wait(dve, "max")
            nc.vector.tensor_reduce(mx[:], flat, AX.X, ALU.max).then_inc(step.sem, 1)
            step.wait(dve, "max1")
            nc.vector.tensor_reduce(mx1[:], B[1][0:NB * AH, 0:P], AX.X, ALU.max).then_inc(step.sem, 1)
            step.wait(dve, "diag")
            nc.vector.tensor_scalar(diag[:], keep["ident"][0:NB * AH, 0:NB * AH], mx1[:], None, ALU.mult).then_inc(step.sem, 1)
            step.wait(dve, "minus")
            nc.vector.tensor_tensor(flat, flat, B[2][:, 0:NB * AH].unsqueeze(2).to_broadcast([P, NB * AH, PAGES + 1]), ALU.subtract).then_inc(step.sem, 1)
            step.wait(dve, "sums")
            nc.vector.tensor_reduce(mx[:], flat, AX.X, ALU.add).then_inc(step.sem, 1)
            step.wait(dve, "inverse")
            nc.vector.reciprocal(total[:], B[3][:, 0:NB * AH]).then_inc(step.sem, 1)
            step.wait(dve, "norm")
            nc.vector.tensor_tensor(flat, flat, total[:].unsqueeze(2).to_broadcast([P, NB * AH, PAGES + 1]), ALU.mult).then_inc(step.sem, 1)

        @block.tensor
        def _(pe):
            pe.wait_ge(loads["rows"], 64)
            step.wait(pe, "turn")
            for i in range(4):
                for h in range(AH):
                    op = nc.tensor.transpose(B[2 * i + h // 4][:, (h % 4) * P:(h % 4 + 1) * P], rows[:, i, h:D:AH], keep["ident"][:])
            op.then_inc(step.sem, 1)
            step.wait(pe, "suffix")
            for b in range(NB):
                nc.tensor.matmul(B[b][:], keep["after"][:], lf[:, b, :], start=True, stop=False)
                op = nc.tensor.matmul(B[b][:], keep["ones"][:], later[:, b, :], start=False, stop=True)
            op.then_inc(step.sem, 1)
            step.wait(pe, "cum")
            nc.tensor.matmul(B[0][:, 0:P], keep["upto"][:], plf_h[:].rearrange("p h t -> p (h t)"), start=True, stop=False)
            nc.tensor.matmul(B[0][:, 0:P], keep["ones"][:], pincl[:], start=False, stop=True).then_inc(step.sem, 1)
            step.wait(pe, "turn_max")
            nc.tensor.transpose(B[1][0:NB * AH, 0:P], mx[:], keep["ident"][:]).then_inc(step.sem, 1)
            step.wait(pe, "spread")
            nc.tensor.matmul(B[2][:, 0:NB * AH], keep["ones"][0:NB * AH, :], diag[:], start=True, stop=True).then_inc(step.sem, 1)
            step.wait(pe, "spread_sums")
            nc.tensor.matmul(B[3][:, 0:NB * AH], keep["ones"][:], mx[:], start=True, stop=True).then_inc(step.sem, 1)


def attend(nc, io, keep):
    with ExitStack() as st:
        s = Scope(nc, st, "at")
        w_out = s.sb("w_out", [P, KC, D])
        KT = s.sb("KT", [AD + 1, AH, SEQ])
        V = s.sb("V", [P, NT, AW])
        QT = s.sb("QT", [AD + 1, AH, P])
        k_in = s.sb("k_in", [P, AH, AD + 1])
        q_in = s.sb("q_in", [P, AH, AD + 1])
        q_head = [s.sb(f"q_head{i}", [AD + 1, P]) for i in range(2)]
        prob = [s.sb(f"prob{i}", [P, SEQ]) for i in range(2)]
        probT = [s.sb(f"probT{i}", [P, 512]) for i in range(2)]
        mix = s.sb("mix", [P, D])
        x_in = s.sb("x_in", [P, D])
        yT = s.sb("yT", [P, KC, P])
        h_out = s.sb("h_out", [P, D])
        vpage = [s.sb(f"vpage{i}", [P, AW]) for i in range(4)]
        nmax = [s.sb(f"nmax{i}", [P, 1]) for i in range(2)]
        psum = [s.sb(f"psum{i}", [P, AH]) for i in range(2)]
        pinv = s.sb("pinv", [P, AH])
        zero = s.sb("zero", [P, 8])
        pages = s.sb("pages", [1, NB * PAGES], I32)
        S = s.ps("S", (P, SEQ))
        T = [s.ps(f"T{i}") for i in range(2)]
        O = s.ps("O")
        DEC = s.ps("DEC")

        w_in, consts, pages_in = s.sem("w_in"), s.sem("consts"), s.sem("pages_in")
        ld = s.sems("k q v mix x vp0 vp1 vp2 vp3")
        h_stored = s.sem("h_stored")
        q_ready = s.sem("q_ready")
        scored = s.sem("scored")
        maxed = s.sem("maxed")
        exped = s.sem("exped")
        turned = s.sem("turned")
        evac = s.sem("evac")
        used = s.sem("used")
        summed = s.sem("summed")
        augmented = s.sem("augmented")
        inverse, scaled, gated, h_ready = (s.sem(n) for n in ("inverse", "scaled", "gated", "h_ready"))
        C = 2

        def blocks(t):
            return -(-(t + 1) // 4)

        base, pbase = [4], [0]
        for u in range(NT):
            base.append(base[-1] + AH * blocks(u) + 8)
            pbase.append(pbase[-1] + AH * blocks(u))

        def head_item(t, h):
            late = 4 if isinstance(h, int) and h == AH - 1 and t < NT - 1 else 0
            return h * blocks(t) + (base[t] + late)

        def kq_item(t):
            return base[t - 1] + (AH - 1) * blocks(t - 1) if t else 0

        def y_item(t):
            return base[t] + AH * blocks(t) + (4 if t < NT - 1 else 0)

        main = st.enter_context(ExitStack())
        block = main.enter_context(nc.Block())

        @block.sync
        def _(sp):
            for j in range(4):
                sp.sem_inc(ld[f"vp{j}"], 16 * C)
            sp.dma_start(pages[:], io["page_table"].rearrange("(o b) p -> o (b p)", o=1)).then_inc(pages_in, 16)

            def rows(t):
                at = slice(t * P, (t + 1) * P)
                if t:
                    sp.wait_ge(turned, C + kq_item(t - 1) + 4)
                sp.dma_start(k_in[:, :, 0:AD], io["k_prompt"][at, :].rearrange("p (h d) -> p h d", h=AH)).then_inc(ld["k"], 16)
                sp.dma_start(q_in[:, :, 0:AD], io["q_prompt"][at, :].rearrange("p (h d) -> p h d", h=AH)).then_inc(ld["q"], 16)
                sp.dma_start(V[:, t, :], io["v_prompt"][at, :]).then_inc(ld["v"], 16)
            rows(0)
            sp.wait_ge(pages_in, 16)
            for k in range(KC):
                sp.dma_start(w_out[:, k, :], io["even_w_out"][k * P:(k + 1) * P, :]).then_inc(w_in, 16)
            for t in range(NT):
                if t + 1 < NT:
                    rows(t + 1)
                with sp.Fori(0, AH) as h:
                    sp.wait_ge(summed, h + (C + t * AH))
                    for j in range(4):
                        page = sp.value_load(pages[0:1, bass.ds(h * 4 + (t * 32 + j), 1)], min_val=0, max_val=N_PHYS - 1)
                        sp.dma_start(vpage[j][:], io["cache_v"][bass.ds(page * P, P), :]).then_inc(ld[f"vp{j}"], 16)

        @block.gpsimd
        def _(pool):
            pool.sem_inc(q_ready, C)
            nc.gpsimd.memset(q_in[:, :, AD:AD + 1], 1.0).then_inc(consts, 1)
            nc.gpsimd.memset(zero[:], 0.0).then_inc(consts, 1)

            def augment(t):
                if t:
                    pool.wait_ge(turned, C + kq_item(t - 1) + 4)
                nc.gpsimd.tensor_copy(k_in[:, :, AD:AD + 1], keep["negc"][:, t, :].unsqueeze(2)).then_inc(augmented, 1)

            def rows(t):
                if t:
                    pool.wait_ge(turned, C + y_item(t - 1) + 2)
                pool.dma_start(mix[:], io["mix_scratch"][t * P:(t + 1) * P, :]).then_inc(ld["mix"], 16)
                if t:
                    pool.wait_ge(h_ready, t)
                pool.dma_start(x_in[:], io["x_prompt"][t * P:(t + 1) * P, :]).then_inc(ld["x"], 16)
            augment(0)
            rows(0)

            def copy_query(t, h, r):
                pool.wait_ge(scored, h + (C + t * AH - 1))
                nc.gpsimd.tensor_copy(q_head[r][:], QT[:, bass.ds(h, 1), :].rearrange("p a n -> p (a n)")).then_inc(q_ready, 1)

            def first_queries(t):
                pool.wait_ge(evac, C + kq_item(t) + 4)
                copy_query(t, 0, 0)
                copy_query(t, 1, 1)
            first_queries(0)
            for t in range(NT):
                if t + 1 < NT:
                    augment(t + 1)
                with pool.Fori(0, AH // 2 - 1) as i:
                    copy_query(t, i * 2 + 2, 0)
                    copy_query(t, i * 2 + 3, 1)
                if t + 1 < NT:
                    first_queries(t + 1)
                pool.wait_ge(evac, C + y_item(t) + 4)
                pool.wait_ge(ld["x"], 16 * (t + 1))
                nc.gpsimd.tensor_tensor(h_out[:], h_out[:], x_in[:], ALU.add).then_inc(h_ready, 1)
                pool.wait_ge(h_ready, t + 1)
                pool.dma_start(io["h1"][t * P:(t + 1) * P, :], h_out[:]).then_inc(h_stored, 16)
                if t + 1 < NT:
                    rows(t + 1)
            pool.wait_ge(h_stored, 16 * NT)

        @block.scalar
        def _(act):
            act.sem_inc(exped, C)
            act.sem_inc(evac, C)

            def keys_queries(t):
                n = kq_item(t)
                if t:
                    act.wait_ge(q_ready, C + t * AH)
                for m in range(4):
                    dst = (KT[:, 4 * m:4 * m + 4, t * P:(t + 1) * P] if m < 2 else QT[:, 4 * m - 8:4 * m - 4, :])
                    act.wait_ge(turned, n + m + C + 1)
                    nc.scalar.activation(dst, T[(n + m) % 2][0:AD + 1, :].rearrange("p (h n) -> p h n", h=4), ACT.Copy).then_inc(evac, 1)

            def exp(t, h, r):
                cols = (t + 1) * P
                lo = 1024 * r if t < 8 else 0
                act.wait_ge(maxed, h + (C + t * AH + 1))
                act.wait_ge(inverse, C + t - 1)
                nc.scalar.activation(prob[r][:, 0:cols], S[:, lo:lo + cols], ACT.Exp, bias=nmax[r][:],
                                     accum_out=psum[t % 2][:, bass.ds(h, 1)]).then_inc(exped, 1)

            def evacuate(t, h, r):
                nb = blocks(t)
                for b in range(nb):
                    i = (r * nb + b) % 2
                    cols = min(512, (t + 1) * P - 512 * b)
                    act.wait_ge(turned, head_item(t, h) + (b + C + 1))
                    act.wait_ge(used, h * nb + (pbase[t] + b + C - 1))
                    nc.scalar.activation(probT[i][:, 0:cols], T[i][:, 0:cols], ACT.Copy).then_inc(evac, 1)

            keys_queries(0)
            exp(0, 0, 0)
            for t in range(NT):
                with act.Fori(0, AH // 2 - 1) as i:
                    evacuate(t, i * 2, 0)
                    exp(t, i * 2 + 1, 1)
                    evacuate(t, i * 2 + 1, 1)
                    exp(t, i * 2 + 2, 0)
                evacuate(t, AH - 2, 0)
                exp(t, AH - 1, 1)
                if t + 1 < NT:
                    keys_queries(t + 1)
                evacuate(t, AH - 1, 1)
                if t + 1 < NT:
                    exp(t + 1, 0, 0)
                n = y_item(t)
                for m in range(2):
                    act.wait_ge(turned, C + n + m + 1)
                    nc.scalar.activation(yT[:, 4 * m:4 * m + 4, :], T[m][:].rearrange("p (k n) -> p k n", k=4), ACT.Copy).then_inc(evac, 1)
                for m in range(2):
                    act.wait_ge(turned, C + n + 2 + m + 1)
                    if t:
                        act.wait_ge(h_stored, 16 * t)
                    nc.scalar.activation(h_out[:, 512 * m:512 * m + 512], T[m][:], ACT.Copy).then_inc(evac, 1)

        @block.vector
        def _(dve):
            dve.sem_inc(maxed, C)
            dve.sem_inc(inverse, C)

            def maximum(t, h, r):
                cols = (t + 1) * P
                lo = 1024 * r if t < 8 else 0
                dve.wait_ge(scored, h + (C + t * AH + 1))
                dve.wait_ge(exped, h + (C + t * AH - 1))
                nc.vector.tensor_reduce(nmax[r][:], S[:, lo:lo + cols], AX.X, ALU.max, negate=True).then_inc(maxed, 1)

            maximum(0, 0, 0)
            for t in range(NT):
                with dve.Fori(0, AH // 2 - 1) as i:
                    maximum(t, i * 2 + 1, 1)
                    maximum(t, i * 2 + 2, 0)
                maximum(t, AH - 1, 1)
                dve.wait_ge(exped, C + (t + 1) * AH)
                nc.vector.reciprocal(pinv[:], psum[t % 2][:]).then_inc(inverse, 1)
                if t + 1 < NT:
                    maximum(t + 1, 0, 0)
                wide = pinv[:].unsqueeze(2).to_broadcast([P, AH, AD])
                dve.wait_ge(used, C + pbase[t + 1])
                dve.wait_ge(inverse, C + t + 1)
                if t:
                    dve.wait_ge(h_stored, 16 * t)
                nc.vector.scalar_tensor_tensor(h_out[:, 0:AW].rearrange("p (h d) -> p h d", h=AH), O[:].rearrange("p (h d) -> p h d", h=AH),
                                               0.5, wide, ALU.mult, ALU.mult).then_inc(scaled, 1)
                dve.wait_ge(scaled, t + 1)
                dve.wait_ge(ld["mix"], 16 * (t + 1))
                nc.vector.tensor_tensor(mix[:, 0:AW], mix[:, 0:AW], h_out[:, 0:AW], ALU.mult).then_inc(gated, 1)
            dve.wait_ge(summed, C + NT * AH)
            nc.vector.tensor_copy(keep["s_dec"][:], DEC[:, 0:64]).then_inc(consts, 1)

        @block.tensor
        def _(pe):
            for q in (scored, turned, used, summed):
                pe.sem_inc(q, C)

            def keys_queries(t):
                n = kq_item(t)
                pe.wait_ge(ld["k"], 16 * (t + 1))
                pe.wait_ge(ld["q"], 16 * (t + 1))
                pe.wait_ge(ld["v"], 16 * (t + 1))
                pe.wait_ge(augmented, t + 1)
                for m in range(4):
                    pe.wait_ge(evac, n + m + C - 1)
                    src = k_in if m < 2 else q_in
                    for j in range(4):
                        op = nc.tensor.transpose(T[(n + m) % 2][0:AD + 1, j * P:(j + 1) * P], src[:, 4 * (m % 2) + j, :], keep["ident"][:])
                    op.then_inc(turned, 1)

            def score(t, h, r):
                lo = 1024 * r if t < 8 else 0
                pe.wait_ge(q_ready, h + (C + t * AH + 1))
                pe.wait_ge(exped, h + (C + t * AH - (1 if t < 8 else 0)))
                end = (t + 1) * P
                for b in range(blocks(t)):
                    hi = min(end, 512 * b + 512)
                    nc.tensor.matmul(S[:, lo + 512 * b:lo + hi], q_head[r][:],
                                     KT[:, bass.ds(h, 1), 512 * b:hi].rearrange("p a n -> p (a n)"), start=True, stop=True)
                nc.tensor.matmul(S[:, lo + end - P:lo + end], keep["ident_bf"][:], keep["mask_bf"][:], start=False, stop=True,
                                 skip_group_check=True).then_inc(scored, 1)

            def weigh(t, h, r):
                nb = blocks(t)
                pe.wait_ge(exped, h + (C + t * AH + 1))

                def turn(b):
                    i = (r * nb + b) % 2
                    pe.wait_ge(evac, head_item(t, h) + (b + C - 1))
                    for j in range(4 * b, min(4 * b + 4, t + 1)):
                        op = nc.tensor.transpose(T[i][:, (j - 4 * b) * P:(j - 4 * b + 1) * P], prob[r][:, j * P:(j + 1) * P], keep["ident"][:])
                    op.then_inc(turned, 1)

                def product(b):
                    i = (r * nb + b) % 2
                    pe.wait_ge(evac, head_item(t, h) + (b + C + 1))
                    for j in range(4 * b, min(4 * b + 4, t + 1)):
                        op = nc.tensor.matmul(O[:, bass.ds(h * AD, AD)], probT[i][:, (j - 4 * b) * P:(j - 4 * b + 1) * P],
                                              V[:, j, bass.ds(h * AD, AD)], start=j == 0, stop=j == t, skip_group_check=True)
                    op.then_inc(used, 1)
                    return op
                turn(0)
                for b in range(nb):
                    if b + 1 < nb:
                        turn(b + 1)
                    product(b)

            def pages_of(t, h):
                for j in range(4):
                    pe.wait_ge(ld[f"vp{j}"], h * 16 + 16 * (C + t * AH + 1))
                    for c in range(4):
                        col = (t // 2) * 8 + 2 * c
                        op = nc.tensor.matmul(DEC[:, col:col + 2], vpage[j][:, c * P:(c + 1) * P],
                                              keep["scores"][:, t // 2, 2 * c:2 * c + 2, bass.ds(h * 4 + ((t % 2) * 32 + j), 1)].rearrange("p h a -> p (h a)"),
                                              start=False, stop=False, skip_group_check=True)
                op.then_inc(summed, 1)

            pe.wait_ge(consts, 2)
            keys_queries(0)
            pe.wait_ge(evac, C + 4)
            score(0, 0, 0)
            for t in range(NT):
                if t:
                    pe.wait_ge(scaled, t)
                if t % 2 == 0:
                    nc.tensor.matmul(DEC[:, (t // 2) * 8:(t // 2) * 8 + 8], keep["ident"][:], zero[:], start=True, stop=False, skip_group_check=True)
                with pe.Fori(0, AH // 2 - 1) as i:
                    for r in range(2):
                        score(t, i * 2 + (r + 1), 1 - r)
                        weigh(t, i * 2 + r, r)
                        pages_of(t, i * 2 + r)
                score(t, AH - 1, 1)
                weigh(t, AH - 2, 0)
                pages_of(t, AH - 2)
                if t + 1 < NT:
                    keys_queries(t + 1)
                weigh(t, AH - 1, 1)
                pages_of(t, AH - 1)
                if t + 1 < NT:
                    pe.wait_ge(evac, C + kq_item(t + 1) + 4)
                    score(t + 1, 0, 0)
                n = y_item(t)
                pe.wait_ge(gated, t + 1)
                for m in range(2):
                    pe.wait_ge(evac, n + m + C - 1)
                    for j in range(4):
                        op = nc.tensor.transpose(T[m][:, j * P:(j + 1) * P], mix[:, (4 * m + j) * P:(4 * m + j + 1) * P], keep["ident"][:])
                    op.then_inc(turned, 1)
                if t == 0:
                    pe.wait_ge(w_in, 16 * KC)
                for m in range(2):
                    pe.wait_ge(evac, n + 2 + m + C)
                    for k in range(KC):
                        op = nc.tensor.matmul(T[m][:], yT[:, k, :], w_out[:, k, 512 * m:512 * m + 512], start=k == 0, stop=k == KC - 1)
                    op.then_inc(turned, 1)

        main.close()

        with ExitStack() as st2:
            s2 = Scope(nc, st2, "as")
            step = Chain(s2.sem("step"), "evens odds turn self_v add_v gate turn_y yT project residual".split())
            load, stored = s2.sem("load"), s2.sem("stored")
            attT = probT[0][:, 0:4 * NB].rearrange("p (c b) -> p c b", b=NB)
            rows, xs, vs, own = mix[0:NB, :], x_in[0:NB, :], h_out[0:NB, 0:AW], h_out[0:NB, AW:D]
            block = st2.enter_context(nc.Block())
            v3 = lambda ap: ap.rearrange("p (h d) -> p h d", h=AH)

            @block.sync
            def _(sp):
                sp.dma_start(rows, io["s_mixed"]).then_inc(load, 16)
                sp.dma_start(xs, io["x_sample"]).then_inc(load, 16)
                sp.dma_start(vs, io["v_sample"]).then_inc(load, 16)
                sp.wait_ge(step.sem, len(step.names))
                sp.dma_start(io["h1_sample"], xs).then_inc(stored, 16)
                sp.wait_ge(stored, 16)

            @block.scalar
            def _(act):
                step.wait(act, "yT")
                nc.scalar.activation(yT[:, :, 0:NB], T[1][:, 0:KC * NB].rearrange("p (k b) -> p k b", b=NB), ACT.Copy).then_inc(step.sem, 1)

            @block.vector
            def _(dve):
                dec = keep["s_dec"][:].rearrange("p (b c e) -> p c b e", b=NB, c=4)
                nc.vector.tensor_copy(attT[0:AD, :, :], dec[0:AD, :, :, 0]).then_inc(step.sem, 1)
                step.wait(dve, "odds")
                nc.vector.tensor_copy(attT[AD:P, :, :], dec[AD:P, :, :, 1]).then_inc(step.sem, 1)
                dve.wait_ge(load, 48)
                step.wait(dve, "self_v")
                nc.vector.tensor_tensor(v3(own), v3(vs), keep["s_self"][:].unsqueeze(2).to_broadcast([NB, AH, AD]), ALU.mult).then_inc(step.sem, 1)
                step.wait(dve, "add_v")
                nc.vector.tensor_tensor(own, own, T[0][0:NB, :], ALU.add).then_inc(step.sem, 1)
                step.wait(dve, "gate")
                nc.vector.scalar_tensor_tensor(rows[:, 0:AW], own, 0.5, rows[:, 0:AW], ALU.mult, ALU.mult).then_inc(step.sem, 1)
                step.wait(dve, "residual")
                nc.vector.tensor_tensor(xs, xs, S[0:NB, 0:D], ALU.add).then_inc(step.sem, 1)

            @block.tensor
            def _(pe):
                step.wait(pe, "turn")
                for c in range(4):
                    op = nc.tensor.transpose(T[0][0:NB, c * P:(c + 1) * P], attT[:, c, :], keep["ident"][:])
                op.then_inc(step.sem, 1)
                step.wait(pe, "turn_y")
                for k in range(KC):
                    op = nc.tensor.transpose(T[1][:, k * NB:(k + 1) * NB], rows[:, k * P:(k + 1) * P], keep["ident"][0:NB, 0:NB])
                op.then_inc(step.sem, 1)
                step.wait(pe, "project")
                for m in range(2):
                    for k in range(KC):
                        op = nc.tensor.matmul(S[0:NB, 512 * m:512 * m + 512], yT[:, k, 0:NB], w_out[:, k, 512 * m:512 * m + 512], start=k == 0, stop=k == KC - 1)
                op.then_inc(step.sem, 1)


def mlstm(nc, io, keep):
    with ExitStack() as st:
        s = Scope(nc, st, "ml")
        w = s.sb("w", [P, KC, ODD_COLS])
        wq, wk, wv = (s.sb(n, [P, CH, 2, CD]) for n in ("wq", "wk", "wv"))
        g_row, ngh, skiph = (s.sb(n, [P, D]) for n in ("g_row", "ngh", "skiph"))
        cw = s.sb("cw", [P, KC, 4])
        cb = s.sb("cb", [P, KC])
        b_if = s.sb("b_if", [P, 2 * CH])
        B = [s.ps(f"B{i}") for i in range(8)]
        GATES = 3 * CW
        A1 = CD + 1

        with ExitStack() as st2:
            s2 = Scope(nc, st2, "mp")
            x = s2.sb("x", [P, D])
            xT = s2.sb("xT", [P, KC, P])
            xcT = s2.sb("xcT", [P, KC, P + 3])
            cv = s2.sb("cv", [P, KC, P])
            th = s2.sb("th", [P, KC, P])
            qT, kT = s2.sb("qT", [P, KC, P]), s2.sb("kT", [P, KC, P])
            kw = s2.sb("kw", [P, CW])
            va = s2.sb("va", [P, CH, A1])
            state = s2.sb("state", [P, CH, 2, A1])
            sz, tho = s2.sb("sz", [P, D]), s2.sb("tho", [P, D])
            inter = s2.sb("inter", [P, CH, A1])
            wt = s2.sb("wt", [P, CH, P])
            smT = s2.sb("smT", [P, CH, P])
            skx = s2.sb("skx", [P, D])
            ssq, msq, rstd = (s2.sb(n, [P, 1]) for n in ("ssq", "msq", "rstd"))
            g8, e4, lf, bb, gg, ml, mbc, wlh, den, dinv, var4, rs4 = (
                s2.sb(n, [P, k]) for n, k in (("g8", 8), ("e4", 4), ("lf", 4), ("bb", 8), ("gg", 4), ("ml", 4), ("mbc", 4),
                                              ("wlh", 4), ("den", 4), ("dinv", 4), ("var4", 4), ("rs4", 4)))
            dd = s2.sb("dd", [P, 16])
            st6 = s2.sb("st6", [P, CH, 6])
            mv = s2.sb("mv", [P, CH, 2])
            mrow, blrow = s2.sb("mrow", [CH, 1]), s2.sb("blrow", [CH, 1])
            M = s2.sb("M", [CH, P])
            low = s2.sb("low", [CH, P])
            sel = s2.sb("sel", [CH, CH, P])
            loads, const = s2.sem("loads"), s2.sem("const")
            ld = s2.sems("x")
            y_stored = s2.sem("y_stored")
            last_out = s2.sem("last_out")
            q = s2.sems("ssq msq rstd xn "
                        "p_xT p_xc p_z p_g p_o p_cum p_q p_k p_kt p_v p_skip p_gT p_M p_S p_inter p_intra p_c "
                        "a_xT a_xc a_th a_cv0 a_z a_abs a_e a_ln a_o a_q a_k a_kw a_v a_w a_dd a_inter "
                        "d_cv0 d_cv1 d_cv2 d_cv carried d_sz d_g8 d_lf d_bb d_gg d_M d_ml d_dd d_wlh d_m d_skip d_sm d_num "
                        "d_den d_den2 d_dinv d_hc d_st d_mv d_var d_hn d_A d_B d_E d_y d_c rs4")
            INTER, INTRA = (5, 6, 7, 1), (0, 2, 3, 4)
            UPD = INTER + INTRA
            block = st2.enter_context(nc.Block())

            def tiles(eng, body):
                body(0, first=True)
                with eng.Fori(1, NT - 1) as t:
                    body(t)
                body(NT - 1, last=True)

            def begin(eng, names):
                for n in names.split():
                    eng.sem_inc(q[n], LEAD * {"p_inter": 4, "p_intra": 4, "p_c": 8, "a_inter": 4, "d_num": 4, "d_c": 8}.get(n, 1))

            @block.sync
            def _(sp):
                sp.sem_inc(ld["x"], 16 * LEAD)
                sp.sem_inc(y_stored, 16 * LEAD)
                sp.dma_start(x[:], io["h1"][0:P, :]).then_inc(ld["x"], 16)
                for k in range(KC):
                    sp.dma_start(w[:, k, :], io["odd_w_in"][k * P:(k + 1) * P, :]).then_inc(loads, 16)
                for n, dst in (("w_q", wq), ("w_k", wk), ("w_v", wv)):
                    sp.dma_start(dst[:], io[n].rearrange("h (c p) e -> p h c e", p=P)).then_inc(loads, 16)

                def body(t, first=False, last=False):
                    if not last:
                        wait_stage(sp, q["p_xT"], t)
                        sp.dma_start(x[:], io["h1"][bass.ds((t + 1) * P, P), :]).then_inc(ld["x"], 16)
                    wait_stage(sp, q["d_y"], t)
                    sp.dma_start(io["y2"][bass.ds(t * P, P), :], sz[:]).then_inc(y_stored, 16)
                tiles(sp, body)
                wait_stage(sp, q["d_c"], NT - 1, per_tile=8)
                sp.dma_start(io["c_prompt"].rearrange("(h c p) v -> p (h c) v", p=P, c=2), state[:, :, :, 0:CD].rearrange("p h c v -> p (h c) v")).then_inc(last_out, 16)
                with nc.allow_non_contiguous_dma(reason="small outputs"):
                    sp.dma_start(io["n_prompt"].rearrange("o (h c p) -> p (o h) c", p=P, c=2), state[:, :, :, CD]).then_inc(last_out, 16)
                    wait_stage(sp, q["d_m"], NT - 1)
                    sp.dma_start(io["m_prompt"].rearrange("o h -> h o"), mrow[:]).then_inc(last_out, 16)
                    for c in range(KC):
                        sp.dma_start(io["conv_prompt"][:, c * P:(c + 1) * P].rearrange("j p -> p j"), xcT[:, c, P:P + 3]).then_inc(last_out, 16)
                sp.wait_ge(last_out, 16 * (3 + KC))
                wait_dma(sp, y_stored, NT - 1)

            @block.gpsimd
            def _(pool):
                begin(pool, "rstd rs4")
                nc.gpsimd.memset(xcT[:, :, 0:3], 0.0).then_inc(const, 1)
                nc.gpsimd.memset(state[:], 0.0).then_inc(const, 1)
                nc.gpsimd.memset(va[:, :, CD:A1], 1.0).then_inc(const, 1)
                nc.gpsimd.memset(mrow[:], 0.0).then_inc(const, 1)
                nc.gpsimd.memset(mbc[:], 0.0).then_inc(const, 1)
                nc.gpsimd.memset(low[:], -3e38).then_inc(const, 1)
                nc.gpsimd.memset(sel[:], 0.0).then_inc(const, 1)
                pool.wait_ge(const, 7)
                nc.gpsimd.affine_select(out=sel[:], in_=sel[:], compare_op=ALU.not_equal, fill=1.0, base=0,
                                        pattern=[[-1, CH], [0, P]], channel_multiplier=1).then_inc(const, 1)
                pool.wait_ge(loads, 16 * 21)
                nc.gpsimd.tensor_tensor(ngh[:], ngh[:], keep["half"][:].to_broadcast([P, D]), ALU.mult).then_inc(const, 1)
                nc.gpsimd.tensor_tensor(skiph[:], skiph[:], keep["half"][:].to_broadcast([P, D]), ALU.mult).then_inc(const, 1)

                def norm(t):
                    wait_stage(pool, q["xn"], t, back=1)
                    wait_stage(pool, q["msq"], t)
                    nc.gpsimd.tensor_tensor(rstd[:], msq[:], keep["minus_half"][:], ALU.pow).then_inc(q["rstd"], 1)
                norm(0)

                def body(t, first=False, last=False):
                    if not last:
                        norm(t + 1)
                    wait_stage(pool, q["d_var"], t)
                    wait_stage(pool, q["d_hn"], t, back=1)
                    nc.gpsimd.tensor_tensor(rs4[:], var4[:], keep["minus_half"][:].to_broadcast([P, CH]), ALU.pow).then_inc(q["rs4"], 1)
                tiles(pool, body)

            @block.scalar
            def _(act):
                act.dma_start(g_row[:], io["norm_g"][1, :].partition_broadcast(P)).then_inc(loads, 16)
                act.dma_start(ngh[:], io["norm_c"].partition_broadcast(P)).then_inc(loads, 16)
                act.dma_start(skiph[:], io["skip"].partition_broadcast(P)).then_inc(loads, 16)
                act.dma_start(b_if[:, 0:CH], io["odd_b_i"].partition_broadcast(P)).then_inc(loads, 16)
                act.dma_start(b_if[:, CH:2 * CH], io["odd_b_f"].partition_broadcast(P)).then_inc(loads, 16)
                with nc.allow_non_contiguous_dma(reason="convolution weights by channel"):
                    act.dma_start(cb[:], io["conv_b"].rearrange("(c p) -> p c", p=P)).then_inc(loads, 16)
                    act.dma_start(cw[:, :, 0], io["conv_w"][0, :].rearrange("(c p) -> p c", p=P)).then_inc(loads, 16)
                    for j in range(1, 4):
                        act.dma_start(cw[:, :, j], io["conv_w"][j, :].rearrange("(c p) -> p c", p=P)).then_inc(loads, 16)
                begin(act, "ssq a_xT a_xc a_th a_cv0 a_z a_abs a_e a_ln a_o a_q a_k a_kw a_v a_w a_dd a_inter")
                act.wait_ge(loads, 16 * 21)

                def square(t):
                    wait_dma(act, ld["x"], t)
                    wait_stage(act, q["msq"], t, back=1)
                    wait_stage(act, q["d_cv"], t, back=1)
                    nc.scalar.activation(th[:].rearrange("p k n -> p (k n)"), x[:], ACT.Square, accum_out=ssq[:]).then_inc(q["ssq"], 1)

                def turn_out(t):
                    wait_stage(act, q["p_xT"], t)
                    wait_stage(act, q["p_o"], t, back=1)
                    nc.scalar.activation(xT[:, 0:4, :], B[1][:].rearrange("p (k n) -> p k n", k=4), ACT.Copy)
                    nc.scalar.activation(xT[:, 4:8, :], B[4][:].rearrange("p (k n) -> p k n", k=4), ACT.Copy).then_inc(q["a_xT"], 1)
                square(0)
                turn_out(0)

                def body(t, first=False, last=False):
                    k4 = lambda ap: ap.rearrange("p (k n) -> p k n", k=4)
                    wait_stage(act, q["p_xc"], t)
                    wait_stage(act, q["p_v"], t, back=1)
                    wait_stage(act, q["carried"], t, back=1)
                    if first:
                        act.wait_ge(const, 1)
                    for m in range(2):
                        op = nc.scalar.activation(xcT[:, 4 * m:4 * m + 4, 3:P + 3], k4(B[m][:]), ACT.Copy)
                    op.then_inc(q["a_xc"], 1)
                    wait_stage(act, q["a_xc"], t)
                    wait_stage(act, q["p_skip"], t, back=1)
                    wait_stage(act, q["p_kt"], t, back=1)
                    for c in range(KC):
                        op = nc.scalar.activation(cv[:, c, :], xcT[:, c, 3:P + 3], ACT.Identity, bias=cb[:, c:c + 1], scale=cw[:, c, 3:4])
                    op.then_inc(q["a_cv0"], 1)
                    wait_stage(act, q["p_z"], t)
                    wait_dma(act, y_stored, t, back=1)
                    for m in range(2):
                        op = nc.scalar.activation(sz[:, 512 * m:512 * m + 512], B[6 + m][:], ACT.Tanh, scale=0.5)
                    op.then_inc(q["a_z"], 1)
                    wait_stage(act, q["d_cv2"], t)
                    nc.scalar.activation(th[:], cv[:], ACT.Tanh, scale=0.5).then_inc(q["a_th"], 1)
                    wait_stage(act, q["p_o"], t)
                    wait_stage(act, q["d_A"], t, back=1)
                    for m in range(2):
                        op = nc.scalar.activation(tho[:, 512 * m:512 * m + 512], B[m][:], ACT.Tanh, scale=0.5)
                    op.then_inc(q["a_o"], 1)
                    wait_stage(act, q["d_g8"], t)
                    wait_stage(act, q["d_lf"], t, back=1)
                    nc.scalar.activation(e4[:], g8[:, CH:2 * CH], ACT.Abs).then_inc(q["a_abs"], 1)
                    wait_stage(act, q["a_abs"], t)
                    nc.scalar.activation(e4[:], e4[:], ACT.Exp, scale=-1.0).then_inc(q["a_e"], 1)
                    wait_stage(act, q["a_e"], t)
                    nc.scalar.activation(e4[:], e4[:], ACT.Ln, bias=1.0).then_inc(q["a_ln"], 1)
                    wait_stage(act, q["p_q"], t)
                    wait_stage(act, q["p_inter"], t, back=1, per_tile=4)
                    for m in range(2):
                        op = nc.scalar.activation(qT[:, 4 * m:4 * m + 4, :], k4(B[4 + m][:]), ACT.Copy, scale=0.5 * CD ** -0.5)
                    op.then_inc(q["a_q"], 1)
                    wait_stage(act, q["p_k"], t)
                    wait_stage(act, q["p_S"], t, back=1)
                    for m in range(2):
                        op = nc.scalar.activation(kT[:, 4 * m:4 * m + 4, :], k4(B[6 + m][:]), ACT.Copy, scale=0.5)
                    op.then_inc(q["a_k"], 1)
                    wait_stage(act, q["p_v"], t)
                    wait_stage(act, q["p_c"], t, back=1, per_tile=8)
                    for m in range(2):
                        op = nc.scalar.activation(va[:, 2 * m:2 * m + 2, 0:CD], B[4 + m][:].rearrange("p (h v) -> p h v", h=2), ACT.Copy)
                    op.then_inc(q["a_v"], 1)
                    wait_stage(act, q["p_M"], t)
                    wait_stage(act, q["d_gg"], t)
                    wait_stage(act, q["d_sm"], t, back=1)
                    for h in range(CH):
                        op = nc.scalar.activation(wt[:, h, :], B[3][:, h * P:(h + 1) * P], ACT.Exp, bias=gg[:, h:h + 1], scale=-1.0)
                    op.then_inc(q["a_w"], 1)
                    wait_stage(act, q["d_dd"], t)
                    nc.scalar.activation(dd[:], dd[:], ACT.Exp).then_inc(q["a_dd"], 1)
                    wait_stage(act, q["d_wlh"], t)
                    wait_stage(act, q["p_kt"], t)
                    for h in range(CH):
                        op = nc.scalar.activation(kw[:, h * CD:(h + 1) * CD], B[h // 2][:, (h % 2) * CD:(h % 2 + 1) * CD], ACT.Identity, scale=wlh[:, h:h + 1])
                    op.then_inc(q["a_kw"], 1)
                    if not last:
                        square(t + 1)
                        turn_out(t + 1)
                    for h in range(CH):
                        wait_stage(act, q["p_inter"], t, per_tile=4, nth=h + 1)
                        wait_stage(act, q["d_num"], t, back=1, per_tile=4)
                        nc.scalar.activation(inter[:, h, :], B[INTER[h]][:, 0:A1], ACT.Identity, scale=dd[:, h:h + 1]).then_inc(q["a_inter"], 1)
                tiles(act, body)

            @block.vector
            def _(dve):
                begin(dve, "msq xn d_cv0 d_cv1 d_cv2 d_cv carried d_sz d_g8 d_lf d_bb d_gg d_M d_ml d_dd d_wlh d_m d_skip d_sm d_num "
                           "d_den d_den2 d_dinv d_hc d_st d_mv d_var d_hn d_A d_B d_E d_y d_c")
                dve.wait_ge(loads, 16 * 21)
                dve.wait_ge(const, 10)

                def mean_square(t):
                    wait_stage(dve, q["ssq"], t)
                    wait_stage(dve, q["rstd"], t, back=1)
                    nc.vector.tensor_scalar(msq[:], ssq[:], 1.0 / D, EPS, ALU.mult, ALU.add).then_inc(q["msq"], 1)

                def normed(t):
                    wait_stage(dve, q["rstd"], t)
                    nc.vector.scalar_tensor_tensor(x[:], x[:], rstd[:], g_row[:], ALU.mult, ALU.mult).then_inc(q["xn"], 1)
                mean_square(0)
                normed(0)

                def body(t, first=False, last=False):
                    flat = lambda ap: ap.rearrange("p k n -> p (k n)")

                    def small(stage, op):
                        op.then_inc(q[stage], 1)
                        wait_stage(dve, q[stage], t)
                    wait_stage(dve, q["a_cv0"], t)
                    for j, stage in ((0, "d_cv0"), (1, "d_cv1"), (2, "d_cv2")):
                        for c in range(KC):
                            op = nc.vector.scalar_tensor_tensor(cv[:, c, :], xcT[:, c, j:j + P], cw[:, c, j:j + 1], cv[:, c, :], ALU.mult, ALU.add)
                        op.then_inc(q[stage], 1)
                        wait_stage(dve, q[stage], t)
                    if not last:
                        nc.vector.tensor_copy(xcT[:, :, 0:3], xcT[:, :, P:P + 3]).then_inc(q["carried"], 1)
                    wait_stage(dve, q["a_th"], t)
                    nc.vector.scalar_tensor_tensor(flat(cv[:]), flat(th[:]), 1.0, flat(cv[:]), ALU.add, ALU.mult).then_inc(q["d_cv"], 1)
                    wait_stage(dve, q["a_z"], t)
                    for m in range(2):
                        op = nc.vector.scalar_tensor_tensor(sz[:, 512 * m:512 * m + 512], sz[:, 512 * m:512 * m + 512], 1.0, B[6 + m][:], ALU.add, ALU.mult)
                    op.then_inc(q["d_sz"], 1)
                    wait_stage(dve, q["p_g"], t)
                    small("d_g8", nc.vector.tensor_tensor(g8[:], B[2][:, 0:8], b_if[:], ALU.add))
                    wait_stage(dve, q["a_ln"], t)
                    wait_stage(dve, q["p_cum"], t, back=1)
                    small("d_lf", nc.vector.scalar_tensor_tensor(lf[:], g8[:, CH:2 * CH], 0.0, e4[:], ALU.min, ALU.subtract))
                    wait_stage(dve, q["p_cum"], t)
                    small("d_bb", nc.vector.tensor_copy(bb[:], B[2][:, 8:16]))
                    nc.vector.tensor_copy(blrow[:], B[2][0:CH, 16:17])
                    wait_stage(dve, q["a_w"], t, back=1)
                    small("d_gg", nc.vector.tensor_tensor(gg[:], g8[:, 0:CH], bb[:, 0:CH], ALU.subtract))
                    wait_stage(dve, q["p_gT"], t)
                    small("d_M", nc.vector.tensor_tensor_scan(M[:], low[:], B[2][0:CH, 32:32 + P], mrow[:], ALU.max, ALU.max))
                    wait_stage(dve, q["a_w"], t)
                    small("d_ml", nc.vector.tensor_copy(ml[:], B[3][:, P - 1:4 * P:P]))
                    wait_stage(dve, q["d_c"], t, back=1, per_tile=8)
                    nc.vector.tensor_tensor(dd[:, 0:4], mbc[:], B[2][:, 20:24], ALU.subtract)
                    nc.vector.tensor_tensor(dd[:, 4:8], gg[:], ml[:], ALU.subtract)
                    nc.vector.tensor_tensor(dd[:, 8:12], mbc[:], ml[:], ALU.subtract)
                    small("d_dd", nc.vector.scalar_tensor_tensor(dd[:, 12:16], bb[:, 0:4], -1.0, B[2][:, 20:24], ALU.mult, ALU.subtract))
                    nc.vector.tensor_tensor(mbc[:], ml[:], bb[:, 4:8], ALU.add)
                    small("d_m", nc.vector.tensor_tensor(mrow[:], M[:, P - 1:P], blrow[:], ALU.add))
                    wait_stage(dve, q["a_dd"], t)
                    small("d_wlh", nc.vector.tensor_scalar(wlh[:], dd[:, 4:8], 0.5, None, ALU.mult))
                    if not last:
                        mean_square(t + 1)
                    wait_stage(dve, q["p_skip"], t)
                    for m in range(2):
                        op = nc.vector.tensor_tensor(skx[:, 512 * m:512 * m + 512], B[6 + m][:], skiph[:, 512 * m:512 * m + 512], ALU.mult)
                    op.then_inc(q["d_skip"], 1)
                    wait_stage(dve, q["a_w"], t)
                    wait_stage(dve, q["p_S"], t)
                    nc.vector.tensor_tensor(flat(smT[:]), flat(wt[:]), B[0][:], ALU.mult).then_inc(q["d_sm"], 1)
                    if not last:
                        normed(t + 1)
                    for h in range(CH):
                        wait_stage(dve, q["a_inter"], t, per_tile=4, nth=h + 1)
                        wait_stage(dve, q["p_intra"], t, per_tile=4, nth=h + 1)
                        nc.vector.tensor_tensor(inter[:, h, :], inter[:, h, :], B[INTRA[h]][:, 0:A1], ALU.add).then_inc(q["d_num"], 1)
                    for n in range(8):
                        h, c = n // 2, n % 2
                        wait_stage(dve, q["p_c"], t, per_tile=8, nth=n + 1)
                        nc.vector.scalar_tensor_tensor(state[:, h, c, :], state[:, h, c, :], dd[:, 8 + h:9 + h], B[UPD[n]][:, 0:A1], ALU.mult, ALU.add).then_inc(q["d_c"], 1)
                    wait_stage(dve, q["d_num"], t, per_tile=4)
                    dcol = inter[:, :, CD]
                    small("d_den", nc.vector.scalar_tensor_tensor(den[:], dcol, -1.0, dcol, ALU.mult, ALU.max))
                    small("d_den2", nc.vector.tensor_tensor(den[:], den[:], dd[:, 12:16], ALU.max))
                    small("d_dinv", nc.vector.reciprocal(dinv[:], den[:]))
                    for h in range(CH):
                        op = nc.vector.tensor_scalar(inter[:, h, 0:CD], inter[:, h, 0:CD], dinv[:, h:h + 1], None, ALU.mult)
                    small("d_hc", op)
                    for h in range(CH):
                        op = nc.vector.bn_stats(st6[:, h, :], inter[:, h, 0:CD])
                    small("d_st", op)
                    nc.vector.tensor_copy(den[:], dinv[:])
                    for h in range(CH):
                        op = nc.vector.bn_aggr(mv[:, h, :], st6[:, h, :])
                    small("d_mv", op)
                    small("d_var", nc.vector.tensor_scalar(var4[:], mv[:, :, 1], 1.0, EPS, ALU.mult, ALU.add))
                    wait_stage(dve, q["rs4"], t)
                    for h in range(CH):
                        op = nc.vector.tensor_scalar(inter[:, h, 0:CD], inter[:, h, 0:CD], mv[:, h, 0:1], rs4[:, h:h + 1], ALU.subtract, ALU.mult)
                    small("d_hn", op)
                    t4 = tho[:].rearrange("p (h v) -> p h v", h=CH)
                    wait_stage(dve, q["a_o"], t)
                    small("d_A", nc.vector.scalar_tensor_tensor(inter[:, :, 0:CD], t4, 1.0, inter[:, :, 0:CD], ALU.add, ALU.mult))
                    small("d_B", nc.vector.tensor_tensor(inter[:, :, 0:CD], inter[:, :, 0:CD], ngh[:].rearrange("p (h v) -> p h v", h=CH), ALU.mult))
                    small("d_E", nc.vector.tensor_tensor(inter[:, :, 0:CD], inter[:, :, 0:CD], skx[:].rearrange("p (h v) -> p h v", h=CH), ALU.add))
                    sz4 = sz[:].rearrange("p (h v) -> p h v", h=CH)
                    small("d_y", nc.vector.scalar_tensor_tensor(sz4, inter[:, :, 0:CD], 0.5, sz4, ALU.mult, ALU.mult))
                tiles(dve, body)

            @block.tensor
            def _(pe):
                begin(pe, "p_xT p_xc p_z p_g p_o p_cum p_q p_k p_kt p_v p_skip p_gT p_M p_S p_inter p_intra p_c")
                pe.wait_ge(loads, 16 * 21)
                pe.wait_ge(const, 10)

                def turn(t):
                    wait_stage(pe, q["xn"], t)
                    wait_stage(pe, q["a_kw"], t, back=1)
                    wait_stage(pe, q["a_v"], t, back=1)
                    for k in range(KC):
                        op = nc.tensor.transpose(B[1 if k < 4 else 4][:, (k % 4) * P:(k % 4 + 1) * P], x[:, k * P:(k + 1) * P], keep["ident"][:])
                    op.then_inc(q["p_xT"], 1)
                turn(0)

                def body(t, first=False, last=False):
                    def project(banks, col, stage):
                        for m in range(2):
                            for k in range(KC):
                                op = nc.tensor.matmul(B[banks[m]][:], xT[:, k, :], w[:, k, col + 512 * m:col + 512 * m + 512], start=k == 0, stop=k == KC - 1)
                        op.then_inc(q[stage], 1)
                    wait_stage(pe, q["a_xT"], t)
                    wait_stage(pe, q["d_c"], t, back=1, per_tile=8)
                    for c in range(KC):
                        for k in range(KC):
                            op = nc.tensor.matmul(B[c // 4][:, (c % 4) * P:(c % 4 + 1) * P], w[:, k, c * P:(c + 1) * P], xT[:, k, :], start=k == 0, stop=k == KC - 1)
                    op.then_inc(q["p_xc"], 1)
                    project((6, 7), CW, "p_z")
                    for k in range(KC):
                        op = nc.tensor.matmul(B[2][:, 0:8], xT[:, k, :], w[:, k, GATES:GATES + 8], start=k == 0, stop=k == KC - 1)
                    op.then_inc(q["p_g"], 1)
                    wait_stage(pe, q["a_xc"], t)
                    project((0, 1), 2 * CW, "p_o")
                    wait_stage(pe, q["d_lf"], t)
                    nc.tensor.matmul(B[2][:, 8:12], keep["upto"][:], lf[:], start=True, stop=True)
                    nc.tensor.matmul(B[2][:, 12:16], keep["ones"][:], lf[:], start=True, stop=True)
                    nc.tensor.matmul(B[2][0:CH, 16:17], lf[:], keep["ones"][:, 0:1], start=True, stop=True).then_inc(q["p_cum"], 1)
                    wait_stage(pe, q["d_cv"], t)
                    for banks, wt_, stage in (((4, 5), wq, "p_q"), ((6, 7), wk, "p_k")):
                        if stage == "p_k":
                            wait_stage(pe, q["d_sz"], t)
                        for n in range(8):
                            h, e = n // 2, n % 2
                            for c in range(2):
                                op = nc.tensor.matmul(B[banks[n // 4]][:, (n % 4) * P:(n % 4 + 1) * P], wt_[:, h, c, e * P:(e + 1) * P],
                                                      cv[:, 2 * h + c, :], start=c == 0, stop=c == 1)
                        op.then_inc(q[stage], 1)
                    wait_stage(pe, q["a_o"], t)
                    for h in range(CH):
                        for c in range(2):
                            op = nc.tensor.matmul(B[h // 2][:, (h % 2) * CD:(h % 2 + 1) * CD], cv[:, 2 * h + c, :], wk[:, h, c, :], start=c == 0, stop=c == 1)
                    op.then_inc(q["p_kt"], 1)
                    wait_stage(pe, q["d_gg"], t)
                    nc.tensor.transpose(B[2][0:CH, 32:32 + P], gg[:], keep["ident"][:]).then_inc(q["p_gT"], 1)
                    wait_stage(pe, q["a_q"], t)
                    for h in range(CH):
                        for c in range(2):
                            op = nc.tensor.matmul(B[4 + h // 2][:, (h % 2) * CD:(h % 2 + 1) * CD], xcT[:, 2 * h + c, 3:P + 3], wv[:, h, c, :], start=c == 0, stop=c == 1)
                    op.then_inc(q["p_v"], 1)
                    wait_stage(pe, q["a_k"], t)
                    for k in range(KC):
                        op = nc.tensor.transpose(B[6 + k // 4][:, (k % 4) * P:(k % 4 + 1) * P], cv[:, k, :], keep["ident"][:])
                    op.then_inc(q["p_skip"], 1)
                    wait_stage(pe, q["d_M"], t)
                    for h in range(CH):
                        nc.tensor.matmul(B[3][:, h * P:(h + 1) * P], sel[:, h, :], M[:], start=True, stop=True)
                        nc.tensor.matmul(B[3][:, h * P:(h + 1) * P], keep["ident_bf"][:], keep["maskT_bf"][:], start=False, stop=True, skip_group_check=True)
                    nc.tensor.transpose(B[2][:, 20:24], M[:], keep["ident"][0:CH, 0:CH]).then_inc(q["p_M"], 1)
                    wait_stage(pe, q["a_kw"], t)
                    for h in range(CH):
                        for c in range(2):
                            op = nc.tensor.matmul(B[0][:, h * P:(h + 1) * P], kT[:, 2 * h + c, :], qT[:, 2 * h + c, :], start=c == 0, stop=c == 1)
                    op.then_inc(q["p_S"], 1)
                    if not last:
                        turn(t + 1)
                    wait_stage(pe, q["a_v"], t)
                    wait_stage(pe, q["d_skip"], t)
                    wait_stage(pe, q["d_c"], t, back=1, per_tile=8)
                    for h in range(CH):
                        if h == 3 and not last:
                            wait_stage(pe, q["a_xT"], t + 1)
                        for c in range(2):
                            op = nc.tensor.matmul(B[INTER[h]][:, 0:A1], qT[:, 2 * h + c, :], state[:, h, c, :], start=c == 0, stop=c == 1)
                        op.then_inc(q["p_inter"], 1)
                    wait_stage(pe, q["d_sm"], t)
                    wait_stage(pe, q["d_dd"], t)
                    for h in range(CH):
                        nc.tensor.matmul(B[INTRA[h]][:, 0:A1], smT[:, h, :], va[:, h, :], start=True, stop=True).then_inc(q["p_intra"], 1)
                    for n in range(8):
                        h, c = n // 2, n % 2
                        if n < 4:
                            wait_stage(pe, q["a_inter"], t, per_tile=4, nth=n + 1)
                        else:
                            wait_stage(pe, q["d_num"], t, per_tile=4, nth=n - 3)
                        nc.tensor.matmul(B[UPD[n]][:, 0:A1], kw[:, h * CD + c * P:h * CD + (c + 1) * P], va[:, h, :], start=True, stop=True).then_inc(q["p_c"], 1)
                tiles(pe, body)

        with ExitStack() as st2:
            s2 = Scope(nc, st2, "md")
            xs, xc, sz, tho, acc, qs, ks, vs = (s2.sb(n, [NB, D]) for n in ("xs", "xc", "sz", "tho", "acc", "qs", "ks", "vs"))
            buf = s2.sb("buf", [NB, 3, D])
            tap = s2.sb("tap", [NB, 4, D])
            xT, cT, xcT = (s2.sb(n, [P, KC, NB]) for n in ("xT", "cT", "xcT"))
            qTm = s2.sb("qTm", [P, KC, NB, NB])
            eye = s2.sb("eye", [P, NB, NB])
            C = [s2.sb(f"C{i}", [P, 2, CD]) for i in range(3)]
            ad = s2.sb("ad", [NB, NB, CH])
            a_bc = s2.sb("a_bc", [P, NB * CH])
            ssq, msq, rstd = (s2.sb(n, [NB, 1]) for n in ("ssq", "msq", "rstd"))
            g8 = s2.sb("g8", [NB, 8])
            e4, lf, m4, pr, mt, qk, qn, smw, den, dinv, var4, rs4 = (s2.sb(n, [NB, CH]) for n in (
                "e4", "lf", "m4", "pr", "mt", "qk", "qn", "smw", "den", "dinv", "var4", "rs4"))
            dd = s2.sb("dd", [NB, 12])
            st6, mv = s2.sb("st6", [NB, CH, 6]), s2.sb("mv", [NB, CH, 2])
            load, nload, stored, eyed, end = (s2.sem(n) for n in ("load", "nload", "stored", "eyed", "end"))
            c_in = [s2.sem(f"c_in{i}") for i in range(3)]
            c_out = [s2.sem(f"c_out{i}") for i in range(3)]
            masked, crossed, updated = s2.sem("masked"), s2.sem("crossed"), s2.sem("updated")
            step = Chain(s2.sem("step"), (
                "square msq rstd xn turn xT project gates sz g8 abs exp ln lf prior mt dd edd "
                "taps add0 add1 add2 add3 cth cs turn_c cT qkv qkv_out qk1 qk2 qn2 smw aqn den absd dmax dinv "
                "wk an nn turn_q qTm ad spread a_bc loop n1 n2 n3 hc st mv var rs hn A B skip E y").split())
            n = xs
            kw, tmp, th = tap[:, 1, :], tap[:, 2, :], tap[:, 3, :]
            km = [tap[:, 0, :], tap[:, 3, :]]
            h4 = lambda ap: ap.rearrange("p (h v) -> p h v", h=CH)
            wide = lambda ap: ap.unsqueeze(2).to_broadcast([NB, CH, CD])
            block = st2.enter_context(nc.Block())
            PAIRS = [(b, h) for b in range(NB) for h in range(CH)]

            @block.sync
            def _(sp):
                sp.dma_start(xs[:], io["h1_sample"]).then_inc(load, 16)
                sp.dma_start(buf[:], io["state_conv"]).then_inc(load, 16)
                sp.dma_start(m4[:], io["state_m"]).then_inc(load, 16)
                sp.dma_start(acc[:], io["conv_b"].partition_broadcast(NB)).then_inc(load, 16)
                for j in range(4):
                    sp.dma_start(tap[:, j, :], io["conv_w"][j, :].partition_broadcast(NB)).then_inc(load, 16)
                state = io["state_c"].rearrange("(n c p) v -> n p c v", c=2, p=P)
                new = io["c_sample"].rearrange("(n c p) v -> n p c v", c=2, p=P)
                for i in range(3):
                    sp.dma_start(C[i][:], state[i]).then_inc(c_in[i], 16)
                sp.wait_ge(step.sem, step.names.index("turn") + 1)
                sp.dma_start(n[:], io["state_n"]).then_inc(nload, 16)
                sp.wait_ge(step.sem, step.names.index("mt") + 1)
                sp.dma_start(io["m_sample"], mt[:]).then_inc(stored, 16)
                sp.wait_ge(step.sem, step.names.index("gates") + 1)
                sp.dma_start(io["conv_sample"][:, 0:2, :], buf[:, 1:3, :]).then_inc(stored, 16)
                sp.dma_start(io["conv_sample"][:, 2, :], xc[:]).then_inc(stored, 16)
                sp.wait_ge(step.sem, step.names.index("nn") + 1)
                sp.dma_start(io["n_sample"], n[:]).then_inc(stored, 16)
                for i in range(len(PAIRS)):
                    sp.wait_ge(updated, i + 1)
                    sp.dma_start(new[i], C[i % 3][:]).then_inc(c_out[i % 3], 16)
                    if i + 3 < len(PAIRS):
                        sp.wait_ge(c_out[i % 3], 16 * (i // 3 + 1))
                        sp.dma_start(C[i % 3][:], state[i + 3]).then_inc(c_in[i % 3], 16)
                for i in range(3):
                    sp.wait_ge(c_out[i], 16 * len(PAIRS[i::3]))
                sp.wait_ge(step.sem, len(step.names))
                sp.dma_start(io["y2_sample"], sz[:]).then_inc(stored, 16)
                sp.wait_ge(stored, 16 * 5)

            @block.gpsimd
            def _(pool):
                nc.gpsimd.memset(eye[:], 0.0).then_inc(eyed, 1)
                pool.wait_ge(eyed, 1)
                nc.gpsimd.affine_select(out=eye[:], in_=eye[:], compare_op=ALU.not_equal, fill=1.0, base=0,
                                        pattern=[[1, NB], [-1, NB]], channel_multiplier=0).then_inc(eyed, 1)
                step.wait(pool, "rstd")
                nc.gpsimd.tensor_tensor(rstd[:], msq[:], keep["minus_half"][0:NB, :], ALU.pow).then_inc(step.sem, 1)
                step.wait(pool, "rs")
                nc.gpsimd.tensor_tensor(rs4[:], var4[:], keep["minus_half"][0:NB, :].to_broadcast([NB, CH]), ALU.pow).then_inc(step.sem, 1)

            @block.scalar
            def _(act):
                act.wait_ge(load, 16 * 8)
                nc.scalar.activation(qs[:], xs[:], ACT.Square, accum_out=ssq[:]).then_inc(step.sem, 1)
                step.wait(act, "xT")
                nc.scalar.activation(xT[:], B[0][:, 0:KC * NB].rearrange("p (k b) -> p k b", b=NB), ACT.Copy).then_inc(step.sem, 1)
                step.wait(act, "gates")
                for m in range(2):
                    nc.scalar.activation(xc[:, 512 * m:512 * m + 512], B[1 + m][0:NB, :], ACT.Copy)
                    nc.scalar.activation(sz[:, 512 * m:512 * m + 512], B[3 + m][0:NB, :], ACT.Tanh, scale=0.5)
                    op = nc.scalar.activation(tho[:, 512 * m:512 * m + 512], B[5 + m][0:NB, :], ACT.Tanh, scale=0.5)
                op.then_inc(step.sem, 1)
                step.wait(act, "abs")
                nc.scalar.activation(e4[:], g8[:, CH:2 * CH], ACT.Abs).then_inc(step.sem, 1)
                step.wait(act, "exp")
                nc.scalar.activation(e4[:], e4[:], ACT.Exp, scale=-1.0).then_inc(step.sem, 1)
                step.wait(act, "ln")
                nc.scalar.activation(e4[:], e4[:], ACT.Ln, bias=1.0).then_inc(step.sem, 1)
                step.wait(act, "edd")
                nc.scalar.activation(dd[:], dd[:], ACT.Exp).then_inc(step.sem, 1)
                step.wait(act, "cth")
                nc.scalar.activation(th, acc[:], ACT.Tanh, scale=0.5).then_inc(step.sem, 1)
                step.wait(act, "cT")
                nc.scalar.activation(cT[:], B[0][:, 0:KC * NB].rearrange("p (k b) -> p k b", b=NB), ACT.Copy, scale=0.5)
                nc.scalar.activation(xcT[:], B[0][:, KC * NB:2 * KC * NB].rearrange("p (k b) -> p k b", b=NB), ACT.Copy).then_inc(step.sem, 1)
                step.wait(act, "qkv_out")
                for m in range(2):
                    nc.scalar.activation(qs[:, 512 * m:512 * m + 512], B[1 + m][0:NB, :], ACT.Copy, scale=CD ** -0.5)
                    nc.scalar.activation(ks[:, 512 * m:512 * m + 512], B[3 + m][0:NB, :], ACT.Copy)
                    op = nc.scalar.activation(vs[:, 512 * m:512 * m + 512], B[5 + m][0:NB, :], ACT.Copy)
                op.then_inc(step.sem, 1)

            @block.vector
            def _(dve):
                V = nc.vector

                def do(name, make):
                    step.wait(dve, name)
                    make().then_inc(step.sem, 1)
                do("msq", lambda: V.tensor_scalar(msq[:], ssq[:], 1.0 / D, EPS, ALU.mult, ALU.add))
                do("xn", lambda: V.scalar_tensor_tensor(xs[:], xs[:], rstd[:], g_row[0:NB, :], ALU.mult, ALU.mult))
                step.wait(dve, "sz")
                for m in range(2):
                    op = V.scalar_tensor_tensor(sz[:, 512 * m:512 * m + 512], sz[:, 512 * m:512 * m + 512], 1.0, B[3 + m][0:NB, :], ALU.add, ALU.mult)
                op.then_inc(step.sem, 1)
                do("g8", lambda: V.tensor_tensor(g8[:], B[7][0:NB, 0:8], b_if[0:NB, :], ALU.add))
                do("lf", lambda: V.scalar_tensor_tensor(lf[:], g8[:, CH:2 * CH], 0.0, e4[:], ALU.min, ALU.subtract))
                do("prior", lambda: V.tensor_tensor(pr[:], lf[:], m4[:], ALU.add))
                do("mt", lambda: V.tensor_tensor(mt[:], pr[:], g8[:, 0:CH], ALU.max))
                step.wait(dve, "dd")
                V.tensor_tensor(dd[:, 0:4], g8[:, 0:CH], mt[:], ALU.subtract)
                V.tensor_tensor(dd[:, 4:8], pr[:], mt[:], ALU.subtract)
                V.tensor_scalar(dd[:, 8:12], mt[:], -1.0, None, ALU.mult).then_inc(step.sem, 1)
                step.wait(dve, "taps")
                for j in range(3):
                    V.tensor_tensor(tap[:, j, :], tap[:, j, :], buf[:, j, :], ALU.mult)
                V.tensor_tensor(tap[:, 3, :], tap[:, 3, :], xc[:], ALU.mult).then_inc(step.sem, 1)
                for j in range(4):
                    do(f"add{j}", lambda: V.tensor_tensor(acc[:], acc[:], tap[:, j, :], ALU.add))
                do("cs", lambda: V.scalar_tensor_tensor(acc[:], th, 1.0, acc[:], ALU.add, ALU.mult))
                step.wait(dve, "qk1")
                dve.wait_ge(nload, 16)
                V.tensor_tensor(tmp, qs[:], ks[:], ALU.mult)
                V.tensor_tensor(th, qs[:], n[:], ALU.mult).then_inc(step.sem, 1)
                do("qk2", lambda: V.tensor_reduce(qk[:], h4(tmp), AX.X, ALU.add))
                do("qn2", lambda: V.tensor_reduce(qn[:], h4(th), AX.X, ALU.add))
                do("smw", lambda: V.tensor_tensor(smw[:], qk[:], dd[:, 0:4], ALU.mult))
                do("aqn", lambda: V.tensor_tensor(qn[:], qn[:], dd[:, 4:8], ALU.mult))
                do("den", lambda: V.tensor_tensor(den[:], smw[:], qn[:], ALU.add))
                do("absd", lambda: V.scalar_tensor_tensor(den[:], den[:], -1.0, den[:], ALU.mult, ALU.max))
                do("dmax", lambda: V.tensor_tensor(den[:], den[:], dd[:, 8:12], ALU.max))
                do("dinv", lambda: V.reciprocal(dinv[:], den[:]))
                do("wk", lambda: V.tensor_tensor(h4(kw), h4(ks[:]), wide(dd[:, 0:4]), ALU.mult))
                do("an", lambda: V.tensor_tensor(h4(n[:]), h4(n[:]), wide(dd[:, 4:8]), ALU.mult))
                do("nn", lambda: V.tensor_tensor(n[:], n[:], kw, ALU.add))
                dve.wait_ge(eyed, 2)
                step.wait(dve, "qTm")
                for k in range(KC):
                    op = V.tensor_tensor(qTm[:, k, :, :], B[0][:, k * NB:(k + 1) * NB].unsqueeze(2).to_broadcast([P, NB, NB]), eye[:], ALU.mult)
                op.then_inc(step.sem, 1)
                do("ad", lambda: V.tensor_tensor(ad[:], dd[:, 4:8].unsqueeze(1).to_broadcast([NB, NB, CH]),
                                                 keep["ident"][0:NB, 0:NB].unsqueeze(2).to_broadcast([NB, NB, CH]), ALU.mult))
                do("a_bc", lambda: V.tensor_copy(a_bc[:], B[7][:, 0:NB * CH]))
                for i, (b, h) in enumerate(PAIRS):
                    if h == 0:
                        if b == 0:
                            step.wait(dve, "loop")
                        if b >= 2:
                            dve.wait_ge(crossed, CH * (b - 1))
                        V.tensor_scalar(km[b % 2], kw, keep["ident"][0:NB, b:b + 1], None, ALU.mult).then_inc(masked, 1)
                    dve.wait_ge(crossed, i + 1)
                    op = V.scalar_tensor_tensor(C[i % 3][:].rearrange("p c v -> p (c v)"), C[i % 3][:].rearrange("p c v -> p (c v)"),
                                                a_bc[:, i:i + 1], B[5 + i % 2][:], ALU.mult, ALU.add)
                    op.then_inc(updated, 1)
                dve.wait_ge(updated, len(PAIRS))
                dve.sem_inc(step.sem, 1)
                step.wait(dve, "n1")
                for h in range(CH):
                    op = V.tensor_scalar(qs[:, h * CD:(h + 1) * CD], B[1 + h][0:NB, 0:CD], dd[:, 4 + h:5 + h], None, ALU.mult)
                op.then_inc(step.sem, 1)
                do("n2", lambda: V.tensor_tensor(h4(vs[:]), h4(vs[:]), wide(smw[:]), ALU.mult))
                do("n3", lambda: V.tensor_tensor(qs[:], qs[:], vs[:], ALU.add))
                do("hc", lambda: V.tensor_tensor(h4(qs[:]), h4(qs[:]), wide(dinv[:]), ALU.mult))
                step.wait(dve, "st")
                for h in range(CH):
                    op = V.bn_stats(st6[:, h, :], qs[:, h * CD:(h + 1) * CD])
                op.then_inc(step.sem, 1)
                step.wait(dve, "mv")
                for h in range(CH):
                    op = V.bn_aggr(mv[:, h, :], st6[:, h, :])
                op.then_inc(step.sem, 1)
                do("var", lambda: V.tensor_scalar(var4[:], mv[:, :, 1], 1.0, EPS, ALU.mult, ALU.add))
                step.wait(dve, "hn")
                for h in range(CH):
                    op = V.tensor_scalar(qs[:, h * CD:(h + 1) * CD], qs[:, h * CD:(h + 1) * CD], mv[:, h, 0:1], rs4[:, h:h + 1], ALU.subtract, ALU.mult)
                op.then_inc(step.sem, 1)
                do("A", lambda: V.scalar_tensor_tensor(qs[:], tho[:], 1.0, qs[:], ALU.add, ALU.mult))
                do("B", lambda: V.tensor_tensor(qs[:], qs[:], ngh[0:NB, :], ALU.mult))
                do("skip", lambda: V.tensor_tensor(acc[:], acc[:], skiph[0:NB, :], ALU.mult))
                do("E", lambda: V.tensor_tensor(qs[:], qs[:], acc[:], ALU.add))
                do("y", lambda: V.scalar_tensor_tensor(sz[:], qs[:], 0.5, sz[:], ALU.mult, ALU.mult))

            @block.tensor
            def _(pe):
                ident8 = keep["ident"][0:NB, 0:NB]
                step.wait(pe, "turn")
                for k in range(KC):
                    op = nc.tensor.transpose(B[0][:, k * NB:(k + 1) * NB], xs[:, k * P:(k + 1) * P], ident8)
                op.then_inc(step.sem, 1)
                step.wait(pe, "project")
                for j in range(6):
                    for k in range(KC):
                        nc.tensor.matmul(B[1 + j][0:NB, :], xT[:, k, :], w[:, k, 512 * j:512 * j + 512], start=k == 0, stop=k == KC - 1)
                for k in range(KC):
                    op = nc.tensor.matmul(B[7][0:NB, 0:8], xT[:, k, :], w[:, k, GATES:GATES + 8], start=k == 0, stop=k == KC - 1)
                op.then_inc(step.sem, 1)
                step.wait(pe, "turn_c")
                for j, src in enumerate((acc, xc)):
                    for k in range(KC):
                        op = nc.tensor.transpose(B[0][:, (j * KC + k) * NB:(j * KC + k + 1) * NB], src[:, k * P:(k + 1) * P], ident8)
                op.then_inc(step.sem, 1)
                step.wait(pe, "qkv")
                for j, (src, wt_) in enumerate(((cT, wq), (cT, wk), (xcT, wv))):
                    for h in range(CH):
                        for c in range(2):
                            op = nc.tensor.matmul(B[1 + 2 * j + h // 2][0:NB, (h % 2) * CD:(h % 2 + 1) * CD], src[:, 2 * h + c, :], wt_[:, h, c, :],
                                                  start=c == 0, stop=c == 1)
                op.then_inc(step.sem, 1)
                step.wait(pe, "turn_q")
                for k in range(KC):
                    op = nc.tensor.transpose(B[0][:, k * NB:(k + 1) * NB], qs[:, k * P:(k + 1) * P], ident8)
                op.then_inc(step.sem, 1)
                step.wait(pe, "spread")
                nc.tensor.matmul(B[7][:, 0:NB * CH], keep["ones"][0:NB, :], ad[:].rearrange("p b h -> p (b h)"), start=True, stop=True).then_inc(step.sem, 1)
                for i, (b, h) in enumerate(PAIRS):
                    pe.wait_ge(c_in[i % 3], 16 * (i // 3 + 1))
                    pe.wait_ge(masked, b + 1)
                    if i >= 2:
                        pe.wait_ge(updated, i - 1)
                    for c in range(2):
                        nc.tensor.matmul(B[1 + h][0:NB, 0:CD], qTm[:, 2 * h + c, b, :], C[i % 3][:, c, :], start=b == 0 and c == 0, stop=b == NB - 1 and c == 1)
                    for c in range(2):
                        op = nc.tensor.matmul(B[5 + i % 2][:, c * CD:(c + 1) * CD], km[b % 2][:, h * CD + c * P:h * CD + (c + 1) * P], vs[:, h * CD:(h + 1) * CD],
                                              start=True, stop=True)
                    op.then_inc(crossed, 1)


def finish(nc, io, keep):
    LAST = NT
    with ExitStack() as st:
        s = Scope(nc, st, "fi")
        w = s.sb("w", [P, KC, D])
        g_row = s.sb("g_row", [P, D])
        y = [s.sb(f"y{i}", [P, D]) for i in range(2)]
        h = [s.sb(f"h{i}", [P, D]) for i in range(2)]
        yT = [s.sb(f"yT{i}", [P, KC, P]) for i in range(2)]
        o = [s.sb(f"o{i}", [P, D]) for i in range(2)]
        ssq, msq, rstd = (s.sb(n, [P, 1]) for n in ("ssq", "msq", "rstd"))
        T = [s.ps(f"T{i}") for i in range(4)]
        O = [s.ps(f"O{i}") for i in range(4)]
        loads = s.sem("loads")
        ld = s.sems("y0 y1 h0 h1")
        out = s.sems("o0 o1")
        q = s.sems("turned yT projected summed ssq msq rstd normed")
        block = st.enter_context(nc.Block())

        def tiles(eng, body):
            with eng.Fori(0, NT // 2 - 1) as i:
                body(i * 2, i, 0)
                body(i * 2 + 1, i, 1)
            body(NT - 2, NT // 2 - 1, 0)
            body(NT - 1, NT // 2 - 1, 1)
            body(LAST, NT // 2, 0, n=NB)

        def begin(eng, names):
            for n in names.split():
                eng.sem_inc(q[n], LEAD)

        @block.sync
        def _(sp):
            for i in range(2):
                sp.sem_inc(out[f"o{i}"], 16 * LEAD)
                for n in "yh":
                    sp.sem_inc(ld[f"{n}{i}"], 16 * LEAD)
            for k in range(KC):
                sp.dma_start(w[:, k, :], io["odd_w_out"][k * P:(k + 1) * P, :]).then_inc(loads, 16)
            sp.dma_start(g_row[:], io["final_g"].partition_broadcast(P)).then_inc(loads, 16)

            def rows(t, r, n=P):
                wait_stage(sp, q["turned"], t, back=2)
                src_y, src_h = (io["y2_sample"], io["h1_sample"]) if n == NB else (io["y2"][bass.ds(t * P, P), :], io["h1"][bass.ds(t * P, P), :])
                sp.dma_start(y[r][0:n, :], src_y).then_inc(ld[f"y{r}"], 16)
                wait_stage(sp, q["ssq"], t, back=2)
                sp.dma_start(h[r][0:n, :], src_h).then_inc(ld[f"h{r}"], 16)
            rows(0, 0)

            def body(t, pair, r, n=P):
                if n == P:
                    rows(t + 1, 1 - r, NB if isinstance(t, int) and t + 1 == LAST else P)
                wait_stage(sp, q["normed"], t)
                dst = io["y_sample"] if n == NB else io["y_prompt"][bass.ds(t * P, P), :]
                sp.dma_start(dst, o[r][0:n, :]).then_inc(out[f"o{r}"], 16)
            tiles(sp, body)
            sp.wait_ge(out["o0"], 16 * (LEAD + NT // 2 + 1))
            sp.wait_ge(out["o1"], 16 * (LEAD + NT // 2))

        @block.gpsimd
        def _(pool):
            begin(pool, "rstd")

            def body(t, pair, r, n=P):
                wait_stage(pool, q["normed"], t, back=1)
                wait_stage(pool, q["msq"], t)
                nc.gpsimd.tensor_tensor(rstd[0:n, :], msq[0:n, :], keep["minus_half"][0:n, :], ALU.pow).then_inc(q["rstd"], 1)
            tiles(pool, body)

        @block.scalar
        def _(act):
            begin(act, "yT ssq")

            def body(t, pair, r, n=P):
                wait_stage(act, q["turned"], t)
                wait_stage(act, q["projected"], t, back=2)
                for m in range(2):
                    op = nc.scalar.activation(yT[r][:, 4 * m:4 * m + 4, 0:n], T[2 * r + m][:, 0:4 * n].rearrange("p (k n) -> p k n", k=4), ACT.Copy)
                op.then_inc(q["yT"], 1)
                wait_stage(act, q["summed"], t)
                wait_stage(act, q["msq"], t, back=1)
                nc.scalar.activation(h[r][0:n, :], o[r][0:n, :], ACT.Square, accum_out=ssq[0:n, :]).then_inc(q["ssq"], 1)
            tiles(act, body)

        @block.vector
        def _(dve):
            begin(dve, "summed msq normed")
            dve.wait_ge(loads, 16 * (KC + 1))

            def body(t, pair, r, n=P):
                wait_stage(dve, q["projected"], t)
                dve.wait_ge(ld[f"h{r}"], (pair + (LEAD + 1)) * 16)
                dve.wait_ge(out[f"o{r}"], (pair + LEAD) * 16)
                for m in range(2):
                    op = nc.vector.tensor_tensor(o[r][0:n, 512 * m:512 * m + 512], h[r][0:n, 512 * m:512 * m + 512], O[2 * r + m][0:n, :], ALU.add)
                op.then_inc(q["summed"], 1)
                wait_stage(dve, q["ssq"], t)
                wait_stage(dve, q["rstd"], t, back=1)
                nc.vector.tensor_scalar(msq[0:n, :], ssq[0:n, :], 1.0 / D, EPS, ALU.mult, ALU.add).then_inc(q["msq"], 1)
                wait_stage(dve, q["rstd"], t)
                nc.vector.scalar_tensor_tensor(o[r][0:n, :], o[r][0:n, :], rstd[0:n, :], g_row[0:n, :], ALU.mult, ALU.mult).then_inc(q["normed"], 1)
            tiles(dve, body)

        @block.tensor
        def _(pe):
            begin(pe, "turned projected")

            def turn(t, pair, r, n=P):
                pe.wait_ge(ld[f"y{r}"], (pair + (LEAD + 1)) * 16)
                wait_stage(pe, q["yT"], t, back=2)
                for k in range(KC):
                    op = nc.tensor.transpose(T[2 * r + k // 4][:, (k % 4) * n:(k % 4 + 1) * n], y[r][0:n, k * P:(k + 1) * P], keep["ident"][0:n, 0:n])
                op.then_inc(q["turned"], 1)
            turn(0, 0, 0)
            pe.wait_ge(loads, 16 * (KC + 1))

            def body(t, pair, r, n=P):
                if n == P:
                    turn(t + 1, pair + r, 1 - r, NB if isinstance(t, int) and t + 1 == LAST else P)
                wait_stage(pe, q["yT"], t)
                wait_stage(pe, q["summed"], t, back=2)
                for m in range(2):
                    for k in range(KC):
                        op = nc.tensor.matmul(O[2 * r + m][0:n, :], yT[r][:, k, 0:n], w[:, k, 512 * m:512 * m + 512], start=k == 0, stop=k == KC - 1)
                op.then_inc(q["projected"], 1)
            tiles(pe, body)


def build(nc, ins, outs):
    def scratch(name, shape):
        return nc.dram_tensor(f"scratch_{name}", shape, F32, kind="Internal").ap()

    io = {
        "x_prompt": ins["x_prompt"].rearrange("a s d -> (a s) d"),
        "x_sample": ins["x_sample"].rearrange("b a d -> (b a) d"),
        "cache_k": ins["cache_k"].rearrange("l n p h d -> (l n p) (h d)"),
        "cache_v": ins["cache_v"].rearrange("l n p h d -> (l n p) (h d)"),
        "cache_logf": ins["cache_logf"].rearrange("l n p h -> (l n) (p h)"),
        "state_c": ins["state_c"].rearrange("l b h k v -> (l b h k) v"),
        "state_n": ins["state_n"].rearrange("l b h k -> (l b) (h k)"),
        "state_m": ins["state_m"].rearrange("l b h -> (l b) h"),
        "state_conv": ins["state_conv"].rearrange("l b j c -> (l b) j c"),
        "page_table": ins["page_table"],
        "norm_g": ins["norm_g"], "final_g": ins["final_g"],
        "even_w_in": ins["even_w_in"][0], "even_b_f": ins["even_b_f"][0, :], "gmlp_ln_g": ins["gmlp_ln_g"][0, :],
        "gmlp_ln_b": ins["gmlp_ln_b"][0, :], "gmlp_w_s": ins["gmlp_w_s"][0], "gmlp_b_s": ins["gmlp_b_s"][0],
        "even_w_out": ins["even_w_out"][0], "odd_w_in": ins["odd_w_in"][0], "odd_b_i": ins["odd_b_i"][0, :],
        "odd_b_f": ins["odd_b_f"][0, :], "conv_w": ins["conv_w"][0], "conv_b": ins["conv_b"][0, :],
        "w_q": ins["mlstm_w_q"][0], "w_k": ins["mlstm_w_k"][0], "w_v": ins["mlstm_w_v"][0],
        "norm_c": ins["mlstm_norm_g"][0, :], "skip": ins["mlstm_skip"][0, :], "odd_w_out": ins["odd_w_out"][0],
        "y_prompt": outs["y_prompt"].rearrange("a s d -> (a s) d"),
        "y_sample": outs["y_sample"].rearrange("b a d -> (b a) d"),
        "k_prompt": outs["k_prompt"].rearrange("l a s h d -> (l a s) (h d)"),
        "v_prompt": outs["v_prompt"].rearrange("l a s h d -> (l a s) (h d)"),
        "logf_prompt": outs["logf_prompt"].rearrange("l a s h -> (l a s) h"),
        "k_sample": outs["k_sample"].rearrange("l b a h d -> (l b a) (h d)"),
        "v_sample": outs["v_sample"].rearrange("l b a h d -> (l b a) (h d)"),
        "logf_sample": outs["logf_sample"].rearrange("l b a h -> (l b a) h"),
        "chunk_v": outs["chunk_v_sample"].rearrange("l b a c -> (l b a) c"),
        "c_prompt": outs["c_prompt"].rearrange("l a h k v -> (l a h k) v"),
        "n_prompt": outs["n_prompt"].rearrange("l a h k -> (l a) (h k)"),
        "m_prompt": outs["m_prompt"].rearrange("l a h -> (l a) h"),
        "conv_prompt": outs["conv_prompt"].rearrange("l a j c -> (l a j) c"),
        "c_sample": outs["c_sample"].rearrange("l b h k v -> (l b h k) v"),
        "n_sample": outs["n_sample"].rearrange("l b h k -> (l b) (h k)"),
        "m_sample": outs["m_sample"].rearrange("l b h -> (l b) h"),
        "conv_sample": outs["conv_sample"].rearrange("l b j c -> (l b) j c"),
        "q_sample": scratch("q_sample", (NB, AW)), "q_prompt": scratch("q_prompt", (SEQ, AW)),
        "mix_scratch": scratch("mix", (SEQ, D)), "h1": scratch("h1", (SEQ, D)), "h1_sample": scratch("h1_sample", (NB, D)),
        "y2": scratch("y2", (SEQ, D)), "y2_sample": scratch("y2_sample", (NB, D)),
        "s_mixed": scratch("s_mixed", (NB, D)), "self_row": scratch("self_row", (NB, AH)),
    }
    io["q_sample_flat"] = io["q_sample"].rearrange("b c -> (b c)")
    with ExitStack() as stack:
        g = Scope(nc, stack, "g")
        keep = {
            "ident": g.sb("ident", [P, P]), "ones": g.sb("ones", [P, P]),
            "upto": g.sb("upto", [P, P]), "after": g.sb("after", [P, P]),
            "mask_bf": g.sb("mask_bf", [P, P], BF16), "maskT_bf": g.sb("maskT_bf", [P, P], BF16),
            "ident_bf": g.sb("ident_bf", [P, P], BF16), "minus_half": g.sb("minus_half", [P, 1]),
            "half": g.sb("half", [P, 1]),
            "fg": g.sb("fg", [P, NT, AH]), "negc": g.sb("negc", [P, NT, AH]),
            "s_dec": g.sb("s_dec", [P, 64]), "s_fg": g.sb("s_fg", [NB, AH]), "s_self": g.sb("s_self", [NB, AH]),
        }
        with ExitStack() as layer0:
            keep["scores"] = Scope(nc, layer0, "g0").sb("scores", [P, NB, AH, PAGES + 1])
            even_project(nc, io, keep)
            decode_softmax(nc, io, keep)
            attend(nc, io, keep)
        mlstm(nc, io, keep)
        finish(nc, io, keep)


_INS = ['x_prompt', 'x_sample', 'cache_k', 'cache_v', 'cache_logf', 'state_c', 'state_n', 'state_m', 'state_conv', 'page_table',
        'norm_g', 'final_g', 'even_w_in', 'even_b_f', 'gmlp_ln_g', 'gmlp_ln_b', 'gmlp_w_s', 'gmlp_b_s', 'even_w_out',
        'odd_w_in', 'odd_b_i', 'odd_b_f', 'conv_w', 'conv_b', 'mlstm_w_q', 'mlstm_w_k', 'mlstm_w_v', 'mlstm_norm_g',
        'mlstm_skip', 'odd_w_out']
_OUTS = [("y_prompt", (1, 2048, 1024)), ("y_sample", (8, 1, 1024)),
         ("k_prompt", (1, 1, 2048, 8, 64)), ("v_prompt", (1, 1, 2048, 8, 64)), ("logf_prompt", (1, 1, 2048, 8)),
         ("k_sample", (1, 8, 1, 8, 64)), ("v_sample", (1, 8, 1, 8, 64)), ("logf_sample", (1, 8, 1, 8)),
         ("chunk_v_sample", (1, 8, 1, 512)),
         ("c_prompt", (1, 1, 4, 256, 256)), ("n_prompt", (1, 1, 4, 256)), ("m_prompt", (1, 1, 4)), ("conv_prompt", (1, 1, 3, 1024)),
         ("c_sample", (1, 8, 4, 256, 256)), ("n_sample", (1, 8, 4, 256)), ("m_sample", (1, 8, 4)), ("conv_sample", (1, 8, 3, 1024))]


def kernel(**inputs):
    import numpy as _np
    import concourse.bacc as _bacc
    from concourse import mybir as _mybir
    from concourse.bass_utils import run_bass_kernel_spmd as _run

    nc = _bacc.Bacc("TRN2", target_bir_lowering=False, num_devices=1)
    arrays, ins, outs = {}, {}, {}
    for name in _INS:
        a = _np.ascontiguousarray(inputs[name])
        arrays[f"in_{name}_dram"] = a
        ins[name] = nc.dram_tensor(f"in_{name}_dram", a.shape, _mybir.dt.from_np(a.dtype), kind="ExternalInput").ap()
    for name, shape in _OUTS:
        outs[name] = nc.dram_tensor(f"out_{name}_dram", shape, _mybir.dt.float32, kind="ExternalOutput").ap()
    build(nc, ins, outs)
    r = _run(nc, [arrays], core_ids=[0])
    return tuple(r.results[0][f"out_{name}_dram"] for name, _ in _OUTS)
```

```python
import concourse.bass as bass
from concourse import mybir
from contextlib import ExitStack

F32 = mybir.dt.float32
BF16 = mybir.dt.bfloat16
I32 = mybir.dt.int32
ALU = mybir.AluOpType
ACT = mybir.ActivationFunctionType
AX = mybir.AxisListType

P = 128
D = 1024
KC = D // P
SEQ = 2048
NT = SEQ // P
NB = 8
PAGES = 64
N_PHYS = 640
AH, AD = 8, 64
AW = AH * AD
BW = 512
BG = 8
CH, CD = 4, 256
CW = CH * CD
EVEN_COLS = 4 * AW + AH + 3 * BW
ODD_COLS = 3 * CW + 2 * CH
EPS = 1e-6
NEG = -1e30

COL = {"q": 0, "k": AW, "v": 2 * AW, "fg": 3 * AW, "za": 3 * AW + AH, "u": 4 * AW + AH,
       "vb": 4 * AW + AH + BW, "zb": 4 * AW + AH + 2 * BW}

LEAD = 2


def wait_stage(eng, stage, tile, back=0, per_tile=1, nth=None):
    nth = per_tile if nth is None else nth
    eng.wait_ge(stage, (tile + (LEAD - back)) * per_tile + nth)


def wait_dma(eng, stage, tile, back=0, dmas=1):
    eng.wait_ge(stage, (tile + (LEAD + 1 - back)) * (16 * dmas))


class Chain:

    def __init__(self, sem, names):
        self.sem, self.names = sem, names

    def wait(self, eng, name):
        n = self.names.index(name)
        if n:
            eng.wait_ge(self.sem, n)


class Scope:

    def __init__(self, nc, stack, tag):
        self.nc, self.stack, self.tag, self.taken = nc, stack, tag, []
        stack.callback(self.close)

    def close(self):
        if self.taken:
            self.nc.all_engine_barrier()
            self.nc.clear_and_free_semaphores(self.taken)
            self.nc.all_engine_barrier()

    def sb(self, name, shape, dt=F32):
        return self.stack.enter_context(self.nc.sbuf_tensor(f"{self.tag}_{name}", shape, dt))

    def ps(self, name, shape=(P, 512), dt=F32):
        return self.stack.enter_context(self.nc.psum_tensor(f"{self.tag}_{name}", list(shape), dt))

    def sem(self, name):
        self.taken.append(self.nc.alloc_semaphore(name=f"{self.tag}_{name}"))
        return self.taken[-1]

    def sems(self, names):
        return {n: self.sem(n) for n in names.split()}


def even_project(nc, io, keep):
    with ExitStack() as stack:
        s = Scope(nc, stack, "ep")
        w = s.sb("w", [P, KC, EVEN_COLS])
        x_in = [s.sb(f"x{i}", [P, D]) for i in range(2)]
        xT = [s.sb(f"xT{i}", [P, KC, P]) for i in range(2)]
        g_row = s.sb("g_row", [P, D])
        ln_g = s.sb("ln_g", [P, BW])
        ln_b = s.sb("ln_b", [P, BW])
        b_sT = s.sb("b_sT", [P, BG])
        mixT = s.sb("mixT", [P, BG, P])
        q_sb, k_sb, v_sb = (s.sb(n, [P, AW]) for n in ("q", "k", "v"))
        vg, ug, thb, tha = (s.sb(n, [P, BW]) for n in ("vg", "ug", "thb", "tha"))
        mixed = s.sb("mixed", [P, D])
        kpage = [s.sb(f"kpage{i}", [P, 2, AW]) for i in range(4)]
        q_bc = [s.sb(f"q_bc{i}", [P, AW]) for i in range(2)]
        b_f = s.sb("b_f", [P, AH])
        ssq = s.sb("ssq", [P, 1])
        msq = s.sb("msq", [P, 1])
        rstd = s.sb("rstd", [P, 1])
        stats = s.sb("stats", [P, 6])
        muvar = s.sb("muvar", [P, 2])
        lnr = s.sb("lnr", [P, 1])
        lnv = s.sb("lnv", [P, 1])
        w00 = s.sb("w00", [NB, BG])
        b0 = s.sb("b0", [NB, BG])
        pages = s.sb("pages", [1, NB * PAGES], I32)
        TR = [s.ps(f"TR{i}") for i in range(2)]
        PJ = [s.ps(f"PJ{i}") for i in range(4)]
        MX = s.ps("MX")
        SM = s.ps("SM")
        BANK = {"vb": PJ[0], "u": PJ[1], "zb": PJ[2], "za": PJ[3], "q": PJ[0], "k": PJ[1], "v": PJ[2]}
        SBANK = {"vb": PJ[0], "u": PJ[1], "zb": PJ[2], "za": PJ[3], "q": TR[0], "k": TR[1], "v": MX}
        w_s_in = xT[1]

        with ExitStack() as st2:
            s2 = Scope(nc, st2, "ep0")
            loads = s2.sems("x vec ws pages")
            w_in = [s2.sem(f"w{k}") for k in range(KC)]
            const = s2.sem("const")
            step = Chain(s2.sem("step"), "mask_ws turn_ws mixT square meansq rstd xn turn xT project gates "
                         "stats muvar lnvar lnrstd vn1 vn2 vn3 gza gzb mix1 mix2 mix3 mix4 fg self1 self2".split())
            stored = s2.sem("stored")
            block = st2.enter_context(nc.Block())
            xs = x_in[0][0:NB, :]

            @block.sync
            def _(sp):
                sp.dma_start(xs, io["x_sample"]).then_inc(loads["x"], 16)
                sp.dma_start(w_s_in[:], io["gmlp_w_s"].rearrange("g t s -> t g s")).then_inc(loads["ws"], 16)
                for k in range(KC):
                    sp.dma_start(w[:, k, :], io["even_w_in"][k * P:(k + 1) * P, :]).then_inc(w_in[k], 16)
                sp.dma_start(pages[:], io["page_table"].rearrange("(o b) p -> o (b p)", o=1)).then_inc(loads["pages"], 16)
                sp.wait_ge(loads["pages"], 16)
                sp.wait_ge(step.sem, step.names.index("gates") + 1)
                sp.dma_start(io["q_sample"], q_sb[0:NB, :]).then_inc(stored, 16)
                sp.dma_start(io["k_sample"], k_sb[0:NB, :]).then_inc(stored, 16)
                sp.dma_start(io["v_sample"], v_sb[0:NB, :]).then_inc(stored, 16)
                sp.wait_ge(step.sem, step.names.index("vn3") + 1)
                sp.dma_start(io["chunk_v"], vg[0:NB, :]).then_inc(stored, 16)
                sp.wait_ge(step.sem, step.names.index("mix4") + 1)
                sp.dma_start(io["s_mixed"], mixed[0:NB, :]).then_inc(stored, 16)
                sp.wait_ge(stored, 80)

            @block.gpsimd
            def _(pool):
                nc.gpsimd.memset(keep["ident"][:], 0.0).then_inc(const, 1)
                nc.gpsimd.memset(keep["ones"][:], 1.0).then_inc(const, 1)
                nc.gpsimd.memset(keep["minus_half"][:], -0.5).then_inc(const, 1)
                nc.gpsimd.memset(keep["half"][:], 0.5).then_inc(const, 1)
                nc.gpsimd.memset(keep["scores"][:, :, :, PAGES:PAGES + 1], NEG).then_inc(const, 1)
                nc.gpsimd.memset(keep["mask_bf"][:], 0.0).then_inc(const, 1)
                nc.gpsimd.memset(keep["maskT_bf"][:], 0.0).then_inc(const, 1)
                nc.gpsimd.memset(keep["ident_bf"][:], 0.0).then_inc(const, 1)
                pool.wait_ge(const, 8)
                nc.gpsimd.affine_select(out=keep["ident"][:], in_=keep["ident"][:], compare_op=ALU.not_equal,
                                        fill=1.0, base=0, pattern=[[-1, P]], channel_multiplier=1).then_inc(const, 1)
                nc.gpsimd.affine_select(out=keep["ident_bf"][:], in_=keep["ident_bf"][:], compare_op=ALU.not_equal,
                                        fill=1.0, base=0, pattern=[[-1, P]], channel_multiplier=1).then_inc(const, 1)
                nc.gpsimd.affine_select(out=keep["upto"][:], in_=keep["ones"][:], compare_op=ALU.is_ge,
                                        fill=0.0, base=0, pattern=[[1, P]], channel_multiplier=-1).then_inc(const, 1)
                nc.gpsimd.affine_select(out=keep["after"][:], in_=keep["ones"][:], compare_op=ALU.is_gt,
                                        fill=0.0, base=0, pattern=[[-1, P]], channel_multiplier=1).then_inc(const, 1)
                nc.gpsimd.affine_select(out=keep["mask_bf"][:], in_=keep["mask_bf"][:], compare_op=ALU.is_ge,
                                        fill=NEG, base=0, pattern=[[-1, P]], channel_multiplier=1).then_inc(const, 1)
                nc.gpsimd.affine_select(out=keep["maskT_bf"][:], in_=keep["maskT_bf"][:], compare_op=ALU.is_ge,
                                        fill=-NEG, base=0, pattern=[[1, P]], channel_multiplier=-1).then_inc(const, 1)
                pool.wait_ge(loads["ws"], 16)
                nc.gpsimd.affine_select(out=w_s_in[:], in_=w_s_in[:], compare_op=ALU.is_ge, fill=0.0, base=0,
                                        pattern=[[0, BG], [-1, P]], channel_multiplier=1).then_inc(step.sem, 1)
                step.wait(pool, "meansq")
                nc.gpsimd.tensor_scalar(msq[0:NB, :], ssq[0:NB, :], 1.0 / D, EPS, ALU.mult, ALU.add).then_inc(step.sem, 1)
                step.wait(pool, "rstd")
                nc.gpsimd.tensor_tensor(rstd[0:NB, :], msq[0:NB, :], keep["minus_half"][0:NB, :], ALU.pow).then_inc(step.sem, 1)
                step.wait(pool, "lnvar")
                nc.gpsimd.tensor_scalar(msq[0:NB, :], muvar[0:NB, 1:2], 1.0, EPS, ALU.mult, ALU.add).then_inc(step.sem, 1)
                step.wait(pool, "lnrstd")
                nc.gpsimd.tensor_tensor(lnr[0:NB, :], msq[0:NB, :], keep["minus_half"][0:NB, :], ALU.pow).then_inc(step.sem, 1)

            @block.scalar
            def _(act):
                act.dma_start(g_row[:], io["norm_g"][0, :].partition_broadcast(P)).then_inc(loads["vec"], 16)
                act.dma_start(ln_g[:], io["gmlp_ln_g"].partition_broadcast(P)).then_inc(loads["vec"], 16)
                act.dma_start(ln_b[:], io["gmlp_ln_b"].partition_broadcast(P)).then_inc(loads["vec"], 16)
                act.dma_start(b_f[:], io["even_b_f"].partition_broadcast(P)).then_inc(loads["vec"], 16)
                with nc.allow_non_contiguous_dma(reason="small vectors"):
                    act.dma_start(b_sT[:], io["gmlp_b_s"].rearrange("g t -> t g")).then_inc(loads["vec"], 16)
                    act.dma_start(w00[:], io["gmlp_w_s"][:, 0, 0].partition_broadcast(NB)).then_inc(loads["vec"], 16)
                    act.dma_start(b0[:], io["gmlp_b_s"][:, 0].partition_broadcast(NB)).then_inc(loads["vec"], 16)
                step.wait(act, "mixT")
                for h in range(2):
                    op = nc.scalar.activation(mixT[:, 4 * h:4 * h + 4, :], TR[h][:].rearrange("p (g t) -> p g t", g=4), ACT.Copy)
                op.then_inc(step.sem, 1)
                act.wait_ge(loads["x"], 16)
                step.wait(act, "square")
                nc.scalar.activation(xT[0][0:NB, :, :].rearrange("p a b -> p (a b)"), xs, ACT.Square, accum_out=ssq[0:NB, :]).then_inc(step.sem, 1)
                step.wait(act, "xT")
                nc.scalar.activation(xT[0][:, :, 0:NB], TR[0][:, 0:KC * NB].rearrange("p (k b) -> p k b", b=NB), ACT.Copy).then_inc(step.sem, 1)
                step.wait(act, "gates")
                nc.scalar.activation(vg[0:NB, :], SBANK["vb"][0:NB, :], ACT.Gelu)
                nc.scalar.activation(ug[0:NB, :], SBANK["u"][0:NB, :], ACT.Gelu)
                nc.scalar.activation(thb[0:NB, :], SBANK["zb"][0:NB, :], ACT.Tanh, scale=0.5)
                nc.scalar.activation(tha[0:NB, :], SBANK["za"][0:NB, :], ACT.Tanh, scale=0.5)
                nc.scalar.activation(q_sb[0:NB, :], SBANK["q"][0:NB, :], ACT.Copy, scale=AD ** -0.5)
                nc.scalar.activation(k_sb[0:NB, :], SBANK["k"][0:NB, :], ACT.Copy)
                nc.scalar.activation(v_sb[0:NB, :], SBANK["v"][0:NB, :], ACT.Copy).then_inc(step.sem, 1)

            @block.vector
            def _(dve):
                dve.wait_ge(loads["vec"], 7 * 16)
                step.wait(dve, "xn")
                nc.vector.scalar_tensor_tensor(xs, xs, rstd[0:NB, :], g_row[0:NB, :], ALU.mult, ALU.mult).then_inc(step.sem, 1)
                step.wait(dve, "stats")
                nc.vector.bn_stats(stats[0:NB, :], vg[0:NB, :]).then_inc(step.sem, 1)
                step.wait(dve, "muvar")
                nc.vector.bn_aggr(muvar[0:NB, :], stats[0:NB, :]).then_inc(step.sem, 1)
                step.wait(dve, "vn1")
                nc.vector.tensor_scalar(vg[0:NB, :], vg[0:NB, :], muvar[0:NB, 0:1], lnr[0:NB, :], ALU.subtract, ALU.mult).then_inc(step.sem, 1)
                step.wait(dve, "vn2")
                nc.vector.tensor_tensor(vg[0:NB, :], vg[0:NB, :], ln_g[0:NB, :], ALU.mult).then_inc(step.sem, 1)
                step.wait(dve, "vn3")
                nc.vector.tensor_tensor(vg[0:NB, :], vg[0:NB, :], ln_b[0:NB, :], ALU.add).then_inc(step.sem, 1)
                step.wait(dve, "gza")
                nc.vector.scalar_tensor_tensor(mixed[0:NB, 0:AW], tha[0:NB, :], 1.0, SBANK["za"][0:NB, :], ALU.add, ALU.mult).then_inc(step.sem, 1)
                step.wait(dve, "gzb")
                nc.vector.scalar_tensor_tensor(thb[0:NB, :], thb[0:NB, :], 1.0, SBANK["zb"][0:NB, :], ALU.add, ALU.mult).then_inc(step.sem, 1)
                step.wait(dve, "mix1")
                v3 = lambda ap: ap.rearrange("p (g c) -> p g c", g=BG)
                wide = lambda ap: ap[:].unsqueeze(2).to_broadcast([NB, BG, 64])
                nc.vector.tensor_tensor(v3(tha[0:NB, :]), v3(vg[0:NB, :]), wide(w00), ALU.mult).then_inc(step.sem, 1)
                step.wait(dve, "mix2")
                nc.vector.tensor_tensor(v3(tha[0:NB, :]), v3(tha[0:NB, :]), wide(b0), ALU.add).then_inc(step.sem, 1)
                step.wait(dve, "mix3")
                nc.vector.scalar_tensor_tensor(ug[0:NB, :], ug[0:NB, :], 0.5, thb[0:NB, :], ALU.mult, ALU.mult).then_inc(step.sem, 1)
                step.wait(dve, "mix4")
                nc.vector.tensor_tensor(mixed[0:NB, AW:D], ug[0:NB, :], tha[0:NB, :], ALU.mult).then_inc(step.sem, 1)
                step.wait(dve, "fg")
                nc.vector.tensor_tensor(keep["s_fg"][:], SM[0:NB, 0:AH], b_f[0:NB, :], ALU.add).then_inc(step.sem, 1)
                step.wait(dve, "self1")
                nc.vector.tensor_tensor(thb[0:NB, :], q_sb[0:NB, :], k_sb[0:NB, :], ALU.mult).then_inc(step.sem, 1)
                step.wait(dve, "self2")
                nc.vector.tensor_reduce(keep["s_self"][:], v3(thb[0:NB, :]), AX.X, ALU.add).then_inc(step.sem, 1)

            @block.tensor
            def _(pe):
                pe.wait_ge(const, 14)
                step.wait(pe, "turn_ws")
                for g in range(BG):
                    op = nc.tensor.transpose(TR[g // 4][:, (g % 4) * P:(g % 4 + 1) * P], w_s_in[:, g, :], keep["ident"][:])
                op.then_inc(step.sem, 1)
                step.wait(pe, "turn")
                for k in range(KC):
                    op = nc.tensor.transpose(TR[0][:, k * NB:(k + 1) * NB], xs[:, k * P:(k + 1) * P], keep["ident"][0:NB, 0:NB])
                op.then_inc(step.sem, 1)
                step.wait(pe, "project")
                for k in range(KC):
                    pe.wait_ge(w_in[k], 16)
                    nc.tensor.matmul(SM[0:NB, 0:AH], xT[0][:, k, 0:NB], w[:, k, COL["fg"]:COL["fg"] + AH], start=k == 0, stop=k == KC - 1)
                    for name in ("vb", "u", "zb", "za", "q", "k", "v"):
                        op = nc.tensor.matmul(SBANK[name][0:NB, :], xT[0][:, k, 0:NB], w[:, k, COL[name]:COL[name] + 512],
                                              start=k == 0, stop=k == KC - 1)
                op.then_inc(step.sem, 1)

        with ExitStack() as st2:
            s2 = Scope(nc, st2, "ep1")
            ld = s2.sems("x0 x1 qb0 qb1 kp0 kp1 kp2 kp3")
            out = {n: s2.sem(f"{n}_stored") for n in ("q", "k", "v", "mixed")}
            st = s2.sems("ssq msq rstd xn turned xT "
                         "p_vb p_u p_zb p_za p_q p_k p_v p_fg p_mix "
                         "a_vb a_u a_zb a_za a_q a_k a_v "
                         "stats muvar lnvar lnr vn1 vn vn2 gza gzb half_y bias_y mixed fg_out scored")
            pr = [s2.sem(f"prod{i}") for i in range(4)]
            fr = [s2.sem(f"free{i}") for i in range(4)]
            block = st2.enter_context(nc.Block())
            GROUPS = 16
            USES = GROUPS // 4

            def tiles(eng, body):
                with eng.Fori(0, NT // 2 - 1) as i:
                    body(i * 2, i, 0, False)
                    body(i * 2 + 1, i, 1, False)
                body(NT - 2, NT // 2 - 1, 0, False)
                body(NT - 1, NT // 2 - 1, 1, True)

            @block.sync
            def _(sp):
                for n in ("x0", "x1", "qb0", "qb1"):
                    sp.sem_inc(ld[n], 16 * LEAD)
                for n in ("kp0", "kp1", "kp2", "kp3"):
                    sp.sem_inc(ld[n], 32 * LEAD * USES)
                sp.sem_inc(out["mixed"], 16 * LEAD)
                sp.dma_start(x_in[0][:], io["x_prompt"][0:P, :]).then_inc(ld["x0"], 16)
                sp.dma_start(q_bc[0][:], io["q_sample"][0, :].partition_broadcast(P)).then_inc(ld["qb0"], 16)

                def body(t, pair, r, last):
                    n = 1 - r
                    if not last:
                        wait_stage(sp, st["turned"], t, back=1)
                        nxt = pair + r
                        sp.dma_start(x_in[n][:], io["x_prompt"][bass.ds((t + 1) * P, P), :]).then_inc(ld[f"x{n}"], 16)
                        wait_stage(sp, st["scored"], t, back=1)
                        sp.dma_start(q_bc[n][:], io["q_sample_flat"][bass.ds(nxt * AW, AW)].partition_broadcast(P)).then_inc(ld[f"qb{n}"], 16)
                    for g in range(GROUPS):
                        wait_stage(sp, fr[g % 4], t, per_tile=USES, nth=g // 4)
                        for j in range(2):
                            page = sp.value_load(pages[0:1, bass.ds(t * 32 + (2 * g + j), 1)], min_val=0, max_val=N_PHYS - 1)
                            sp.dma_start(kpage[g % 4][:, j, :], io["cache_k"][bass.ds(page * P, P), :]).then_inc(ld[f"kp{g % 4}"], 16)
                    wait_stage(sp, st["mixed"], t)
                    sp.dma_start(io["mix_scratch"][bass.ds(t * P, P), :], mixed[:]).then_inc(out["mixed"], 16)
                tiles(sp, body)
                wait_dma(sp, out["mixed"], NT - 1)

            @block.gpsimd
            def _(pool):
                for n in ("rstd", "lnr"):
                    pool.sem_inc(st[n], LEAD)

                def norm(t):
                    wait_stage(pool, st["xn"], t, back=1)
                    wait_stage(pool, st["msq"], t)
                    nc.gpsimd.tensor_tensor(rstd[:], msq[:], keep["minus_half"][:], ALU.pow).then_inc(st["rstd"], 1)
                norm(0)

                def body(t, pair, r, last):
                    if not last:
                        norm(t + 1)
                    wait_stage(pool, st["lnvar"], t)
                    wait_stage(pool, st["vn1"], t, back=1)
                    nc.gpsimd.tensor_tensor(lnr[:], lnv[:], keep["minus_half"][:], ALU.pow).then_inc(st["lnr"], 1)
                tiles(pool, body)

            @block.scalar
            def _(act):
                for n in ("ssq", "xT", "a_vb", "a_u", "a_zb", "a_za", "a_q", "a_k", "a_v"):
                    act.sem_inc(st[n], LEAD)
                for n in ("q", "k", "v"):
                    act.sem_inc(out[n], 16 * LEAD)

                def square(t, slot, nth):
                    act.wait_ge(ld[f"x{slot}"], nth)
                    nc.scalar.activation(xT[slot][:].rearrange("p k n -> p (k n)"), x_in[slot][:],
                                         ACT.Square, accum_out=ssq[:]).then_inc(st["ssq"], 1)

                def turn_out(t, slot):
                    wait_stage(act, st["turned"], t)
                    wait_stage(act, st["p_v"], t, back=2)
                    for h in range(2):
                        op = nc.scalar.activation(xT[slot][:, 4 * h:4 * h + 4, :], TR[h][:].rearrange("p (g t) -> p g t", g=4), ACT.Copy)
                    op.then_inc(st["xT"], 1)
                square(0, 0, 16 * (LEAD + 1))
                turn_out(0, 0)

                def body(t, pair, r, last):
                    if not last:
                        wait_stage(act, st["p_v"], t, back=1)
                        wait_stage(act, st["msq"], t)
                        square(t + 1, 1 - r, (pair + (r + LEAD + 1)) * 16)
                    wait_stage(act, st["p_vb"], t)
                    wait_stage(act, st["p_mix"], t, back=1)
                    nc.scalar.activation(vg[:], BANK["vb"][:], ACT.Gelu).then_inc(st["a_vb"], 1)
                    wait_stage(act, st["p_u"], t)
                    wait_stage(act, st["mixed"], t, back=1)
                    nc.scalar.activation(ug[:], BANK["u"][:], ACT.Gelu).then_inc(st["a_u"], 1)
                    wait_stage(act, st["p_zb"], t)
                    nc.scalar.activation(thb[:], BANK["zb"][:], ACT.Tanh, scale=0.5).then_inc(st["a_zb"], 1)
                    wait_stage(act, st["p_za"], t)
                    wait_stage(act, st["gza"], t, back=1)
                    nc.scalar.activation(tha[:], BANK["za"][:], ACT.Tanh, scale=0.5).then_inc(st["a_za"], 1)
                    for n, buf, scale in (("q", q_sb, AD ** -0.5), ("k", k_sb, 1.0), ("v", v_sb, 1.0)):
                        wait_stage(act, st[f"p_{n}"], t)
                        wait_dma(act, out[n], t, back=1)
                        nc.scalar.activation(buf[:], BANK[n][:], ACT.Copy, scale=scale).then_inc(st[f"a_{n}"], 1)
                        wait_stage(act, st[f"a_{n}"], t)
                        act.dma_start(io[f"{n}_prompt"][bass.ds(t * P, P), :], buf[:]).then_inc(out[n], 16)
                    if not last:
                        turn_out(t + 1, 1 - r)
                tiles(act, body)
                for n in ("q", "k", "v"):
                    wait_dma(act, out[n], NT - 1)

            @block.vector
            def _(dve):
                for n in ("msq", "lnvar", "xn", "stats", "muvar", "vn1", "vn", "vn2", "gza", "gzb", "half_y", "bias_y", "mixed", "fg_out", "scored"):
                    dve.sem_inc(st[n], LEAD)
                for i in range(4):
                    dve.sem_inc(pr[i], LEAD * USES)
                    dve.sem_inc(fr[i], LEAD * USES)

                def mean_square(t):
                    wait_stage(dve, st["ssq"], t)
                    wait_stage(dve, st["rstd"], t, back=1)
                    return nc.vector.tensor_scalar(msq[:], ssq[:], 1.0 / D, EPS, ALU.mult, ALU.add).then_inc(st["msq"], 1)

                def normed(t, slot):
                    wait_stage(dve, st["rstd"], t)
                    nc.vector.scalar_tensor_tensor(x_in[slot][:], x_in[slot][:], rstd[:], g_row[:], ALU.mult, ALU.mult).then_inc(st["xn"], 1)
                mean_square(0)
                normed(0, 0)

                def body(t, pair, r, last):
                    v3 = lambda ap: ap.rearrange("p (g c) -> p g c", g=BG)

                    def score(g):
                        i = g % 4
                        if g == 0:
                            dve.wait_ge(ld[f"qb{r}"], (pair + (LEAD + 1)) * 16)
                        dve.wait_ge(ld[f"kp{i}"], (t + LEAD) * (32 * USES) + 32 * (g // 4 + 1))
                        nc.vector.tensor_tensor(kpage[i][:], kpage[i][:], q_bc[r][:].unsqueeze(1).to_broadcast([P, 2, AW]), ALU.mult).then_inc(pr[i], 1)

                    def total(g):
                        i = g % 4
                        wait_stage(dve, pr[i], t, per_tile=USES, nth=g // 4 + 1)
                        first = r * 32 + 2 * g
                        dst = keep["scores"][:, bass.ds(pair, 1), :, first:first + 2].rearrange("p a h g -> p (a g) h")
                        op = nc.vector.tensor_reduce(dst, kpage[i][:].rearrange("p j (h d) -> p j h d", h=AH), AX.X, ALU.add)
                        op.then_inc(fr[i], 1)

                    def tile_ops():
                        if not last:
                            yield mean_square(t + 1)
                        yield
                        yield
                        if not last:
                            yield normed(t + 1, 1 - r)
                        wait_stage(dve, st["p_fg"], t)
                        yield nc.vector.tensor_tensor(keep["fg"][:, bass.ds(t, 1), :].rearrange("p a h -> p (a h)"), SM[:, 0:AH], b_f[:], ALU.add).then_inc(st["fg_out"], 1)
                        wait_stage(dve, st["a_vb"], t)
                        wait_stage(dve, st["lnr"], t, back=1)
                        yield nc.vector.bn_stats(stats[:], vg[:]).then_inc(st["stats"], 1)
                        wait_stage(dve, st["stats"], t)
                        wait_stage(dve, st["lnr"], t, back=1)
                        yield
                        yield nc.vector.bn_aggr(muvar[:], stats[:]).then_inc(st["muvar"], 1)
                        wait_stage(dve, st["muvar"], t)
                        yield nc.vector.tensor_scalar(lnv[:], muvar[:, 1:2], 1.0, EPS, ALU.mult, ALU.add).then_inc(st["lnvar"], 1)
                        wait_stage(dve, st["a_zb"], t)
                        yield nc.vector.scalar_tensor_tensor(thb[:], thb[:], 1.0, BANK["zb"][:], ALU.add, ALU.mult).then_inc(st["gzb"], 1)
                        wait_stage(dve, st["lnr"], t)
                        yield nc.vector.tensor_scalar(vg[:], vg[:], muvar[:, 0:1], lnr[:], ALU.subtract, ALU.mult).then_inc(st["vn1"], 1)
                        wait_stage(dve, st["vn1"], t)
                        yield nc.vector.tensor_tensor(vg[:], vg[:], ln_g[:], ALU.mult).then_inc(st["vn"], 1)
                        wait_stage(dve, st["vn"], t)
                        yield nc.vector.tensor_tensor(vg[:], vg[:], ln_b[:], ALU.add).then_inc(st["vn2"], 1)
                        wait_stage(dve, st["a_za"], t)
                        wait_dma(dve, out["mixed"], t, back=1)
                        yield nc.vector.scalar_tensor_tensor(mixed[:, 0:AW], tha[:], 1.0, BANK["za"][:], ALU.add, ALU.mult).then_inc(st["gza"], 1)
                        wait_stage(dve, st["a_u"], t)
                        wait_stage(dve, st["gzb"], t)
                        yield nc.vector.scalar_tensor_tensor(ug[:], ug[:], 0.5, thb[:], ALU.mult, ALU.mult).then_inc(st["half_y"], 1)
                        wait_stage(dve, st["p_mix"], t)
                        wait_stage(dve, st["half_y"], t)
                        yield nc.vector.tensor_tensor(v3(thb[:]), v3(MX[:]), b_sT[:].unsqueeze(2).to_broadcast([P, BG, 64]), ALU.add).then_inc(st["bias_y"], 1)
                        wait_stage(dve, st["bias_y"], t)
                        yield nc.vector.tensor_tensor(mixed[:, AW:D], ug[:], thb[:], ALU.mult).then_inc(st["mixed"], 1)

                    ops = tile_ops()
                    for g in range(GROUPS):
                        score(g)
                        next(ops, None)
                        total(g)
                    for _ in ops:
                        pass
                    dve.wait_ge(fr[3], (t + (LEAD + 1)) * USES)
                    dve.sem_inc(st["scored"], 1)
                tiles(dve, body)

            @block.tensor
            def _(pe):
                for n in ("turned", "p_vb", "p_u", "p_zb", "p_za", "p_q", "p_k", "p_v", "p_fg", "p_mix"):
                    pe.sem_inc(st[n], LEAD)

                def turn(t, slot):
                    wait_stage(pe, st["xn"], t)
                    wait_stage(pe, st["xT"], t, back=1)
                    for k in range(KC):
                        op = nc.tensor.transpose(TR[k // 4][:, (k % 4) * P:(k % 4 + 1) * P], x_in[slot][:, k * P:(k + 1) * P], keep["ident"][:])
                    op.then_inc(st["turned"], 1)
                turn(0, 0)

                def body(t, pair, r, last):
                    def project(name, bank_users):
                        for stage, back in bank_users:
                            wait_stage(pe, st[stage], t, back=back)
                        for k in range(KC):
                            op = nc.tensor.matmul(BANK[name][:], xT[r][:, k, :], w[:, k, COL[name]:COL[name] + 512], start=k == 0, stop=k == KC - 1)
                        op.then_inc(st[f"p_{name}"], 1)
                    wait_stage(pe, st["xT"], t)
                    project("vb", [("a_q", 1)])
                    project("u", [("a_k", 1)])
                    project("zb", [("a_v", 1)])
                    wait_stage(pe, st["fg_out"], t, back=1)
                    for k in range(KC):
                        op = nc.tensor.matmul(SM[:, 0:AH], xT[r][:, k, :], w[:, k, COL["fg"]:COL["fg"] + AH], start=k == 0, stop=k == KC - 1)
                    op.then_inc(st["p_fg"], 1)
                    project("za", [("gza", 1)])
                    project("q", [("a_vb", 0)])
                    project("k", [("a_u", 0)])
                    if not last:
                        turn(t + 1, 1 - r)
                    project("v", [("gzb", 0)])
                    wait_stage(pe, st["vn2"], t)
                    wait_stage(pe, st["bias_y"], t, back=1)
                    for g in range(BG):
                        op = nc.tensor.matmul(MX[:, g * 64:(g + 1) * 64], mixT[:, g, :], vg[:, g * 64:(g + 1) * 64], start=True, stop=True)
                    op.then_inc(st["p_mix"], 1)
                tiles(pe, body)


def decode_softmax(nc, io, keep):
    HG = AH * PAGES
    with ExitStack() as st:
        s = Scope(nc, st, "dm")
        rows = s.sb("rows", [P, 4, D])
        lf = s.sb("lf", [P, NB, HG])
        later = s.sb("later", [P, NB, HG])
        run = s.sb("run", [P, NB * HG])
        run_t = s.sb("run_t", [P, AH * NT])
        idx = s.sb("idx", [P, 4], I32)
        pz, sz = s.sb("pz", [P, NT * AH]), s.sb("sz", [NB, AH])
        plf, slf = s.sb("plf", [P, NT, AH]), s.sb("slf", [NB, AH])
        plf_h = s.sb("plf_h", [P, AH, NT])
        pincl = s.sb("pincl", [P, AH * NT])
        mx = s.sb("mx", [P, NB * AH])
        mx1 = s.sb("mx1", [NB * AH, 1])
        diag = s.sb("diag", [NB * AH, NB * AH])
        total = s.sb("total", [P, NB * AH])
        B = [s.ps(f"B{i}") for i in range(8)]
        loads = s.sems("idx rows")
        stored = s.sem("self_out")
        back = s.sem("self_in")
        outs = s.sem("outs")
        run_ready = s.sem("run_ready")
        step = Chain(s.sem("step"), "abs exp ln logf self turn lf "
                     "scan later prompt_h prompt_scan prompt_excl suffix bias cum negc max turn_max max1 diag spread "
                     "minus exps sums spread_sums inverse norm".split())
        scores = keep["scores"]
        flat = scores[:].rearrange("p b h g -> p (b h) g")
        block = st.enter_context(nc.Block())

        @block.sync
        def _(sp):
            with nc.allow_non_contiguous_dma(reason="512 page numbers"):
                sp.dma_start(idx[:], io["page_table"].rearrange("b g -> (b g)").rearrange("(i p) -> p i", p=P)).then_inc(loads["idx"], 16)
            for k in range(KC):
                sp.dma_start(keep["w_out"][:, k, :], io["even_w_out"][k * P:(k + 1) * P, :]).then_inc(keep["w_out_in"], 16)
            sp.wait_ge(step.sem, step.names.index("logf") + 1)
            with nc.allow_non_contiguous_dma(reason="gates are eight wide"):
                sp.dma_start(io["logf_prompt"].rearrange("(t p) h -> p t h", p=P), plf[:]).then_inc(outs, 16)
                sp.dma_start(io["logf_sample"], slf[:]).then_inc(outs, 16)
            sp.wait_ge(step.sem, step.names.index("self") + 1)
            sp.dma_start(io["self_row"], keep["s_self"][:]).then_inc(stored, 16)
            sp.wait_ge(stored, 16)
            with nc.allow_non_contiguous_dma(reason="64 scores"):
                sp.dma_start(scores[0:1, :, :, PAGES], io["self_row"].rearrange("(o b) h -> o b h", o=1)).then_inc(back, 16)
            sp.wait_ge(step.sem, len(step.names))
            with nc.allow_non_contiguous_dma(reason="64 weights"):
                sp.dma_start(io["self_row"].rearrange("(o b) h -> o b h", o=1), scores[0:1, :, :, PAGES]).then_inc(stored, 16)
            sp.wait_ge(stored, 32)
            sp.dma_start(keep["s_self"][:], io["self_row"]).then_inc(back, 16)
            sp.wait_ge(back, 32)
            sp.wait_ge(outs, 32)

        @block.gpsimd
        def _(pool):
            pool.wait_ge(loads["idx"], 16)
            for i in range(4):
                pool.indirect_dma_start(out=rows[:, i, :], out_offset=None, in_=io["cache_logf"],
                                        in_offset=bass.IndirectOffsetOnAxis(ap=idx[:, i:i + 1], axis=0)).then_inc(loads["rows"], 16)
            nc.gpsimd.memset(run[:], 1.0).then_inc(run_ready, 1)
            pool.wait_ge(run_ready, 1)
            nc.gpsimd.memset(run[:].rearrange("p (n g) -> p n g", g=PAGES)[:, :, 0:1], 0.0).then_inc(run_ready, 1)
            nc.gpsimd.memset(run_t[:], 1.0).then_inc(run_ready, 1)
            pool.wait_ge(run_ready, 3)
            nc.gpsimd.memset(run_t[:].rearrange("p (h t) -> p h t", t=NT)[:, :, 0:1], 0.0).then_inc(run_ready, 1)

        @block.scalar
        def _(act):
            nc.scalar.activation(pz[:], keep["fg"][:].rearrange("p t h -> p (t h)"), ACT.Abs)
            nc.scalar.activation(sz[:], keep["s_fg"][:], ACT.Abs).then_inc(step.sem, 1)
            step.wait(act, "exp")
            nc.scalar.activation(pz[:], pz[:], ACT.Exp, scale=-1.0)
            nc.scalar.activation(sz[:], sz[:], ACT.Exp, scale=-1.0).then_inc(step.sem, 1)
            step.wait(act, "ln")
            nc.scalar.activation(pz[:], pz[:], ACT.Ln, bias=1.0)
            nc.scalar.activation(sz[:], sz[:], ACT.Ln, bias=1.0).then_inc(step.sem, 1)
            step.wait(act, "lf")
            for i in range(4):
                for h in range(2):
                    dst = lf[:, 2 * i:2 * i + 2, 256 * h:256 * h + 256].rearrange("p b (h g) -> p h b g", h=4)
                    op = nc.scalar.activation(dst, B[2 * i + h][:].rearrange("p (h b g) -> p h b g", h=4, b=2), ACT.Copy)
            op.then_inc(step.sem, 1)
            step.wait(act, "negc")
            nc.scalar.activation(keep["negc"][:].rearrange("p t h -> p h t"), B[0][:, 0:P].rearrange("p (h t) -> p h t", t=NT), ACT.Copy, scale=-1.0).then_inc(step.sem, 1)
            step.wait(act, "exps")
            nc.scalar.activation(flat, flat, ACT.Exp).then_inc(step.sem, 1)

        @block.vector
        def _(dve):
            step.wait(dve, "logf")
            nc.vector.scalar_tensor_tensor(plf[:].rearrange("p t h -> p (t h)"), keep["fg"][:].rearrange("p t h -> p (t h)"), 0.0, pz[:], ALU.min, ALU.subtract)
            nc.vector.scalar_tensor_tensor(slf[:], keep["s_fg"][:], 0.0, sz[:], ALU.min, ALU.subtract).then_inc(step.sem, 1)
            step.wait(dve, "self")
            nc.vector.tensor_tensor(keep["s_self"][:], keep["s_self"][:], slf[:], ALU.subtract).then_inc(step.sem, 1)
            step.wait(dve, "scan")
            dve.wait_ge(run_ready, 4)
            nc.vector.tensor_tensor_scan(later[:].rearrange("p b n -> p (b n)"), run[:], lf[:].rearrange("p b n -> p (b n)"), 0.0, ALU.mult, ALU.add).then_inc(step.sem, 1)
            step.wait(dve, "later")
            l4 = later[:].rearrange("p b (h g) -> p (b h) g", g=PAGES)
            nc.vector.tensor_copy(total[:], l4[:, :, PAGES - 1:PAGES].rearrange("p n g -> p (n g)")).then_inc(step.sem, 1)
            step.wait(dve, "prompt_h")
            nc.vector.tensor_tensor(l4, total[:].unsqueeze(2).to_broadcast([P, NB * AH, PAGES]), l4, ALU.subtract)
            nc.vector.tensor_copy(plf_h[:], plf[:].rearrange("p t h -> p h t")).then_inc(step.sem, 1)
            step.wait(dve, "prompt_scan")
            nc.vector.tensor_tensor_scan(pincl[:], run_t[:], plf_h[:].rearrange("p h t -> p (h t)"), 0.0, ALU.mult, ALU.add).then_inc(step.sem, 1)
            step.wait(dve, "prompt_excl")
            nc.vector.tensor_tensor(pincl[:], pincl[:], plf_h[:].rearrange("p h t -> p (h t)"), ALU.subtract).then_inc(step.sem, 1)
            step.wait(dve, "bias")
            for b in range(NB):
                op = nc.vector.tensor_tensor(scores[:, b, :, 0:PAGES], scores[:, b, :, 0:PAGES], B[b][:].rearrange("p (h g) -> p h g", h=AH), ALU.add)
            op.then_inc(step.sem, 1)
            dve.wait_ge(back, 16)
            step.wait(dve, "max")
            nc.vector.tensor_reduce(mx[:], flat, AX.X, ALU.max).then_inc(step.sem, 1)
            step.wait(dve, "max1")
            nc.vector.tensor_reduce(mx1[:], B[1][0:NB * AH, 0:P], AX.X, ALU.max).then_inc(step.sem, 1)
            step.wait(dve, "diag")
            nc.vector.tensor_scalar(diag[:], keep["ident"][0:NB * AH, 0:NB * AH], mx1[:], None, ALU.mult).then_inc(step.sem, 1)
            step.wait(dve, "minus")
            nc.vector.tensor_tensor(flat, flat, B[2][:, 0:NB * AH].unsqueeze(2).to_broadcast([P, NB * AH, PAGES + 1]), ALU.subtract).then_inc(step.sem, 1)
            step.wait(dve, "sums")
            nc.vector.tensor_reduce(mx[:], flat, AX.X, ALU.add).then_inc(step.sem, 1)
            step.wait(dve, "inverse")
            nc.vector.reciprocal(total[:], B[3][:, 0:NB * AH]).then_inc(step.sem, 1)
            step.wait(dve, "norm")
            nc.vector.tensor_tensor(flat, flat, total[:].unsqueeze(2).to_broadcast([P, NB * AH, PAGES + 1]), ALU.mult).then_inc(step.sem, 1)

        @block.tensor
        def _(pe):
            pe.wait_ge(loads["rows"], 64)
            step.wait(pe, "turn")
            for i in range(4):
                for h in range(AH):
                    op = nc.tensor.transpose(B[2 * i + h // 4][:, (h % 4) * P:(h % 4 + 1) * P], rows[:, i, h:D:AH], keep["ident"][:])
            op.then_inc(step.sem, 1)
            step.wait(pe, "suffix")
            for b in range(NB):
                nc.tensor.matmul(B[b][:], keep["after"][:], lf[:, b, :], start=True, stop=False)
                op = nc.tensor.matmul(B[b][:], keep["ones"][:], later[:, b, :], start=False, stop=True)
            op.then_inc(step.sem, 1)
            step.wait(pe, "cum")
            nc.tensor.matmul(B[0][:, 0:P], keep["upto"][:], plf_h[:].rearrange("p h t -> p (h t)"), start=True, stop=False)
            nc.tensor.matmul(B[0][:, 0:P], keep["ones"][:], pincl[:], start=False, stop=True).then_inc(step.sem, 1)
            step.wait(pe, "turn_max")
            nc.tensor.transpose(B[1][0:NB * AH, 0:P], mx[:], keep["ident"][:]).then_inc(step.sem, 1)
            step.wait(pe, "spread")
            nc.tensor.matmul(B[2][:, 0:NB * AH], keep["ones"][0:NB * AH, :], diag[:], start=True, stop=True).then_inc(step.sem, 1)
            step.wait(pe, "spread_sums")
            nc.tensor.matmul(B[3][:, 0:NB * AH], keep["ones"][:], mx[:], start=True, stop=True).then_inc(step.sem, 1)


def attend(nc, io, keep):
    with ExitStack() as st:
        s = Scope(nc, st, "at")
        w_out, w_in = keep["w_out"], keep["w_out_in"]
        KT = s.sb("KT", [AD + 1, AH, SEQ])
        V = s.sb("V", [P, NT, AW])
        QT = s.sb("QT", [AD + 1, AH, P])
        k_in = s.sb("k_in", [P, AH, AD + 1])
        q_in = s.sb("q_in", [P, AH, AD + 1])
        q_head = [s.sb(f"q_head{i}", [AD + 1, P]) for i in range(2)]
        prob = [s.sb(f"prob{i}", [P, SEQ]) for i in range(2)]
        probT = [s.sb(f"probT{i}", [P, 512]) for i in range(2)]
        mix = s.sb("mix", [P, D])
        x_in = s.sb("x_in", [P, D])
        yT = mix[:].rearrange("p (k n) -> p k n", n=P)
        vpage = [s.sb(f"vpage{i}", [P, 2, AW]) for i in range(4)]
        acc = s.sb("acc", [P, 2, AW])
        part = [s.sb(f"part{i}", [P, 2]) for i in range(2)]
        nmax = [s.sb(f"nmax{i}", [P, 1]) for i in range(2)]
        psum = [s.sb(f"psum{i}", [P, 2, AH]) for i in range(2)]
        pinv = s.sb("pinv", [P, AH])
        pages = s.sb("pages", [NB, PAGES], I32)
        S = s.ps("S", (P, SEQ))
        T = [s.ps(f"T{i}") for i in range(2)]
        O = s.ps("O")
        Y = s.ps("Y")

        consts, pages_in = s.sem("consts"), s.sem("pages_in")
        ld = s.sems("k q v mix x vp0 vp1 vp2 vp3")
        h_stored = s.sem("h_stored")
        q_ready = s.sem("q_ready")
        scored = s.sem("scored")
        parted = s.sem("parted")
        maxed = s.sem("maxed")
        exped = s.sem("exped")
        turned = s.sem("turned")
        evac = s.sem("evac")
        used = s.sem("used")
        weighed = s.sem("weighed")
        added = s.sem("added")
        dec_summed = s.sem("dec_summed")
        dec_out = s.sem("dec_out")
        augmented = s.sem("augmented")
        totalled, inverse, scaled, gated = (s.sem(n) for n in ("totalled", "inverse", "scaled", "gated"))
        projected = s.sem("projected")
        h_ready = s.sem("h_ready")
        C = 2

        def blocks(t):
            return -(-(t + 1) // 4)

        base, pbase = [4], [0]
        for u in range(NT):
            base.append(base[-1] + AH * blocks(u) + 6)
            pbase.append(pbase[-1] + AH * blocks(u))

        HALVED = 8
        HALF = 1024

        def halves(t):
            return 2 if t >= HALVED else 1

        sbase = [0]
        for u in range(NT):
            sbase.append(sbase[-1] + AH * halves(u))

        def before(t, h):
            if isinstance(h, int) and h < 0:
                return C if t == 0 else before(t - 1, h + AH)
            return h * halves(t) + (C + sbase[t])

        def parts(t, r):
            end = (t + 1) * P
            return [(0, HALF, 0), (HALF, end, HALF)] if t >= HALVED else [(HALF * r, HALF * r + end, 0)]

        def head_item(t, h):
            late = 4 if isinstance(h, int) and h == AH - 1 and t < NT - 1 else 0
            return h * blocks(t) + (base[t] + late)

        def kq_item(t):
            return base[t - 1] + (AH - 1) * blocks(t - 1) if t else 0

        def y_item(t):
            return base[t] + AH * blocks(t) + (4 if t < NT - 1 else 0)

        main = st.enter_context(ExitStack())
        block = main.enter_context(nc.Block())

        @block.sync
        def _(sp):
            sp.dma_start(pages[:], io["page_table"]).then_inc(pages_in, 16)

            def rows(t):
                at = slice(t * P, (t + 1) * P)
                if t:
                    sp.wait_ge(turned, C + kq_item(t - 1) + 4)
                sp.dma_start(k_in[:, :, 0:AD], io["k_prompt"][at, :].rearrange("p (h d) -> p h d", h=AH)).then_inc(ld["k"], 16)
                sp.dma_start(q_in[:, :, 0:AD], io["q_prompt"][at, :].rearrange("p (h d) -> p h d", h=AH)).then_inc(ld["q"], 16)
                sp.dma_start(V[:, t, :], io["v_prompt"][at, :]).then_inc(ld["v"], 16)
            rows(0)
            sp.wait_ge(pages_in, 16)
            for t in range(NT):
                if t + 1 < NT:
                    rows(t + 1)
                with sp.Fori(0, AH // 2) as i:
                    for r in range(2):
                        for g in range(2):
                            sp.wait_ge(added, i * 4 + (t * 16 + 2 * r + g + 1))
                            for j in range(2):
                                page = sp.value_load(pages[t // 2:t // 2 + 1, bass.ds(i * 8 + ((t % 2) * 32 + 4 * r + 2 * g + j), 1)], min_val=0, max_val=N_PHYS - 1)
                                sp.dma_start(vpage[2 * r + g][:, j, :], io["cache_v"][bass.ds(page * P, P), :]).then_inc(ld[f"vp{2 * r + g}"], 16)

        @block.gpsimd
        def _(pool):
            pool.sem_inc(q_ready, C)
            nc.gpsimd.memset(q_in[:, :, AD:AD + 1], 1.0).then_inc(consts, 1)

            def augment(t):
                if t:
                    pool.wait_ge(turned, C + kq_item(t - 1) + 4)
                nc.gpsimd.tensor_copy(k_in[:, :, AD:AD + 1], keep["negc"][:, t, :].unsqueeze(2)).then_inc(augmented, 1)

            def gates_in(t):
                pool.dma_start(mix[:], io["mix_scratch"][t * P:(t + 1) * P, :]).then_inc(ld["mix"], 16)

            def residual_in(t):
                if t:
                    pool.wait_ge(h_stored, 16 * t)
                pool.dma_start(x_in[:], io["x_prompt"][t * P:(t + 1) * P, :]).then_inc(ld["x"], 16)
            augment(0)
            gates_in(0)
            residual_in(0)

            def copy_query(t, h, r):
                pool.wait_ge(scored, before(t, h - 1))
                nc.gpsimd.tensor_copy(q_head[r][:], QT[:, bass.ds(h, 1), :].rearrange("p a n -> p (a n)")).then_inc(q_ready, 1)

            def first_queries(t):
                pool.wait_ge(evac, C + kq_item(t) + 4)
                copy_query(t, 0, 0)
                copy_query(t, 1, 1)
            first_queries(0)
            for t in range(NT):
                if t + 1 < NT:
                    augment(t + 1)
                with pool.Fori(0, AH // 2 - 1) as i:
                    copy_query(t, i * 2 + 2, 0)
                    copy_query(t, i * 2 + 3, 1)
                if t:
                    pool.wait_ge(h_ready, 2 * t)
                    pool.dma_start(io["h1"][(t - 1) * P:t * P, :], x_in[:]).then_inc(h_stored, 16)
                    gates_in(t)
                if t + 1 < NT:
                    first_queries(t + 1)
                if t:
                    residual_in(t)
            pool.wait_ge(h_ready, 2 * NT)
            pool.dma_start(io["h1"][(NT - 1) * P:NT * P, :], x_in[:]).then_inc(h_stored, 16)
            pool.wait_ge(h_stored, 16 * NT)

        @block.scalar
        def _(act):
            act.sem_inc(exped, C)
            act.sem_inc(evac, C)

            def keys_queries(t):
                n = kq_item(t)
                if t:
                    act.wait_ge(q_ready, C + t * AH)
                for m in range(4):
                    dst = (KT[:, 4 * m:4 * m + 4, t * P:(t + 1) * P] if m < 2 else QT[:, 4 * m - 8:4 * m - 4, :])
                    act.wait_ge(turned, n + m + C + 1)
                    nc.scalar.activation(dst, T[(n + m) % 2][0:AD + 1, :].rearrange("p (h n) -> p h n", h=4), ACT.Copy).then_inc(evac, 1)

            def exp(t, h, r):
                act.wait_ge(maxed, h + (C + t * AH + 1))
                act.wait_ge(inverse, C + t - 1)
                for k, (lo, hi, to) in enumerate(parts(t, r)):
                    nc.scalar.activation(prob[r][:, to:to + hi - lo], S[:, lo:hi], ACT.Exp, bias=nmax[r][:],
                                         accum_out=psum[t % 2][:, k, bass.ds(h, 1)]).then_inc(exped, 1)

            def evacuate(t, h, r):
                nb = blocks(t)
                for b in range(nb):
                    i = (r * nb + b) % 2
                    cols = min(512, (t + 1) * P - 512 * b)
                    act.wait_ge(turned, head_item(t, h) + (b + C + 1))
                    act.wait_ge(used, h * nb + (pbase[t] + b + C - 1))
                    nc.scalar.activation(probT[i][:, 0:cols], T[i][:, 0:cols], ACT.Copy).then_inc(evac, 1)

            keys_queries(0)
            exp(0, 0, 0)
            for t in range(NT):
                with act.Fori(0, AH // 2 - 1) as i:
                    evacuate(t, i * 2, 0)
                    exp(t, i * 2 + 1, 1)
                    evacuate(t, i * 2 + 1, 1)
                    exp(t, i * 2 + 2, 0)
                evacuate(t, AH - 2, 0)
                exp(t, AH - 1, 1)
                if t + 1 < NT:
                    keys_queries(t + 1)
                evacuate(t, AH - 1, 1)
                if t + 1 < NT:
                    exp(t + 1, 0, 0)
                n = y_item(t)
                for m in range(2):
                    act.wait_ge(turned, C + n + 2)
                    nc.scalar.activation(yT[:, 4 * m:4 * m + 4, :], T[m][:].rearrange("p (k n) -> p k n", k=4), ACT.Copy).then_inc(evac, 1)

        @block.vector
        def _(dve):
            dve.sem_inc(maxed, C)
            dve.sem_inc(inverse, C)
            dve.sem_inc(added, 4)

            def maximum(t, h, r):
                dve.wait_ge(exped, before(t, h - 1))
                for k, (lo, hi, _) in enumerate(parts(t, r)):
                    dve.wait_ge(scored, before(t, h) + (k + 1))
                    if t < HALVED:
                        nc.vector.tensor_reduce(nmax[r][:], S[:, lo:hi], AX.X, ALU.max, negate=True).then_inc(maxed, 1)
                    else:
                        nc.vector.tensor_reduce(part[r][:, k:k + 1], S[:, lo:hi], AX.X, ALU.max, negate=True).then_inc(parted, 1)
                if t >= HALVED:
                    dve.wait_ge(parted, h * 2 + ((t - HALVED) * 2 * AH + 2))
                    nc.vector.tensor_tensor(nmax[r][:], part[r][:, 0:1], part[r][:, 1:2], ALU.min).then_inc(maxed, 1)

            def pages_of(t, h, r, use):
                def weigh(g, out, done):
                    dve.wait_ge(ld[f"vp{2 * r + g}"], use * 32 + 32 * (4 * t + 1))
                    w = keep["scores"][:, t // 2, :, bass.ds(h * 4 + ((t % 2) * 32 + 2 * g), 2)]
                    nc.vector.tensor_tensor(out.rearrange("p j (h d) -> p j h d", h=AH), vpage[2 * r + g][:].rearrange("p j (h d) -> p j h d", h=AH),
                                            w.rearrange("p h j -> p j h").unsqueeze(3).to_broadcast([P, 2, AH, AD]), ALU.mult).then_inc(done, 1)

                first = isinstance(h, int) and h == 0 and t % 2 == 0
                if first:
                    if t:
                        dve.wait_ge(dec_summed, t // 2)
                    weigh(0, acc[:], added)
                    dve.sem_inc(weighed, 1)
                else:
                    weigh(0, vpage[2 * r][:], weighed)
                weigh(1, vpage[2 * r + 1][:], weighed)
                for g in range(1 if first else 0, 2):
                    dve.wait_ge(weighed, h * 2 + (16 * t + g + 1))
                    dve.wait_ge(added, h * 2 + (16 * t + g + 4))
                    nc.vector.tensor_tensor(acc[:], acc[:], vpage[2 * r + g][:], ALU.add).then_inc(added, 1)

            def residual(t, m):
                dve.wait_ge(projected, 2 * t + m + 1)
                dve.wait_ge(ld["x"], 16 * (t + 1))
                half = x_in[:, 512 * m:512 * m + 512]
                nc.vector.tensor_tensor(half, half, Y[:], ALU.add).then_inc(h_ready, 1)

            maximum(0, 0, 0)
            for t in range(NT):
                pages_of(t, 0, 0, 0)
                maximum(t, 1, 1)
                pages_of(t, 1, 1, 0)
                if t:
                    residual(t - 1, 0)
                with dve.Fori(1, AH // 2 - 1) as i:
                    maximum(t, i * 2, 0)
                    pages_of(t, i * 2, 0, i)
                    maximum(t, i * 2 + 1, 1)
                    pages_of(t, i * 2 + 1, 1, i)
                maximum(t, AH - 2, 0)
                pages_of(t, AH - 2, 0, AH // 2 - 1)
                maximum(t, AH - 1, 1)
                if t:
                    residual(t - 1, 1)
                pages_of(t, AH - 1, 1, AH // 2 - 1)
                dve.wait_ge(exped, C + sbase[t + 1])
                if t < HALVED:
                    nc.vector.reciprocal(pinv[:], psum[t % 2][:, 0, :]).then_inc(inverse, 1)
                else:
                    nc.vector.tensor_tensor(pinv[:], psum[t % 2][:, 0, :], psum[t % 2][:, 1, :], ALU.add).then_inc(totalled, 1)
                    dve.wait_ge(totalled, t - HALVED + 1)
                    nc.vector.reciprocal(pinv[:], pinv[:]).then_inc(inverse, 1)
                if t + 1 < NT:
                    maximum(t + 1, 0, 0)
                gate = mix[:, 0:AW].rearrange("p (h d) -> p h d", h=AH)
                dve.wait_ge(inverse, C + t + 1)
                dve.wait_ge(ld["mix"], 16 * (t + 1))
                nc.vector.tensor_tensor(gate, gate, pinv[:].unsqueeze(2).to_broadcast([P, AH, AD]), ALU.mult).then_inc(scaled, 1)
                dve.wait_ge(used, C + pbase[t + 1])
                dve.wait_ge(scaled, t + 1)
                nc.vector.scalar_tensor_tensor(mix[:, 0:AW], O[:], 0.5, mix[:, 0:AW], ALU.mult, ALU.mult).then_inc(gated, 1)
                if t % 2 == 1:
                    dve.wait_ge(dec_summed, t // 2 + 1)
                    nc.vector.tensor_copy(keep["s_dec"][:, 4 * (t // 2):4 * (t // 2) + 4], Y[:, 0:4]).then_inc(dec_out, 1)
            for m in range(2):
                residual(NT - 1, m)

        @block.tensor
        def _(pe):
            for q in (scored, turned, used):
                pe.sem_inc(q, C)

            def keys_queries(t):
                n = kq_item(t)
                pe.wait_ge(ld["k"], 16 * (t + 1))
                pe.wait_ge(ld["q"], 16 * (t + 1))
                pe.wait_ge(ld["v"], 16 * (t + 1))
                pe.wait_ge(augmented, t + 1)
                for m in range(4):
                    pe.wait_ge(evac, n + m + C - 1)
                    src = k_in if m < 2 else q_in
                    for j in range(4):
                        op = nc.tensor.transpose(T[(n + m) % 2][0:AD + 1, j * P:(j + 1) * P], src[:, 4 * (m % 2) + j, :], keep["ident"][:])
                    op.then_inc(turned, 1)

            def score(t, h, r):
                pe.wait_ge(q_ready, h + (C + t * AH + 1))
                for k, (lo, hi, to) in enumerate(parts(t, r)):
                    if t < HALVED:
                        pe.wait_ge(exped, before(t, h - 1))
                    elif t == HALVED and isinstance(h, int) and h == 0:
                        pe.wait_ge(exped, before(t, 0))
                    else:
                        pe.wait_ge(exped, before(t, h - 1) + (k + 1))
                    for at in range(lo, hi, 512):
                        n = min(512, hi - at)
                        op = nc.tensor.matmul(S[:, at:at + n], q_head[r][:],
                                              KT[:, bass.ds(h, 1), at - lo + to:at - lo + to + n].rearrange("p a n -> p (a n)"), start=True, stop=True)
                    if k == halves(t) - 1:
                        op = nc.tensor.matmul(S[:, hi - P:hi], keep["ident_bf"][:], keep["mask_bf"][:], start=False, stop=True,
                                              skip_group_check=True)
                    op.then_inc(scored, 1)

            def weigh(t, h, r):
                nb = blocks(t)
                if t >= HALVED:
                    for b in range(nb):
                        product(t, h, r, b)
                        if b + 2 < nb:
                            turn(t, h, r, b + 2)
                else:
                    turn(t, h, r, 0)
                    for b in range(nb):
                        if b + 1 < nb:
                            turn(t, h, r, b + 1)
                        product(t, h, r, b)

            def begin(t, h, r):
                if t >= HALVED:
                    turn(t, h, r, 0)
                    turn(t, h, r, 1)

            def turn(t, h, r, b):
                i = (r * blocks(t) + b) % 2
                if b % 2 == 0:
                    pe.wait_ge(exped, before(t, h) + (b // 2 + 1))
                pe.wait_ge(evac, head_item(t, h) + (b + C - 1))
                for j in range(4 * b, min(4 * b + 4, t + 1)):
                    op = nc.tensor.transpose(T[i][:, (j - 4 * b) * P:(j - 4 * b + 1) * P], prob[r][:, j * P:(j + 1) * P], keep["ident"][:])
                op.then_inc(turned, 1)

            def product(t, h, r, b):
                i = (r * blocks(t) + b) % 2
                pe.wait_ge(evac, head_item(t, h) + (b + C + 1))
                for j in range(4 * b, min(4 * b + 4, t + 1)):
                    op = nc.tensor.matmul(O[:, bass.ds(h * AD, AD)], probT[i][:, (j - 4 * b) * P:(j - 4 * b + 1) * P],
                                          V[:, j, bass.ds(h * AD, AD)], start=j == 0, stop=j == t, skip_group_check=True)
                op.then_inc(used, 1)

            def project(t, m):
                if t == 0 and m == 0:
                    pe.wait_ge(w_in, 16 * KC)
                pe.wait_ge(evac, C + y_item(t) + 2)
                if m == 0 and t % 2 == 1:
                    pe.wait_ge(dec_out, t // 2 + 1)
                if 2 * t + m:
                    pe.wait_ge(h_ready, 2 * t + m)
                for k in range(KC):
                    op = nc.tensor.matmul(Y[:], yT[:, k, :], w_out[:, k, 512 * m:512 * m + 512], start=k == 0, stop=k == KC - 1)
                op.then_inc(projected, 1)

            pe.wait_ge(consts, 1)
            keys_queries(0)
            pe.wait_ge(evac, C + 4)
            score(0, 0, 0)
            for t in range(NT):
                begin(t, 0, 0)
                score(t, 1, 1)
                if t:
                    project(t - 1, 0)
                weigh(t, 0, 0)
                begin(t, 1, 1)
                score(t, 2, 0)
                weigh(t, 1, 1)
                with pe.Fori(1, AH // 2 - 1) as i:
                    for r in range(2):
                        begin(t, i * 2 + r, r)
                        score(t, i * 2 + (r + 1), 1 - r)
                        weigh(t, i * 2 + r, r)
                begin(t, AH - 2, 0)
                score(t, AH - 1, 1)
                if t:
                    project(t - 1, 1)
                weigh(t, AH - 2, 0)
                if t + 1 < NT:
                    keys_queries(t + 1)
                begin(t, AH - 1, 1)
                weigh(t, AH - 1, 1)
                if t + 1 < NT:
                    pe.wait_ge(evac, C + kq_item(t + 1) + 4)
                    score(t + 1, 0, 0)
                if t % 2 == 1:
                    pe.wait_ge(added, 4 + 16 * (t + 1))
                    pe.wait_ge(h_ready, 2 * t)
                    for c in range(4):
                        for j in range(2):
                            op = nc.tensor.matmul(Y[:, c:c + 1], acc[:, j, c * P:(c + 1) * P], keep["ones"][:, 0:1], start=j == 0, stop=j == 1, skip_group_check=True)
                    op.then_inc(dec_summed, 1)
                n = y_item(t)
                pe.wait_ge(gated, t + 1)
                for m in range(2):
                    pe.wait_ge(evac, n + m + C - 1)
                    for j in range(4):
                        op = nc.tensor.transpose(T[m][:, j * P:(j + 1) * P], mix[:, (4 * m + j) * P:(4 * m + j + 1) * P], keep["ident"][:])
                    op.then_inc(turned, 1)
            for m in range(2):
                project(NT - 1, m)

        main.close()

        with ExitStack() as st2:
            s2 = Scope(nc, st2, "as")
            step = Chain(s2.sem("step"), "order turn self_v add_v gate turn_y yT project residual".split())
            load, stored = s2.sem("load"), s2.sem("stored")
            attT = probT[0][:, 0:4 * NB].rearrange("p (c b) -> p c b", b=NB)
            rows, xs, vs, own = mix[0:NB, :], x_in[0:NB, :], k_in[0:NB, :, 0:AD], acc[0:NB, 0, :]
            block = st2.enter_context(nc.Block())
            v3 = lambda ap: ap.rearrange("p (h d) -> p h d", h=AH)

            @block.sync
            def _(sp):
                sp.dma_start(rows, io["s_mixed"]).then_inc(load, 16)
                sp.dma_start(xs, io["x_sample"]).then_inc(load, 16)
                sp.dma_start(vs, io["v_sample"].rearrange("b (h d) -> b h d", h=AH)).then_inc(load, 16)
                sp.wait_ge(step.sem, len(step.names))
                sp.dma_start(io["h1_sample"], xs).then_inc(stored, 16)
                sp.wait_ge(stored, 16)

            @block.scalar
            def _(act):
                step.wait(act, "yT")
                nc.scalar.activation(yT[:, :, 0:NB], T[1][:, 0:KC * NB].rearrange("p (k b) -> p k b", b=NB), ACT.Copy).then_inc(step.sem, 1)

            @block.vector
            def _(dve):
                nc.vector.tensor_copy(attT, keep["s_dec"][:, 0:4 * NB].rearrange("p (b c) -> p c b", c=4)).then_inc(step.sem, 1)
                dve.wait_ge(load, 48)
                step.wait(dve, "self_v")
                nc.vector.tensor_tensor(v3(own), vs, keep["s_self"][:].unsqueeze(2).to_broadcast([NB, AH, AD]), ALU.mult).then_inc(step.sem, 1)
                step.wait(dve, "add_v")
                nc.vector.tensor_tensor(own, own, T[0][0:NB, :], ALU.add).then_inc(step.sem, 1)
                step.wait(dve, "gate")
                nc.vector.scalar_tensor_tensor(rows[:, 0:AW], own, 0.5, rows[:, 0:AW], ALU.mult, ALU.mult).then_inc(step.sem, 1)
                step.wait(dve, "residual")
                nc.vector.tensor_tensor(xs, xs, S[0:NB, 0:D], ALU.add).then_inc(step.sem, 1)

            @block.tensor
            def _(pe):
                step.wait(pe, "turn")
                for c in range(4):
                    op = nc.tensor.transpose(T[0][0:NB, c * P:(c + 1) * P], attT[:, c, :], keep["ident"][:])
                op.then_inc(step.sem, 1)
                step.wait(pe, "turn_y")
                for k in range(KC):
                    op = nc.tensor.transpose(T[1][:, k * NB:(k + 1) * NB], rows[:, k * P:(k + 1) * P], keep["ident"][0:NB, 0:NB])
                op.then_inc(step.sem, 1)
                step.wait(pe, "project")
                for m in range(2):
                    for k in range(KC):
                        op = nc.tensor.matmul(S[0:NB, 512 * m:512 * m + 512], yT[:, k, 0:NB], w_out[:, k, 512 * m:512 * m + 512], start=k == 0, stop=k == KC - 1)
                op.then_inc(step.sem, 1)


def mlstm(nc, io, keep):
    with ExitStack() as st:
        s = Scope(nc, st, "ml")
        w = s.sb("w", [P, KC, ODD_COLS])
        wq, wk, wv = (s.sb(n, [P, CH, 2, CD]) for n in ("wq", "wk", "wv"))
        g_row, ngh, skiph = (s.sb(n, [P, D]) for n in ("g_row", "ngh", "skiph"))
        cw = s.sb("cw", [P, KC, 4])
        cb = s.sb("cb", [P, KC])
        b_if = s.sb("b_if", [P, 2 * CH])
        bank_stack = st.enter_context(ExitStack())
        bank_scope = Scope(nc, bank_stack, "mb")
        B = [bank_scope.ps(f"B{i}") for i in range(8)]
        w_final_in = s.sem("w_final_in")
        GATES = 3 * CW
        A1 = CD + 1

        with ExitStack() as st2:
            s2 = Scope(nc, st2, "mp")
            x = s2.sb("x", [P, D])
            xT = s2.sb("xT", [P, KC, P])
            xcT = s2.sb("xcT", [P, KC, P + 3])
            cv = s2.sb("cv", [P, KC, P])
            th = s2.sb("th", [P, KC, P])
            qT, kT = s2.sb("qT", [P, KC, P]), s2.sb("kT", [P, KC, P])
            kw = s2.sb("kw", [P, CW])
            va = s2.sb("va", [P, CH, A1])
            state = s2.sb("state", [P, CH, 2, A1])
            sz, tho = s2.sb("sz", [P, D]), s2.sb("tho", [P, D])
            inter = s2.sb("inter", [P, CH, A1])
            wt = s2.sb("wt", [P, CH, P])
            smT = s2.sb("smT", [P, CH, P])
            skx = s2.sb("skx", [P, D])
            ssq, msq, rstd = (s2.sb(n, [P, 1]) for n in ("ssq", "msq", "rstd"))
            g8, e4, lf, bb, gg, ml, mbc, wlh, den, dinv, var4, rs4 = (
                s2.sb(n, [P, k]) for n, k in (("g8", 8), ("e4", 4), ("lf", 4), ("bb", 8), ("gg", 4), ("ml", 4), ("mbc", 4),
                                              ("wlh", 4), ("den", 4), ("dinv", 4), ("var4", 4), ("rs4", 4)))
            dd = s2.sb("dd", [P, 16])
            st6 = s2.sb("st6", [P, CH, 6])
            mv = s2.sb("mv", [P, CH, 2])
            mrow, blrow = s2.sb("mrow", [CH, 1]), s2.sb("blrow", [CH, 1])
            M = s2.sb("M", [CH, P])
            low = s2.sb("low", [CH, P])
            sel = s2.sb("sel", [CH, CH, P])
            loads, const = s2.sem("loads"), s2.sem("const")
            w_first, w_rest, w_heads = (s2.sem(n) for n in ("w_first", "w_rest", "w_heads"))
            ld = s2.sems("x")
            y_stored = s2.sem("y_stored")
            last_out = s2.sem("last_out")
            q = s2.sems("ssq msq rstd xn "
                        "p_xT p_xc p_z p_g p_o p_cum p_q p_k p_kt p_v p_skip p_gT p_M p_S p_inter p_intra p_c "
                        "a_xT a_xc a_th a_cv0 a_z a_abs a_e a_ln a_o a_q a_k a_kw a_v a_w a_dd a_inter "
                        "d_cv0 d_cv1 d_cv2 d_cv carried d_sz d_g8 d_lf d_bb d_gg d_M d_ml d_dd d_wlh d_m d_skip d_sm d_num "
                        "d_den d_den2 d_dinv d_hc d_st d_mv d_var d_hn d_A d_B d_E d_y d_c rs4")
            INTER, INTRA = (5, 0, 7, 1), (6, 2, 3, 4)
            UPD = INTER + INTRA
            block = st2.enter_context(nc.Block())

            def tiles(eng, body):
                body(0, first=True)
                with eng.Fori(1, NT - 1) as t:
                    body(t)
                body(NT - 1, last=True)

            def begin(eng, names):
                for n in names.split():
                    eng.sem_inc(q[n], LEAD * {"p_inter": 4, "p_intra": 4, "p_c": 8, "a_inter": 4, "d_num": 4, "d_c": 8}.get(n, 1))

            @block.sync
            def _(sp):
                sp.sem_inc(ld["x"], 16 * LEAD)
                sp.sem_inc(y_stored, 16 * LEAD)
                sp.dma_start(x[:], io["h1"][0:P, :]).then_inc(ld["x"], 16)
                for sem, lo, hi in ((w_first, 0, CW), (w_rest, CW, ODD_COLS)):
                    for k in range(KC):
                        sp.dma_start(w[:, k, lo:hi], io["odd_w_in"][k * P:(k + 1) * P, lo:hi]).then_inc(sem, 16)
                for n, dst in (("w_q", wq), ("w_k", wk), ("w_v", wv)):
                    sp.dma_start(dst[:], io[n].rearrange("h (c p) e -> p h c e", p=P)).then_inc(w_heads, 16)

                def body(t, first=False, last=False):
                    if not last:
                        wait_stage(sp, q["p_xT"], t)
                        sp.dma_start(x[:], io["h1"][bass.ds((t + 1) * P, P), :]).then_inc(ld["x"], 16)
                    wait_stage(sp, q["d_y"], t)
                    sp.dma_start(io["y2"][bass.ds(t * P, P), :], sz[:]).then_inc(y_stored, 16)
                tiles(sp, body)
                wait_stage(sp, q["d_c"], NT - 1, per_tile=8)
                sp.dma_start(io["c_prompt"].rearrange("(h c p) v -> p (h c) v", p=P, c=2), state[:, :, :, 0:CD].rearrange("p h c v -> p (h c) v")).then_inc(last_out, 16)
                with nc.allow_non_contiguous_dma(reason="small outputs"):
                    sp.dma_start(io["n_prompt"].rearrange("o (h c p) -> p (o h) c", p=P, c=2), state[:, :, :, CD]).then_inc(last_out, 16)
                    wait_stage(sp, q["d_m"], NT - 1)
                    sp.dma_start(io["m_prompt"].rearrange("o h -> h o"), mrow[:]).then_inc(last_out, 16)
                    for c in range(KC):
                        sp.dma_start(io["conv_prompt"][:, c * P:(c + 1) * P].rearrange("j p -> p j"), xcT[:, c, P:P + 3]).then_inc(last_out, 16)
                sp.wait_ge(last_out, 16 * (3 + KC))
                wait_dma(sp, y_stored, NT - 1)

            @block.gpsimd
            def _(pool):
                begin(pool, "rstd rs4")
                nc.gpsimd.memset(xcT[:, :, 0:3], 0.0).then_inc(const, 1)
                nc.gpsimd.memset(state[:], 0.0).then_inc(const, 1)
                nc.gpsimd.memset(va[:, :, CD:A1], 1.0).then_inc(const, 1)
                nc.gpsimd.memset(mrow[:], 0.0).then_inc(const, 1)
                nc.gpsimd.memset(mbc[:], 0.0).then_inc(const, 1)
                nc.gpsimd.memset(low[:], -3e38).then_inc(const, 1)
                nc.gpsimd.memset(sel[:], 0.0).then_inc(const, 1)
                pool.wait_ge(const, 7)
                nc.gpsimd.affine_select(out=sel[:], in_=sel[:], compare_op=ALU.not_equal, fill=1.0, base=0,
                                        pattern=[[-1, CH], [0, P]], channel_multiplier=1).then_inc(const, 1)
                pool.wait_ge(loads, 16 * 10)
                nc.gpsimd.tensor_tensor(ngh[:], ngh[:], keep["half"][:].to_broadcast([P, D]), ALU.mult).then_inc(const, 1)
                nc.gpsimd.tensor_tensor(skiph[:], skiph[:], keep["half"][:].to_broadcast([P, D]), ALU.mult).then_inc(const, 1)

                def norm(t):
                    wait_stage(pool, q["xn"], t, back=1)
                    wait_stage(pool, q["msq"], t)
                    nc.gpsimd.tensor_tensor(rstd[:], msq[:], keep["minus_half"][:], ALU.pow).then_inc(q["rstd"], 1)
                norm(0)

                def body(t, first=False, last=False):
                    if not last:
                        norm(t + 1)
                    wait_stage(pool, q["d_var"], t)
                    wait_stage(pool, q["d_hn"], t, back=1)
                    nc.gpsimd.tensor_tensor(rs4[:], var4[:], keep["minus_half"][:].to_broadcast([P, CH]), ALU.pow).then_inc(q["rs4"], 1)
                tiles(pool, body)

            @block.scalar
            def _(act):
                act.dma_start(g_row[:], io["norm_g"][1, :].partition_broadcast(P)).then_inc(loads, 16)
                act.dma_start(ngh[:], io["norm_c"].partition_broadcast(P)).then_inc(loads, 16)
                act.dma_start(skiph[:], io["skip"].partition_broadcast(P)).then_inc(loads, 16)
                act.dma_start(b_if[:, 0:CH], io["odd_b_i"].partition_broadcast(P)).then_inc(loads, 16)
                act.dma_start(b_if[:, CH:2 * CH], io["odd_b_f"].partition_broadcast(P)).then_inc(loads, 16)
                with nc.allow_non_contiguous_dma(reason="convolution weights by channel"):
                    act.dma_start(cb[:], io["conv_b"].rearrange("(c p) -> p c", p=P)).then_inc(loads, 16)
                    for j in range(4):
                        act.dma_start(cw[:, :, j], io["conv_w"][j, :].rearrange("(c p) -> p c", p=P)).then_inc(loads, 16)
                begin(act, "ssq a_xT a_xc a_th a_cv0 a_z a_abs a_e a_ln a_o a_q a_k a_kw a_v a_w a_dd a_inter")
                act.wait_ge(loads, 16 * 10)

                def square(t):
                    wait_dma(act, ld["x"], t)
                    wait_stage(act, q["msq"], t, back=1)
                    wait_stage(act, q["d_cv"], t, back=1)
                    nc.scalar.activation(th[:].rearrange("p k n -> p (k n)"), x[:], ACT.Square, accum_out=ssq[:]).then_inc(q["ssq"], 1)

                def turn_out(t):
                    wait_stage(act, q["p_xT"], t)
                    wait_stage(act, q["p_o"], t, back=1)
                    nc.scalar.activation(xT[:, 0:4, :], B[1][:].rearrange("p (k n) -> p k n", k=4), ACT.Copy)
                    nc.scalar.activation(xT[:, 4:8, :], B[4][:].rearrange("p (k n) -> p k n", k=4), ACT.Copy).then_inc(q["a_xT"], 1)
                square(0)
                turn_out(0)

                def body(t, first=False, last=False):
                    k4 = lambda ap: ap.rearrange("p (k n) -> p k n", k=4)
                    wait_stage(act, q["p_xc"], t)
                    wait_stage(act, q["p_v"], t, back=1)
                    wait_stage(act, q["carried"], t, back=1)
                    if first:
                        act.wait_ge(const, 1)
                    for m in range(2):
                        op = nc.scalar.activation(xcT[:, 4 * m:4 * m + 4, 3:P + 3], k4(B[m][:]), ACT.Copy)
                    op.then_inc(q["a_xc"], 1)
                    wait_stage(act, q["a_xc"], t)
                    wait_stage(act, q["p_skip"], t, back=1)
                    wait_stage(act, q["p_kt"], t, back=1)
                    for c in range(KC):
                        op = nc.scalar.activation(cv[:, c, :], xcT[:, c, 3:P + 3], ACT.Identity, bias=cb[:, c:c + 1], scale=cw[:, c, 3:4])
                    op.then_inc(q["a_cv0"], 1)
                    wait_stage(act, q["p_z"], t)
                    wait_dma(act, y_stored, t, back=1)
                    for m in range(2):
                        op = nc.scalar.activation(sz[:, 512 * m:512 * m + 512], B[6 + m][:], ACT.Tanh, scale=0.5)
                    op.then_inc(q["a_z"], 1)
                    wait_stage(act, q["d_cv2"], t)
                    nc.scalar.activation(th[:], cv[:], ACT.Tanh, scale=0.5).then_inc(q["a_th"], 1)
                    wait_stage(act, q["p_o"], t)
                    wait_stage(act, q["d_A"], t, back=1)
                    for m in range(2):
                        op = nc.scalar.activation(tho[:, 512 * m:512 * m + 512], B[m][:], ACT.Tanh, scale=0.5)
                    op.then_inc(q["a_o"], 1)
                    wait_stage(act, q["d_g8"], t)
                    wait_stage(act, q["d_lf"], t, back=1)
                    nc.scalar.activation(e4[:], g8[:, CH:2 * CH], ACT.Abs).then_inc(q["a_abs"], 1)
                    wait_stage(act, q["a_abs"], t)
                    nc.scalar.activation(e4[:], e4[:], ACT.Exp, scale=-1.0).then_inc(q["a_e"], 1)
                    wait_stage(act, q["a_e"], t)
                    nc.scalar.activation(e4[:], e4[:], ACT.Ln, bias=1.0).then_inc(q["a_ln"], 1)
                    wait_stage(act, q["p_q"], t)
                    wait_stage(act, q["p_inter"], t, back=1, per_tile=4)
                    for m in range(2):
                        op = nc.scalar.activation(qT[:, 4 * m:4 * m + 4, :], k4(B[4 + m][:]), ACT.Copy, scale=0.5 * CD ** -0.5)
                    op.then_inc(q["a_q"], 1)
                    wait_stage(act, q["p_k"], t)
                    wait_stage(act, q["p_S"], t, back=1)
                    for m in range(2):
                        op = nc.scalar.activation(kT[:, 4 * m:4 * m + 4, :], k4(B[6 + m][:]), ACT.Copy, scale=0.5)
                    op.then_inc(q["a_k"], 1)
                    if not last:
                        square(t + 1)
                    wait_stage(act, q["p_v"], t)
                    wait_stage(act, q["p_c"], t, back=1, per_tile=8)
                    for m in range(2):
                        op = nc.scalar.activation(va[:, 2 * m:2 * m + 2, 0:CD], B[4 + m][:].rearrange("p (h v) -> p h v", h=2), ACT.Copy)
                    op.then_inc(q["a_v"], 1)
                    wait_stage(act, q["p_M"], t)
                    wait_stage(act, q["d_gg"], t)
                    wait_stage(act, q["d_sm"], t, back=1)
                    for h in range(CH):
                        op = nc.scalar.activation(wt[:, h, :], B[3][:, h * P:(h + 1) * P], ACT.Exp, bias=gg[:, h:h + 1], scale=-1.0)
                    op.then_inc(q["a_w"], 1)
                    wait_stage(act, q["d_dd"], t)
                    nc.scalar.activation(dd[:], dd[:], ACT.Exp).then_inc(q["a_dd"], 1)
                    wait_stage(act, q["d_wlh"], t)
                    wait_stage(act, q["p_kt"], t)
                    for h in range(CH):
                        op = nc.scalar.activation(kw[:, h * CD:(h + 1) * CD], B[h // 2][:, (h % 2) * CD:(h % 2 + 1) * CD], ACT.Identity, scale=wlh[:, h:h + 1])
                    op.then_inc(q["a_kw"], 1)
                    if not last:
                        turn_out(t + 1)
                    for h in range(CH):
                        wait_stage(act, q["p_inter"], t, per_tile=4, nth=h + 1)
                        wait_stage(act, q["d_num"], t, back=1, per_tile=4)
                        nc.scalar.activation(inter[:, h, :], B[INTER[h]][:, 0:A1], ACT.Identity, scale=dd[:, h:h + 1]).then_inc(q["a_inter"], 1)
                tiles(act, body)

            @block.vector
            def _(dve):
                begin(dve, "msq xn d_cv0 d_cv1 d_cv2 d_cv carried d_sz d_g8 d_lf d_bb d_gg d_M d_ml d_dd d_wlh d_m d_skip d_sm d_num "
                           "d_den d_den2 d_dinv d_hc d_st d_mv d_var d_hn d_A d_B d_E d_y d_c")
                dve.wait_ge(loads, 16 * 10)
                dve.wait_ge(const, 10)

                def mean_square(t):
                    wait_stage(dve, q["ssq"], t)
                    wait_stage(dve, q["rstd"], t, back=1)
                    nc.vector.tensor_scalar(msq[:], ssq[:], 1.0 / D, EPS, ALU.mult, ALU.add).then_inc(q["msq"], 1)

                def normed(t):
                    wait_stage(dve, q["rstd"], t)
                    nc.vector.scalar_tensor_tensor(x[:], x[:], rstd[:], g_row[:], ALU.mult, ALU.mult).then_inc(q["xn"], 1)
                mean_square(0)
                normed(0)

                def body(t, first=False, last=False):
                    flat = lambda ap: ap.rearrange("p k n -> p (k n)")

                    def small(stage, op):
                        op.then_inc(q[stage], 1)
                        wait_stage(dve, q[stage], t)
                    wait_stage(dve, q["a_cv0"], t)
                    for j, stage in ((0, "d_cv0"), (1, "d_cv1"), (2, "d_cv2")):
                        for c in range(KC):
                            op = nc.vector.scalar_tensor_tensor(cv[:, c, :], xcT[:, c, j:j + P], cw[:, c, j:j + 1], cv[:, c, :], ALU.mult, ALU.add)
                        op.then_inc(q[stage], 1)
                        wait_stage(dve, q[stage], t)
                    if not last:
                        nc.vector.tensor_copy(xcT[:, :, 0:3], xcT[:, :, P:P + 3]).then_inc(q["carried"], 1)
                    wait_stage(dve, q["a_th"], t)
                    nc.vector.scalar_tensor_tensor(flat(cv[:]), flat(th[:]), 1.0, flat(cv[:]), ALU.add, ALU.mult).then_inc(q["d_cv"], 1)
                    wait_stage(dve, q["a_z"], t)
                    for m in range(2):
                        op = nc.vector.scalar_tensor_tensor(sz[:, 512 * m:512 * m + 512], sz[:, 512 * m:512 * m + 512], 1.0, B[6 + m][:], ALU.add, ALU.mult)
                    op.then_inc(q["d_sz"], 1)
                    wait_stage(dve, q["p_g"], t)
                    small("d_g8", nc.vector.tensor_tensor(g8[:], B[2][:, 0:8], b_if[:], ALU.add))
                    wait_stage(dve, q["a_ln"], t)
                    wait_stage(dve, q["p_cum"], t, back=1)
                    small("d_lf", nc.vector.scalar_tensor_tensor(lf[:], g8[:, CH:2 * CH], 0.0, e4[:], ALU.min, ALU.subtract))
                    wait_stage(dve, q["p_cum"], t)
                    small("d_bb", nc.vector.tensor_copy(bb[:], B[2][:, 8:16]))
                    nc.vector.tensor_copy(blrow[:], B[2][0:CH, 16:17])
                    wait_stage(dve, q["a_w"], t, back=1)
                    small("d_gg", nc.vector.tensor_tensor(gg[:], g8[:, 0:CH], bb[:, 0:CH], ALU.subtract))
                    wait_stage(dve, q["p_gT"], t)
                    small("d_M", nc.vector.tensor_tensor_scan(M[:], low[:], B[2][0:CH, 32:32 + P], mrow[:], ALU.max, ALU.max))
                    wait_stage(dve, q["p_skip"], t)
                    for m in range(2):
                        op = nc.vector.tensor_tensor(skx[:, 512 * m:512 * m + 512], B[6 + m][:], skiph[:, 512 * m:512 * m + 512], ALU.mult)
                    op.then_inc(q["d_skip"], 1)
                    wait_stage(dve, q["a_w"], t)
                    small("d_ml", nc.vector.tensor_copy(ml[:], B[3][:, P - 1:4 * P:P]))
                    wait_stage(dve, q["d_c"], t, back=1, per_tile=8)
                    nc.vector.tensor_tensor(dd[:, 0:4], mbc[:], B[2][:, 20:24], ALU.subtract)
                    nc.vector.tensor_tensor(dd[:, 4:8], gg[:], ml[:], ALU.subtract)
                    nc.vector.tensor_tensor(dd[:, 8:12], mbc[:], ml[:], ALU.subtract)
                    small("d_dd", nc.vector.scalar_tensor_tensor(dd[:, 12:16], bb[:, 0:4], -1.0, B[2][:, 20:24], ALU.mult, ALU.subtract))
                    nc.vector.tensor_tensor(mbc[:], ml[:], bb[:, 4:8], ALU.add)
                    small("d_m", nc.vector.tensor_tensor(mrow[:], M[:, P - 1:P], blrow[:], ALU.add))
                    if not last:
                        mean_square(t + 1)
                    wait_stage(dve, q["a_dd"], t)
                    small("d_wlh", nc.vector.tensor_scalar(wlh[:], dd[:, 4:8], 0.5, None, ALU.mult))
                    if not last:
                        normed(t + 1)
                    wait_stage(dve, q["a_w"], t)
                    wait_stage(dve, q["p_S"], t)
                    nc.vector.tensor_tensor(flat(smT[:]), flat(wt[:]), B[6][:], ALU.mult).then_inc(q["d_sm"], 1)
                    for h in range(CH):
                        wait_stage(dve, q["a_inter"], t, per_tile=4, nth=h + 1)
                        wait_stage(dve, q["p_intra"], t, per_tile=4, nth=h + 1)
                        nc.vector.tensor_tensor(inter[:, h, :], inter[:, h, :], B[INTRA[h]][:, 0:A1], ALU.add).then_inc(q["d_num"], 1)
                    for n in range(8):
                        h, c = n // 2, n % 2
                        wait_stage(dve, q["p_c"], t, per_tile=8, nth=n + 1)
                        nc.vector.scalar_tensor_tensor(state[:, h, c, :], state[:, h, c, :], dd[:, 8 + h:9 + h], B[UPD[n]][:, 0:A1], ALU.mult, ALU.add).then_inc(q["d_c"], 1)
                    wait_stage(dve, q["d_num"], t, per_tile=4)
                    dcol = inter[:, :, CD]
                    small("d_den", nc.vector.scalar_tensor_tensor(den[:], dcol, -1.0, dcol, ALU.mult, ALU.max))
                    small("d_den2", nc.vector.tensor_tensor(den[:], den[:], dd[:, 12:16], ALU.max))
                    small("d_dinv", nc.vector.reciprocal(dinv[:], den[:]))
                    for h in range(CH):
                        op = nc.vector.tensor_scalar(inter[:, h, 0:CD], inter[:, h, 0:CD], dinv[:, h:h + 1], None, ALU.mult)
                    small("d_hc", op)
                    for h in range(CH):
                        op = nc.vector.bn_stats(st6[:, h, :], inter[:, h, 0:CD])
                    small("d_st", op)
                    nc.vector.tensor_copy(den[:], dinv[:])
                    for h in range(CH):
                        op = nc.vector.bn_aggr(mv[:, h, :], st6[:, h, :])
                    small("d_mv", op)
                    small("d_var", nc.vector.tensor_scalar(var4[:], mv[:, :, 1], 1.0, EPS, ALU.mult, ALU.add))
                    wait_stage(dve, q["rs4"], t)
                    for h in range(CH):
                        op = nc.vector.tensor_scalar(inter[:, h, 0:CD], inter[:, h, 0:CD], mv[:, h, 0:1], rs4[:, h:h + 1], ALU.subtract, ALU.mult)
                    small("d_hn", op)
                    t4 = tho[:].rearrange("p (h v) -> p h v", h=CH)
                    wait_stage(dve, q["a_o"], t)
                    small("d_A", nc.vector.scalar_tensor_tensor(inter[:, :, 0:CD], t4, 1.0, inter[:, :, 0:CD], ALU.add, ALU.mult))
                    small("d_B", nc.vector.tensor_tensor(inter[:, :, 0:CD], inter[:, :, 0:CD], ngh[:].rearrange("p (h v) -> p h v", h=CH), ALU.mult))
                    small("d_E", nc.vector.tensor_tensor(inter[:, :, 0:CD], inter[:, :, 0:CD], skx[:].rearrange("p (h v) -> p h v", h=CH), ALU.add))
                    sz4 = sz[:].rearrange("p (h v) -> p h v", h=CH)
                    small("d_y", nc.vector.scalar_tensor_tensor(sz4, inter[:, :, 0:CD], 0.5, sz4, ALU.mult, ALU.mult))
                tiles(dve, body)

            @block.tensor
            def _(pe):
                begin(pe, "p_xT p_xc p_z p_g p_o p_cum p_q p_k p_kt p_v p_skip p_gT p_M p_S p_inter p_intra p_c")
                pe.wait_ge(const, 10)

                def turn(t):
                    wait_stage(pe, q["xn"], t)
                    wait_stage(pe, q["a_kw"], t, back=1)
                    wait_stage(pe, q["a_v"], t, back=1)
                    for k in range(KC):
                        op = nc.tensor.transpose(B[1 if k < 4 else 4][:, (k % 4) * P:(k % 4 + 1) * P], x[:, k * P:(k + 1) * P], keep["ident"][:])
                    op.then_inc(q["p_xT"], 1)
                turn(0)

                def body(t, first=False, last=False):
                    def project(banks, col, stage):
                        for m in range(2):
                            for k in range(KC):
                                op = nc.tensor.matmul(B[banks[m]][:], xT[:, k, :], w[:, k, col + 512 * m:col + 512 * m + 512], start=k == 0, stop=k == KC - 1)
                        op.then_inc(q[stage], 1)
                    wait_stage(pe, q["a_xT"], t)
                    wait_stage(pe, q["d_c"], t, back=1, per_tile=8)
                    if first:
                        pe.wait_ge(w_first, 16 * KC)
                    for c in range(KC):
                        for k in range(KC):
                            op = nc.tensor.matmul(B[c // 4][:, (c % 4) * P:(c % 4 + 1) * P], w[:, k, c * P:(c + 1) * P], xT[:, k, :], start=k == 0, stop=k == KC - 1)
                    op.then_inc(q["p_xc"], 1)
                    if first:
                        pe.wait_ge(w_rest, 16 * KC)
                    project((6, 7), CW, "p_z")
                    for k in range(KC):
                        op = nc.tensor.matmul(B[2][:, 0:8], xT[:, k, :], w[:, k, GATES:GATES + 8], start=k == 0, stop=k == KC - 1)
                    op.then_inc(q["p_g"], 1)
                    wait_stage(pe, q["a_xc"], t)
                    project((0, 1), 2 * CW, "p_o")
                    wait_stage(pe, q["d_cv"], t)
                    if first:
                        pe.wait_ge(w_heads, 16 * 3)
                    for banks, wt_, stage in (((4, 5), wq, "p_q"), ((6, 7), wk, "p_k")):
                        if stage == "p_k":
                            wait_stage(pe, q["d_lf"], t)
                            nc.tensor.matmul(B[2][:, 8:12], keep["upto"][:], lf[:], start=True, stop=True)
                            nc.tensor.matmul(B[2][:, 12:16], keep["ones"][:], lf[:], start=True, stop=True)
                            nc.tensor.matmul(B[2][0:CH, 16:17], lf[:], keep["ones"][:, 0:1], start=True, stop=True).then_inc(q["p_cum"], 1)
                            wait_stage(pe, q["d_sz"], t)
                        for n in range(8):
                            h, e = n // 2, n % 2
                            for c in range(2):
                                op = nc.tensor.matmul(B[banks[n // 4]][:, (n % 4) * P:(n % 4 + 1) * P], wt_[:, h, c, e * P:(e + 1) * P],
                                                      cv[:, 2 * h + c, :], start=c == 0, stop=c == 1)
                        op.then_inc(q[stage], 1)
                    wait_stage(pe, q["a_o"], t)
                    for h in range(CH):
                        for c in range(2):
                            op = nc.tensor.matmul(B[h // 2][:, (h % 2) * CD:(h % 2 + 1) * CD], cv[:, 2 * h + c, :], wk[:, h, c, :], start=c == 0, stop=c == 1)
                    op.then_inc(q["p_kt"], 1)
                    wait_stage(pe, q["d_gg"], t)
                    nc.tensor.transpose(B[2][0:CH, 32:32 + P], gg[:], keep["ident"][:]).then_inc(q["p_gT"], 1)
                    wait_stage(pe, q["a_q"], t)
                    for h in range(CH):
                        for c in range(2):
                            op = nc.tensor.matmul(B[4 + h // 2][:, (h % 2) * CD:(h % 2 + 1) * CD], xcT[:, 2 * h + c, 3:P + 3], wv[:, h, c, :], start=c == 0, stop=c == 1)
                    op.then_inc(q["p_v"], 1)
                    wait_stage(pe, q["a_k"], t)
                    for k in range(KC):
                        op = nc.tensor.transpose(B[6 + k // 4][:, (k % 4) * P:(k % 4 + 1) * P], cv[:, k, :], keep["ident"][:])
                    op.then_inc(q["p_skip"], 1)
                    wait_stage(pe, q["d_M"], t)
                    for h in range(CH):
                        nc.tensor.matmul(B[3][:, h * P:(h + 1) * P], sel[:, h, :], M[:], start=True, stop=True)
                        nc.tensor.matmul(B[3][:, h * P:(h + 1) * P], keep["ident_bf"][:], keep["maskT_bf"][:], start=False, stop=True, skip_group_check=True)
                    nc.tensor.transpose(B[2][:, 20:24], M[:], keep["ident"][0:CH, 0:CH]).then_inc(q["p_M"], 1)
                    wait_stage(pe, q["d_skip"], t)
                    for h in range(CH):
                        for c in range(2):
                            op = nc.tensor.matmul(B[6][:, h * P:(h + 1) * P], kT[:, 2 * h + c, :], qT[:, 2 * h + c, :], start=c == 0, stop=c == 1)
                    op.then_inc(q["p_S"], 1)
                    if not last:
                        turn(t + 1)
                    wait_stage(pe, q["a_v"], t)
                    wait_stage(pe, q["a_kw"], t)
                    wait_stage(pe, q["d_c"], t, back=1, per_tile=8)
                    for h in range(CH):
                        if h == 3 and not last:
                            wait_stage(pe, q["a_xT"], t + 1)
                        for c in range(2):
                            op = nc.tensor.matmul(B[INTER[h]][:, 0:A1], qT[:, 2 * h + c, :], state[:, h, c, :], start=c == 0, stop=c == 1)
                        op.then_inc(q["p_inter"], 1)
                    wait_stage(pe, q["d_sm"], t)
                    wait_stage(pe, q["d_dd"], t)
                    for h in range(CH):
                        nc.tensor.matmul(B[INTRA[h]][:, 0:A1], smT[:, h, :], va[:, h, :], start=True, stop=True).then_inc(q["p_intra"], 1)
                    for n in range(8):
                        h, c = n // 2, n % 2
                        if n < 4:
                            wait_stage(pe, q["a_inter"], t, per_tile=4, nth=n + 1)
                        else:
                            wait_stage(pe, q["d_num"], t, per_tile=4, nth=n - 3)
                        nc.tensor.matmul(B[UPD[n]][:, 0:A1], kw[:, h * CD + c * P:h * CD + (c + 1) * P], va[:, h, :], start=True, stop=True).then_inc(q["p_c"], 1)
                tiles(pe, body)

        with ExitStack() as st2:
            s2 = Scope(nc, st2, "md")
            xs, xc, sz, tho, acc, qs, ks, vs = (s2.sb(n, [NB, D]) for n in ("xs", "xc", "sz", "tho", "acc", "qs", "ks", "vs"))
            buf = s2.sb("buf", [NB, 3, D])
            tap = s2.sb("tap", [NB, 4, D])
            xT, cT, xcT = (s2.sb(n, [P, KC, NB]) for n in ("xT", "cT", "xcT"))
            qTm = s2.sb("qTm", [P, KC, NB, NB])
            eye = s2.sb("eye", [P, NB, NB])
            SLOTS = 6
            C = ([s2.sb(f"C{i}", [P, 2, CD])[:] for i in range(SLOTS // 2)]
                 + [w[:, i, D:D + 2 * CD].rearrange("p (c v) -> p c v", c=2) for i in range(SLOTS // 2)])
            ad = s2.sb("ad", [NB, NB, CH])
            a_bc = s2.sb("a_bc", [P, NB * CH])
            ssq, msq, rstd = (s2.sb(n, [NB, 1]) for n in ("ssq", "msq", "rstd"))
            g8 = s2.sb("g8", [NB, 8])
            e4, lf, m4, pr, mt, qk, qn, smw, den, dinv, var4, rs4 = (s2.sb(n, [NB, CH]) for n in (
                "e4", "lf", "m4", "pr", "mt", "qk", "qn", "smw", "den", "dinv", "var4", "rs4"))
            dd = s2.sb("dd", [NB, 12])
            st6, mv = s2.sb("st6", [NB, CH, 6]), s2.sb("mv", [NB, CH, 2])
            xload, load, nload, stored, eyed = (s2.sem(n) for n in ("xload", "load", "nload", "stored", "eyed"))
            c_in = [s2.sem(f"c_in{i}") for i in range(SLOTS)]
            c_out = [s2.sem(f"c_out{i}") for i in range(SLOTS)]
            spread_v, read, crossed, updated = (s2.sem(n) for n in ("spread_v", "read", "crossed", "updated"))
            row_ready = s2.sem("row_ready")
            step = Chain(s2.sem("step"), (
                "square msq rstd xn turn xT project gates sz g8 abs exp ln lf prior mt dd edd "
                "taps add0 add1 add2 add3 cth cs turn_c cT qkv qkv_out qk1 qk2 qn2 smw aqn den absd dmax dinv "
                "wk an nn turn_q qTm wkT ad spread a_bc loop n1 n2 n3 hc st mv var rs hn A B skip E y").split())
            n = xs
            kw, tmp, th = tap[:, 1, :], tap[:, 2, :], tap[:, 3, :]
            row = tap[:, 0, :].rearrange("p (b n) -> p b n", b=NB)
            wkT = s2.sb("wkT", [P, KC * NB])
            fresh = [w[:, i, D + 2 * CD:D + 4 * CD] for i in range(3)]
            VB = [(B[5], B[6]), (B[7], B[0])]
            h4 = lambda ap: ap.rearrange("p (h v) -> p h v", h=CH)
            wide = lambda ap: ap.unsqueeze(2).to_broadcast([NB, CH, CD])
            block = st2.enter_context(nc.Block())
            PAIRS = [(b, h) for b in range(NB) for h in range(CH)]

            @block.sync
            def _(sp):
                sp.dma_start(xs[:], io["h1_sample"]).then_inc(xload, 16)
                sp.dma_start(buf[:], io["state_conv"]).then_inc(load, 16)
                sp.dma_start(m4[:], io["state_m"]).then_inc(load, 16)
                sp.dma_start(acc[:], io["conv_b"].partition_broadcast(NB)).then_inc(load, 16)
                for j in range(4):
                    sp.dma_start(tap[:, j, :], io["conv_w"][j, :].partition_broadcast(NB)).then_inc(load, 16)
                state = io["state_c"].rearrange("(n c p) v -> n p c v", c=2, p=P)
                new = io["c_sample"].rearrange("(n c p) v -> n p c v", c=2, p=P)
                for i in range(SLOTS // 2):
                    sp.dma_start(C[i], state[i]).then_inc(c_in[i], 16)
                sp.wait_ge(step.sem, step.names.index("turn") + 1)
                sp.dma_start(n[:], io["state_n"]).then_inc(nload, 16)
                sp.wait_ge(step.sem, step.names.index("project") + 1)
                for i in range(SLOTS // 2, SLOTS):
                    sp.dma_start(C[i], state[i]).then_inc(c_in[i], 16)
                for k in range(KC):
                    sp.dma_start(w[:, k, 0:D], io["odd_w_out"][k * P:(k + 1) * P, :]).then_inc(w_final_in, 16)
                sp.wait_ge(step.sem, step.names.index("mt") + 1)
                sp.dma_start(io["m_sample"], mt[:]).then_inc(stored, 16)
                sp.wait_ge(step.sem, step.names.index("gates") + 1)
                sp.dma_start(io["conv_sample"][:, 0:2, :], buf[:, 1:3, :]).then_inc(stored, 16)
                sp.dma_start(io["conv_sample"][:, 2, :], xc[:]).then_inc(stored, 16)
                sp.wait_ge(step.sem, step.names.index("nn") + 1)
                sp.dma_start(io["n_sample"], n[:]).then_inc(stored, 16)
                for i in range(len(PAIRS)):
                    sp.wait_ge(updated, i + 1)
                    sp.dma_start(new[i], C[i % SLOTS]).then_inc(c_out[i % SLOTS], 16)
                    old = i - SLOTS // 2
                    if old >= 0 and old + SLOTS < len(PAIRS):
                        sp.wait_ge(c_out[old % SLOTS], 16 * (old // SLOTS + 1))
                        sp.dma_start(C[old % SLOTS], state[old + SLOTS]).then_inc(c_in[old % SLOTS], 16)
                for i in range(SLOTS):
                    sp.wait_ge(c_out[i], 16 * len(PAIRS[i::SLOTS]))
                sp.wait_ge(step.sem, len(step.names))
                sp.dma_start(io["y2_sample"], sz[:]).then_inc(stored, 16)
                sp.wait_ge(stored, 16 * 5)

            @block.gpsimd
            def _(pool):
                nc.gpsimd.memset(eye[:], 0.0).then_inc(eyed, 1)
                pool.wait_ge(eyed, 1)
                nc.gpsimd.affine_select(out=eye[:], in_=eye[:], compare_op=ALU.not_equal, fill=1.0, base=0,
                                        pattern=[[1, NB], [-1, NB]], channel_multiplier=0).then_inc(eyed, 1)
                step.wait(pool, "rstd")
                nc.gpsimd.tensor_tensor(rstd[:], msq[:], keep["minus_half"][0:NB, :], ALU.pow).then_inc(step.sem, 1)
                pool.wait_ge(step.sem, step.names.index("add0") + 1)
                nc.gpsimd.memset(row, 0.0).then_inc(row_ready, 1)
                pool.wait_ge(row_ready, 1)
                nc.gpsimd.affine_select(out=row, in_=row, compare_op=ALU.not_equal, fill=1.0, base=0,
                                        pattern=[[-1, NB], [0, P]], channel_multiplier=1).then_inc(row_ready, 1)
                step.wait(pool, "rs")
                nc.gpsimd.tensor_tensor(rs4[:], var4[:], keep["minus_half"][0:NB, :].to_broadcast([NB, CH]), ALU.pow).then_inc(step.sem, 1)

            @block.scalar
            def _(act):
                act.wait_ge(xload, 16)
                nc.scalar.activation(qs[:], xs[:], ACT.Square, accum_out=ssq[:]).then_inc(step.sem, 1)
                step.wait(act, "xT")
                nc.scalar.activation(xT[:], B[0][:, 0:KC * NB].rearrange("p (k b) -> p k b", b=NB), ACT.Copy).then_inc(step.sem, 1)
                step.wait(act, "gates")
                for m in range(2):
                    nc.scalar.activation(xc[:, 512 * m:512 * m + 512], B[1 + m][0:NB, :], ACT.Copy)
                    nc.scalar.activation(sz[:, 512 * m:512 * m + 512], B[3 + m][0:NB, :], ACT.Tanh, scale=0.5)
                    op = nc.scalar.activation(tho[:, 512 * m:512 * m + 512], B[5 + m][0:NB, :], ACT.Tanh, scale=0.5)
                op.then_inc(step.sem, 1)
                step.wait(act, "abs")
                nc.scalar.activation(e4[:], g8[:, CH:2 * CH], ACT.Abs).then_inc(step.sem, 1)
                step.wait(act, "exp")
                nc.scalar.activation(e4[:], e4[:], ACT.Exp, scale=-1.0).then_inc(step.sem, 1)
                step.wait(act, "ln")
                nc.scalar.activation(e4[:], e4[:], ACT.Ln, bias=1.0).then_inc(step.sem, 1)
                step.wait(act, "edd")
                nc.scalar.activation(dd[:], dd[:], ACT.Exp).then_inc(step.sem, 1)
                step.wait(act, "cth")
                nc.scalar.activation(th, acc[:], ACT.Tanh, scale=0.5).then_inc(step.sem, 1)
                step.wait(act, "cT")
                nc.scalar.activation(cT[:], B[0][:, 0:KC * NB].rearrange("p (k b) -> p k b", b=NB), ACT.Copy, scale=0.5)
                nc.scalar.activation(xcT[:], B[0][:, KC * NB:2 * KC * NB].rearrange("p (k b) -> p k b", b=NB), ACT.Copy).then_inc(step.sem, 1)
                step.wait(act, "qkv_out")
                for m in range(2):
                    nc.scalar.activation(qs[:, 512 * m:512 * m + 512], B[1 + m][0:NB, :], ACT.Copy, scale=CD ** -0.5)
                    nc.scalar.activation(ks[:, 512 * m:512 * m + 512], B[3 + m][0:NB, :], ACT.Copy)
                    op = nc.scalar.activation(vs[:, 512 * m:512 * m + 512], B[5 + m][0:NB, :], ACT.Copy)
                op.then_inc(step.sem, 1)
                act.wait_ge(step.sem, step.names.index("loop"))
                for i, (b, h) in enumerate(PAIRS):
                    if h == 0:
                        act.wait_ge(spread_v, b + 1)
                    if i >= 3:
                        act.wait_ge(updated, i - 2)
                    v = VB[b % 2][h // 2][:, (h % 2) * CD:(h % 2 + 1) * CD]
                    for c in range(2):
                        k = (2 * h + c) * NB + b
                        op = nc.scalar.activation(fresh[i % 3][:, c * CD:(c + 1) * CD], v, ACT.Identity, scale=wkT[:, k:k + 1])
                    op.then_inc(crossed, 1)

            @block.vector
            def _(dve):
                V = nc.vector

                def do(name, make):
                    step.wait(dve, name)
                    make().then_inc(step.sem, 1)
                do("msq", lambda: V.tensor_scalar(msq[:], ssq[:], 1.0 / D, EPS, ALU.mult, ALU.add))
                do("xn", lambda: V.scalar_tensor_tensor(xs[:], xs[:], rstd[:], g_row[0:NB, :], ALU.mult, ALU.mult))
                step.wait(dve, "sz")
                for m in range(2):
                    op = V.scalar_tensor_tensor(sz[:, 512 * m:512 * m + 512], sz[:, 512 * m:512 * m + 512], 1.0, B[3 + m][0:NB, :], ALU.add, ALU.mult)
                op.then_inc(step.sem, 1)
                do("g8", lambda: V.tensor_tensor(g8[:], B[7][0:NB, 0:8], b_if[0:NB, :], ALU.add))
                do("lf", lambda: V.scalar_tensor_tensor(lf[:], g8[:, CH:2 * CH], 0.0, e4[:], ALU.min, ALU.subtract))
                dve.wait_ge(load, 16 * 7)
                do("prior", lambda: V.tensor_tensor(pr[:], lf[:], m4[:], ALU.add))
                do("mt", lambda: V.tensor_tensor(mt[:], pr[:], g8[:, 0:CH], ALU.max))
                step.wait(dve, "dd")
                V.tensor_tensor(dd[:, 0:4], g8[:, 0:CH], mt[:], ALU.subtract)
                V.tensor_tensor(dd[:, 4:8], pr[:], mt[:], ALU.subtract)
                V.tensor_scalar(dd[:, 8:12], mt[:], -1.0, None, ALU.mult).then_inc(step.sem, 1)
                step.wait(dve, "taps")
                dve.wait_ge(load, 16 * 7)
                for j in range(3):
                    V.tensor_tensor(tap[:, j, :], tap[:, j, :], buf[:, j, :], ALU.mult)
                V.tensor_tensor(tap[:, 3, :], tap[:, 3, :], xc[:], ALU.mult).then_inc(step.sem, 1)
                for j in range(4):
                    do(f"add{j}", lambda: V.tensor_tensor(acc[:], acc[:], tap[:, j, :], ALU.add))
                do("cs", lambda: V.scalar_tensor_tensor(acc[:], th, 1.0, acc[:], ALU.add, ALU.mult))
                step.wait(dve, "qk1")
                dve.wait_ge(nload, 16)
                V.tensor_tensor(tmp, qs[:], ks[:], ALU.mult)
                V.tensor_tensor(th, qs[:], n[:], ALU.mult).then_inc(step.sem, 1)
                do("qk2", lambda: V.tensor_reduce(qk[:], h4(tmp), AX.X, ALU.add))
                do("qn2", lambda: V.tensor_reduce(qn[:], h4(th), AX.X, ALU.add))
                do("smw", lambda: V.tensor_tensor(smw[:], qk[:], dd[:, 0:4], ALU.mult))
                do("aqn", lambda: V.tensor_tensor(qn[:], qn[:], dd[:, 4:8], ALU.mult))
                do("den", lambda: V.tensor_tensor(den[:], smw[:], qn[:], ALU.add))
                do("absd", lambda: V.scalar_tensor_tensor(den[:], den[:], -1.0, den[:], ALU.mult, ALU.max))
                do("dmax", lambda: V.tensor_tensor(den[:], den[:], dd[:, 8:12], ALU.max))
                do("dinv", lambda: V.reciprocal(dinv[:], den[:]))
                do("wk", lambda: V.tensor_tensor(h4(kw), h4(ks[:]), wide(dd[:, 0:4]), ALU.mult))
                do("an", lambda: V.tensor_tensor(h4(n[:]), h4(n[:]), wide(dd[:, 4:8]), ALU.mult))
                do("nn", lambda: V.tensor_tensor(n[:], n[:], kw, ALU.add))
                dve.wait_ge(eyed, 2)
                step.wait(dve, "qTm")
                for k in range(KC):
                    op = V.tensor_tensor(qTm[:, k, :, :], B[0][:, k * NB:(k + 1) * NB].unsqueeze(2).to_broadcast([P, NB, NB]), eye[:], ALU.mult)
                op.then_inc(step.sem, 1)
                do("wkT", lambda: V.tensor_copy(wkT[:], B[0][:, KC * NB:2 * KC * NB]))
                do("ad", lambda: V.tensor_tensor(ad[:], dd[:, 4:8].unsqueeze(1).to_broadcast([NB, NB, CH]),
                                                 keep["ident"][0:NB, 0:NB].unsqueeze(2).to_broadcast([NB, NB, CH]), ALU.mult))
                do("a_bc", lambda: V.tensor_copy(a_bc[:], B[7][:, 0:NB * CH]))
                for i, (b, h) in enumerate(PAIRS):
                    dve.wait_ge(crossed, i + 1)
                    dve.wait_ge(read, i + 1)
                    op = V.scalar_tensor_tensor(C[i % SLOTS].rearrange("p c v -> p (c v)"), C[i % SLOTS].rearrange("p c v -> p (c v)"),
                                                a_bc[:, i:i + 1], fresh[i % 3], ALU.mult, ALU.add)
                    op.then_inc(updated, 1)
                dve.wait_ge(updated, len(PAIRS))
                step.wait(dve, "loop")
                dve.sem_inc(step.sem, 1)
                step.wait(dve, "n1")
                for h in range(CH):
                    op = V.tensor_scalar(qs[:, h * CD:(h + 1) * CD], B[1 + h][0:NB, 0:CD], dd[:, 4 + h:5 + h], None, ALU.mult)
                op.then_inc(step.sem, 1)
                do("n2", lambda: V.tensor_tensor(h4(vs[:]), h4(vs[:]), wide(smw[:]), ALU.mult))
                do("n3", lambda: V.tensor_tensor(qs[:], qs[:], vs[:], ALU.add))
                do("hc", lambda: V.tensor_tensor(h4(qs[:]), h4(qs[:]), wide(dinv[:]), ALU.mult))
                step.wait(dve, "st")
                for h in range(CH):
                    op = V.bn_stats(st6[:, h, :], qs[:, h * CD:(h + 1) * CD])
                op.then_inc(step.sem, 1)
                step.wait(dve, "mv")
                for h in range(CH):
                    op = V.bn_aggr(mv[:, h, :], st6[:, h, :])
                op.then_inc(step.sem, 1)
                do("var", lambda: V.tensor_scalar(var4[:], mv[:, :, 1], 1.0, EPS, ALU.mult, ALU.add))
                step.wait(dve, "hn")
                for h in range(CH):
                    op = V.tensor_scalar(qs[:, h * CD:(h + 1) * CD], qs[:, h * CD:(h + 1) * CD], mv[:, h, 0:1], rs4[:, h:h + 1], ALU.subtract, ALU.mult)
                op.then_inc(step.sem, 1)
                do("A", lambda: V.scalar_tensor_tensor(qs[:], tho[:], 1.0, qs[:], ALU.add, ALU.mult))
                do("B", lambda: V.tensor_tensor(qs[:], qs[:], ngh[0:NB, :], ALU.mult))
                do("skip", lambda: V.tensor_tensor(acc[:], acc[:], skiph[0:NB, :], ALU.mult))
                do("E", lambda: V.tensor_tensor(qs[:], qs[:], acc[:], ALU.add))
                do("y", lambda: V.scalar_tensor_tensor(sz[:], qs[:], 0.5, sz[:], ALU.mult, ALU.mult))

            @block.tensor
            def _(pe):
                ident8 = keep["ident"][0:NB, 0:NB]
                step.wait(pe, "turn")
                for k in range(KC):
                    op = nc.tensor.transpose(B[0][:, k * NB:(k + 1) * NB], xs[:, k * P:(k + 1) * P], ident8)
                op.then_inc(step.sem, 1)
                step.wait(pe, "project")
                for j in range(6):
                    for k in range(KC):
                        nc.tensor.matmul(B[1 + j][0:NB, :], xT[:, k, :], w[:, k, 512 * j:512 * j + 512], start=k == 0, stop=k == KC - 1)
                for k in range(KC):
                    op = nc.tensor.matmul(B[7][0:NB, 0:8], xT[:, k, :], w[:, k, GATES:GATES + 8], start=k == 0, stop=k == KC - 1)
                op.then_inc(step.sem, 1)
                step.wait(pe, "turn_c")
                for j, src in enumerate((acc, xc)):
                    for k in range(KC):
                        op = nc.tensor.transpose(B[0][:, (j * KC + k) * NB:(j * KC + k + 1) * NB], src[:, k * P:(k + 1) * P], ident8)
                op.then_inc(step.sem, 1)
                step.wait(pe, "qkv")
                for j, (src, wt_) in enumerate(((cT, wq), (cT, wk), (xcT, wv))):
                    for h in range(CH):
                        for c in range(2):
                            op = nc.tensor.matmul(B[1 + 2 * j + h // 2][0:NB, (h % 2) * CD:(h % 2 + 1) * CD], src[:, 2 * h + c, :], wt_[:, h, c, :],
                                                  start=c == 0, stop=c == 1)
                op.then_inc(step.sem, 1)
                step.wait(pe, "turn_q")
                for j, src in enumerate((qs, kw)):
                    for k in range(KC):
                        op = nc.tensor.transpose(B[0][:, (j * KC + k) * NB:(j * KC + k + 1) * NB], src[:, k * P:(k + 1) * P], ident8)
                op.then_inc(step.sem, 1)
                step.wait(pe, "spread")
                nc.tensor.matmul(B[7][:, 0:NB * CH], keep["ones"][0:NB, :], ad[:].rearrange("p b h -> p (b h)"), start=True, stop=True).then_inc(step.sem, 1)
                pe.wait_ge(row_ready, 2)
                pe.wait_ge(step.sem, step.names.index("loop"))

                def spread_values(b):
                    if b >= 2:
                        pe.wait_ge(crossed, CH * (b - 1))
                    for m in range(2):
                        op = nc.tensor.matmul(VB[b % 2][m][:], row[:, b, :], vs[:, 512 * m:512 * m + 512], start=True, stop=True)
                    op.then_inc(spread_v, 1)
                spread_values(0)
                for i, (b, h) in enumerate(PAIRS):
                    if h == 0 and b + 1 < NB:
                        spread_values(b + 1)
                    pe.wait_ge(c_in[i % SLOTS], 16 * (i // SLOTS + 1))
                    for c in range(2):
                        op = nc.tensor.matmul(B[1 + h][0:NB, 0:CD], qTm[:, 2 * h + c, b, :], C[i % SLOTS][:, c, :], start=b == 0 and c == 0, stop=b == NB - 1 and c == 1)
                    op.then_inc(read, 1)

        bank_stack.close()
        finish(nc, io, keep, w[:, :, 0:D], w_final_in)


def finish(nc, io, keep, w, w_in):
    LAST = NT
    with ExitStack() as st:
        s = Scope(nc, st, "fi")
        g_row = s.sb("g_row", [P, D])
        y = [s.sb(f"y{i}", [P, D]) for i in range(2)]
        h = [s.sb(f"h{i}", [P, D]) for i in range(2)]
        yT = [s.sb(f"yT{i}", [P, KC, P]) for i in range(2)]
        o = [s.sb(f"o{i}", [P, D]) for i in range(2)]
        ssq, msq, rstd = (s.sb(n, [P, 1]) for n in ("ssq", "msq", "rstd"))
        T = [s.ps(f"T{i}") for i in range(4)]
        O = [s.ps(f"O{i}") for i in range(4)]
        loads = s.sem("loads")
        ld = s.sems("y0 y1 h0 h1")
        out = s.sems("o0 o1")
        q = s.sems("turned yT projected summed ssq msq rstd normed")
        block = st.enter_context(nc.Block())

        def tiles(eng, body):
            with eng.Fori(0, NT // 2 - 1) as i:
                body(i * 2, i, 0)
                body(i * 2 + 1, i, 1)
            body(NT - 2, NT // 2 - 1, 0)
            body(NT - 1, NT // 2 - 1, 1)
            body(LAST, NT // 2, 0, n=NB)

        def begin(eng, names):
            for n in names.split():
                eng.sem_inc(q[n], LEAD)

        @block.sync
        def _(sp):
            for i in range(2):
                sp.sem_inc(out[f"o{i}"], 16 * LEAD)
                for n in "yh":
                    sp.sem_inc(ld[f"{n}{i}"], 16 * LEAD)
            for i in range(2):
                sp.dma_start(y[i][:], io["y2"][i * P:(i + 1) * P, :]).then_inc(ld[f"y{i}"], 16)
            sp.dma_start(g_row[:], io["final_g"].partition_broadcast(P)).then_inc(loads, 16)

            def gated(t, r, n=P):
                wait_stage(sp, q["turned"], t, back=2)
                sp.dma_start(y[r][0:n, :], io["y2_sample"] if n == NB else io["y2"][bass.ds(t * P, P), :]).then_inc(ld[f"y{r}"], 16)

            def residual(t, r, n=P):
                wait_stage(sp, q["ssq"], t, back=2)
                sp.dma_start(h[r][0:n, :], io["h1_sample"] if n == NB else io["h1"][bass.ds(t * P, P), :]).then_inc(ld[f"h{r}"], 16)
            residual(0, 0)

            def body(t, pair, r, n=P):
                if not isinstance(t, int) or t + 2 <= LAST:
                    gated(t + 2, r, NB if isinstance(t, int) and t + 2 == LAST else P)
                if n == P:
                    residual(t + 1, 1 - r, NB if isinstance(t, int) and t + 1 == LAST else P)
                wait_stage(sp, q["normed"], t)
                dst = io["y_sample"] if n == NB else io["y_prompt"][bass.ds(t * P, P), :]
                sp.dma_start(dst, o[r][0:n, :]).then_inc(out[f"o{r}"], 16)
            tiles(sp, body)
            sp.wait_ge(out["o0"], 16 * (LEAD + NT // 2 + 1))
            sp.wait_ge(out["o1"], 16 * (LEAD + NT // 2))

        @block.gpsimd
        def _(pool):
            begin(pool, "rstd")

            def body(t, pair, r, n=P):
                wait_stage(pool, q["normed"], t, back=1)
                wait_stage(pool, q["msq"], t)
                nc.gpsimd.tensor_tensor(rstd[0:n, :], msq[0:n, :], keep["minus_half"][0:n, :], ALU.pow).then_inc(q["rstd"], 1)
            tiles(pool, body)

        @block.scalar
        def _(act):
            begin(act, "yT ssq")

            def turn_out(t, r, n=P):
                wait_stage(act, q["turned"], t)
                wait_stage(act, q["projected"], t, back=2)
                for m in range(2):
                    op = nc.scalar.activation(yT[r][:, 4 * m:4 * m + 4, 0:n], T[2 * r + m][:, 0:4 * n].rearrange("p (k n) -> p k n", k=4), ACT.Copy)
                op.then_inc(q["yT"], 1)
            turn_out(0, 0)

            def body(t, pair, r, n=P):
                if n == P:
                    turn_out(t + 1, 1 - r, NB if isinstance(t, int) and t + 1 == LAST else P)
                wait_stage(act, q["summed"], t)
                wait_stage(act, q["msq"], t, back=1)
                nc.scalar.activation(h[r][0:n, :], o[r][0:n, :], ACT.Square, accum_out=ssq[0:n, :]).then_inc(q["ssq"], 1)
            tiles(act, body)

        @block.vector
        def _(dve):
            begin(dve, "summed msq normed")
            dve.wait_ge(loads, 16)

            def body(t, pair, r, n=P):
                wait_stage(dve, q["projected"], t)
                dve.wait_ge(ld[f"h{r}"], (pair + (LEAD + 1)) * 16)
                dve.wait_ge(out[f"o{r}"], (pair + LEAD) * 16)
                for m in range(2):
                    op = nc.vector.tensor_tensor(o[r][0:n, 512 * m:512 * m + 512], h[r][0:n, 512 * m:512 * m + 512], O[2 * r + m][0:n, :], ALU.add)
                op.then_inc(q["summed"], 1)
                wait_stage(dve, q["ssq"], t)
                wait_stage(dve, q["rstd"], t, back=1)
                nc.vector.tensor_scalar(msq[0:n, :], ssq[0:n, :], 1.0 / D, EPS, ALU.mult, ALU.add).then_inc(q["msq"], 1)
                wait_stage(dve, q["rstd"], t)
                nc.vector.scalar_tensor_tensor(o[r][0:n, :], o[r][0:n, :], rstd[0:n, :], g_row[0:n, :], ALU.mult, ALU.mult).then_inc(q["normed"], 1)
            tiles(dve, body)

        @block.tensor
        def _(pe):
            begin(pe, "turned projected")

            def turn(t, pair, r, n=P):
                pe.wait_ge(ld[f"y{r}"], (pair + (LEAD + 1)) * 16)
                wait_stage(pe, q["yT"], t, back=2)
                for k in range(KC):
                    op = nc.tensor.transpose(T[2 * r + k // 4][:, (k % 4) * n:(k % 4 + 1) * n], y[r][0:n, k * P:(k + 1) * P], keep["ident"][0:n, 0:n])
                op.then_inc(q["turned"], 1)
            turn(0, 0, 0)
            pe.wait_ge(w_in, 16 * KC)

            def body(t, pair, r, n=P):
                if n == P:
                    turn(t + 1, pair + r, 1 - r, NB if isinstance(t, int) and t + 1 == LAST else P)
                wait_stage(pe, q["yT"], t)
                wait_stage(pe, q["summed"], t, back=2)
                for m in range(2):
                    for k in range(KC):
                        op = nc.tensor.matmul(O[2 * r + m][0:n, :], yT[r][:, k, 0:n], w[:, k, 512 * m:512 * m + 512], start=k == 0, stop=k == KC - 1)
                op.then_inc(q["projected"], 1)
            tiles(pe, body)


def build(nc, ins, outs):
    def scratch(name, shape):
        return nc.dram_tensor(f"scratch_{name}", shape, F32, kind="Internal").ap()

    io = {
        "x_prompt": ins["x_prompt"].rearrange("a s d -> (a s) d"),
        "x_sample": ins["x_sample"].rearrange("b a d -> (b a) d"),
        "cache_k": ins["cache_k"].rearrange("l n p h d -> (l n p) (h d)"),
        "cache_v": ins["cache_v"].rearrange("l n p h d -> (l n p) (h d)"),
        "cache_logf": ins["cache_logf"].rearrange("l n p h -> (l n) (p h)"),
        "state_c": ins["state_c"].rearrange("l b h k v -> (l b h k) v"),
        "state_n": ins["state_n"].rearrange("l b h k -> (l b) (h k)"),
        "state_m": ins["state_m"].rearrange("l b h -> (l b) h"),
        "state_conv": ins["state_conv"].rearrange("l b j c -> (l b) j c"),
        "page_table": ins["page_table"],
        "norm_g": ins["norm_g"], "final_g": ins["final_g"],
        "even_w_in": ins["even_w_in"][0], "even_b_f": ins["even_b_f"][0, :], "gmlp_ln_g": ins["gmlp_ln_g"][0, :],
        "gmlp_ln_b": ins["gmlp_ln_b"][0, :], "gmlp_w_s": ins["gmlp_w_s"][0], "gmlp_b_s": ins["gmlp_b_s"][0],
        "even_w_out": ins["even_w_out"][0], "odd_w_in": ins["odd_w_in"][0], "odd_b_i": ins["odd_b_i"][0, :],
        "odd_b_f": ins["odd_b_f"][0, :], "conv_w": ins["conv_w"][0], "conv_b": ins["conv_b"][0, :],
        "w_q": ins["mlstm_w_q"][0], "w_k": ins["mlstm_w_k"][0], "w_v": ins["mlstm_w_v"][0],
        "norm_c": ins["mlstm_norm_g"][0, :], "skip": ins["mlstm_skip"][0, :], "odd_w_out": ins["odd_w_out"][0],
        "y_prompt": outs["y_prompt"].rearrange("a s d -> (a s) d"),
        "y_sample": outs["y_sample"].rearrange("b a d -> (b a) d"),
        "k_prompt": outs["k_prompt"].rearrange("l a s h d -> (l a s) (h d)"),
        "v_prompt": outs["v_prompt"].rearrange("l a s h d -> (l a s) (h d)"),
        "logf_prompt": outs["logf_prompt"].rearrange("l a s h -> (l a s) h"),
        "k_sample": outs["k_sample"].rearrange("l b a h d -> (l b a) (h d)"),
        "v_sample": outs["v_sample"].rearrange("l b a h d -> (l b a) (h d)"),
        "logf_sample": outs["logf_sample"].rearrange("l b a h -> (l b a) h"),
        "chunk_v": outs["chunk_v_sample"].rearrange("l b a c -> (l b a) c"),
        "c_prompt": outs["c_prompt"].rearrange("l a h k v -> (l a h k) v"),
        "n_prompt": outs["n_prompt"].rearrange("l a h k -> (l a) (h k)"),
        "m_prompt": outs["m_prompt"].rearrange("l a h -> (l a) h"),
        "conv_prompt": outs["conv_prompt"].rearrange("l a j c -> (l a j) c"),
        "c_sample": outs["c_sample"].rearrange("l b h k v -> (l b h k) v"),
        "n_sample": outs["n_sample"].rearrange("l b h k -> (l b) (h k)"),
        "m_sample": outs["m_sample"].rearrange("l b h -> (l b) h"),
        "conv_sample": outs["conv_sample"].rearrange("l b j c -> (l b) j c"),
        "q_sample": scratch("q_sample", (NB, AW)), "q_prompt": scratch("q_prompt", (SEQ, AW)),
        "mix_scratch": scratch("mix", (SEQ, D)), "h1": scratch("h1", (SEQ, D)), "h1_sample": scratch("h1_sample", (NB, D)),
        "y2": scratch("y2", (SEQ, D)), "y2_sample": scratch("y2_sample", (NB, D)),
        "s_mixed": scratch("s_mixed", (NB, D)), "self_row": scratch("self_row", (NB, AH)),
    }
    io["q_sample_flat"] = io["q_sample"].rearrange("b c -> (b c)")
    with ExitStack() as stack:
        g = Scope(nc, stack, "g")
        keep = {
            "ident": g.sb("ident", [P, P]), "ones": g.sb("ones", [P, P]),
            "upto": g.sb("upto", [P, P]), "after": g.sb("after", [P, P]),
            "mask_bf": g.sb("mask_bf", [P, P], BF16), "maskT_bf": g.sb("maskT_bf", [P, P], BF16),
            "ident_bf": g.sb("ident_bf", [P, P], BF16), "minus_half": g.sb("minus_half", [P, 1]),
            "half": g.sb("half", [P, 1]),
            "fg": g.sb("fg", [P, NT, AH]), "negc": g.sb("negc", [P, NT, AH]),
            "s_dec": g.sb("s_dec", [P, 4 * NB]), "s_fg": g.sb("s_fg", [NB, AH]), "s_self": g.sb("s_self", [NB, AH]),
        }
        with ExitStack() as layer0:
            keep["scores"] = Scope(nc, layer0, "g0").sb("scores", [P, NB, AH, PAGES + 1])
            even_project(nc, io, keep)
            layer0_out = Scope(nc, layer0, "g1")
            keep["w_out"], keep["w_out_in"] = layer0_out.sb("w_out", [P, KC, D]), layer0_out.sem("w_out_in")
            decode_softmax(nc, io, keep)
            attend(nc, io, keep)
        mlstm(nc, io, keep)


_INS = ['x_prompt', 'x_sample', 'cache_k', 'cache_v', 'cache_logf', 'state_c', 'state_n', 'state_m', 'state_conv', 'page_table',
        'norm_g', 'final_g', 'even_w_in', 'even_b_f', 'gmlp_ln_g', 'gmlp_ln_b', 'gmlp_w_s', 'gmlp_b_s', 'even_w_out',
        'odd_w_in', 'odd_b_i', 'odd_b_f', 'conv_w', 'conv_b', 'mlstm_w_q', 'mlstm_w_k', 'mlstm_w_v', 'mlstm_norm_g',
        'mlstm_skip', 'odd_w_out']
_OUTS = [("y_prompt", (1, 2048, 1024)), ("y_sample", (8, 1, 1024)),
         ("k_prompt", (1, 1, 2048, 8, 64)), ("v_prompt", (1, 1, 2048, 8, 64)), ("logf_prompt", (1, 1, 2048, 8)),
         ("k_sample", (1, 8, 1, 8, 64)), ("v_sample", (1, 8, 1, 8, 64)), ("logf_sample", (1, 8, 1, 8)),
         ("chunk_v_sample", (1, 8, 1, 512)),
         ("c_prompt", (1, 1, 4, 256, 256)), ("n_prompt", (1, 1, 4, 256)), ("m_prompt", (1, 1, 4)), ("conv_prompt", (1, 1, 3, 1024)),
         ("c_sample", (1, 8, 4, 256, 256)), ("n_sample", (1, 8, 4, 256)), ("m_sample", (1, 8, 4)), ("conv_sample", (1, 8, 3, 1024))]


def kernel(**inputs):
    import numpy as _np
    import concourse.bacc as _bacc
    from concourse import mybir as _mybir
    from concourse.bass_utils import run_bass_kernel_spmd as _run

    nc = _bacc.Bacc("TRN2", target_bir_lowering=False, num_devices=1)
    arrays, ins, outs = {}, {}, {}
    for name in _INS:
        a = _np.ascontiguousarray(inputs[name])
        arrays[f"in_{name}_dram"] = a
        ins[name] = nc.dram_tensor(f"in_{name}_dram", a.shape, _mybir.dt.from_np(a.dtype), kind="ExternalInput").ap()
    for name, shape in _OUTS:
        outs[name] = nc.dram_tensor(f"out_{name}_dram", shape, _mybir.dt.float32, kind="ExternalOutput").ap()
    build(nc, ins, outs)
    r = _run(nc, [arrays], core_ids=[0])
    return tuple(r.results[0][f"out_{name}_dram"] for name, _ in _OUTS)
```
